# Optimizing a Trainium2 kernel written in Bass

```python
import jax, jax.numpy as jnp
from jax import lax
import numpy as np
import math

D_MODEL = 1024
BATCH = 1
SEQ = 256
DEPTH = 2

N_HEADS = 16
N_KV_HEADS = 4
HEAD_DIM = D_MODEL // N_HEADS
GROUP = N_HEADS // N_KV_HEADS
QKV_DIM = (N_HEADS + 2 * N_KV_HEADS) * HEAD_DIM
ROT_DIM = HEAD_DIM // 4
ROPE_THETA = 500000.0
MOBA_BLOCK = 256
MOBA_TOPK = 3
MOBA_QCHUNK = 16
SWA_WINDOW = 128
D_FF = 3584
N_EXPERTS = 8
TOP_K = 2
PLE_DIM = 256
LN_EPS = 1e-5
N_EVEN = (DEPTH + 1) // 2
N_ODD = DEPTH // 2


def rope_tables(positions):
    inv = 1.0 / (ROPE_THETA ** (jnp.arange(0, ROT_DIM, 2, dtype=jnp.float32) / ROT_DIM))
    ang = positions.astype(jnp.float32)[..., None] * inv
    return jnp.cos(ang), jnp.sin(ang)

def apply_partial_rope(x, cos, sin):
    half = ROT_DIM // 2
    c = cos[:, :, None, :].astype(x.dtype)
    s = sin[:, :, None, :].astype(x.dtype)
    x1, x2, xp = x[..., :half], x[..., half:ROT_DIM], x[..., ROT_DIM:]
    return jnp.concatenate([x1 * c - x2 * s, x2 * c + x1 * s, xp], axis=-1)

def layer_norm(x, g, b):
    xf = x.astype(jnp.float32)
    mu = jnp.mean(xf, axis=-1, keepdims=True)
    var = jnp.mean(jnp.square(xf - mu), axis=-1, keepdims=True)
    return ((xf - mu) * lax.rsqrt(var + LN_EPS) * g.astype(jnp.float32) + b.astype(jnp.float32)).astype(x.dtype)

def project_qkv(x, w_qkv, cos, sin):
    B, S, _ = x.shape
    qkv = x @ w_qkv
    nq = N_HEADS * HEAD_DIM
    nk = N_KV_HEADS * HEAD_DIM
    q = qkv[..., :nq].reshape(B, S, N_HEADS, HEAD_DIM)
    k = qkv[..., nq:nq + nk].reshape(B, S, N_KV_HEADS, HEAD_DIM)
    v = qkv[..., nq + nk:].reshape(B, S, N_KV_HEADS, HEAD_DIM)
    return apply_partial_rope(q, cos, sin), apply_partial_rope(k, cos, sin), v

def moba_attention(q, k, v):
    B, S, H, Dh = q.shape
    nb = -(-S // MOBA_BLOCK)
    S_pad = nb * MOBA_BLOCK
    pad = ((0, 0), (0, S_pad - S), (0, 0), (0, 0))
    q = jnp.pad(q * (HEAD_DIM ** -0.5), pad)
    k = jnp.pad(k, pad)
    v = jnp.pad(v, pad)
    kb = k.reshape(B, nb, MOBA_BLOCK, N_KV_HEADS, Dh).transpose(0, 1, 3, 2, 4)
    vb = v.reshape(B, nb, MOBA_BLOCK, N_KV_HEADS, Dh).transpose(0, 1, 3, 2, 4)
    kmean = jnp.mean(kb.astype(jnp.float32), axis=3)
    qg = q.reshape(B, S_pad, N_KV_HEADS, GROUP, Dh).astype(jnp.float32)
    gate = jnp.einsum('bskgd,bnkd->bskgn', qg, kmean).reshape(B, S_pad, H, nb)
    qblk = jnp.arange(S_pad) // MOBA_BLOCK
    past = jnp.arange(nb)[None, :] < qblk[:, None]
    gate = jnp.where(past[None, :, None, :], gate, -jnp.inf)
    n_sel = min(MOBA_TOPK, nb)
    _, sel = lax.top_k(gate, n_sel)

    QC = MOBA_QCHUNK
    NC = S_pad // QC
    q_c = q.reshape(B, NC, QC, H, Dh).transpose(1, 0, 2, 3, 4)
    sel_c = sel.reshape(B, NC, QC, H, n_sel).transpose(1, 0, 2, 3, 4)
    b_idx = jnp.arange(B)[:, None, None, None]
    g_idx = (jnp.arange(H) // GROUP)[None, None, :, None]

    def chunk(args):
        qc, selc, cid = args
        t = cid * QC + jnp.arange(QC)
        c = (cid * QC) // MOBA_BLOCK
        kg = kb[b_idx, selc, g_idx]
        vg = vb[b_idx, selc, g_idx]
        lp = jnp.einsum('bqhd,bqhnjd->bqhnj', qc, kg).astype(jnp.float32)
        valid = jnp.arange(n_sel)[None, :] < (t // MOBA_BLOCK)[:, None]
        lp = jnp.where(valid[None, :, None, :, None], lp, -jnp.inf).reshape(B, QC, H, n_sel * MOBA_BLOCK)
        ko = lax.dynamic_index_in_dim(kb, c, axis=1, keepdims=False)
        vo = lax.dynamic_index_in_dim(vb, c, axis=1, keepdims=False)
        qcg = qc.reshape(B, QC, N_KV_HEADS, GROUP, Dh)
        lo = jnp.einsum('bqkgd,bkjd->bqkgj', qcg, ko).astype(jnp.float32).reshape(B, QC, H, MOBA_BLOCK)
        kpos = c * MOBA_BLOCK + jnp.arange(MOBA_BLOCK)
        lo = jnp.where((kpos[None, :] <= t[:, None])[None, :, None, :], lo, -jnp.inf)
        probs = jax.nn.softmax(jnp.concatenate([lp, lo], axis=-1), axis=-1)
        pp = probs[..., :n_sel * MOBA_BLOCK].reshape(B, QC, H, n_sel, MOBA_BLOCK).astype(v.dtype)
        po = probs[..., n_sel * MOBA_BLOCK:].reshape(B, QC, N_KV_HEADS, GROUP, MOBA_BLOCK).astype(v.dtype)
        out = jnp.einsum('bqhnj,bqhnjd->bqhd', pp, vg) + \
            jnp.einsum('bqkgj,bkjd->bqkgd', po, vo).reshape(B, QC, H, Dh)
        return out

    out = lax.map(chunk, (q_c, sel_c, jnp.arange(NC)))
    return out.transpose(1, 0, 2, 3, 4).reshape(B, S_pad, H, Dh)[:, :S]

def sliding_window_attention(q, k, v, sinks):
    B, S, H, Dh = q.shape
    W = SWA_WINDOW
    n = S // W
    qb = (q * (HEAD_DIM ** -0.5)).reshape(B, n, W, N_KV_HEADS, GROUP, Dh)
    kb = k.reshape(B, n, W, N_KV_HEADS, Dh)
    vb = v.reshape(B, n, W, N_KV_HEADS, Dh)
    zpad = ((0, 0), (1, 0), (0, 0), (0, 0), (0, 0))
    kk = jnp.concatenate([jnp.pad(kb, zpad)[:, :-1], kb], axis=2)
    vv = jnp.concatenate([jnp.pad(vb, zpad)[:, :-1], vb], axis=2)
    logits = jnp.einsum('bnqkgd,bnjkd->bnkgqj', qb, kk).astype(jnp.float32)
    rel = (jnp.arange(W)[:, None] + W) - jnp.arange(2 * W)[None, :]
    band = (rel >= 0) & (rel < W)
    first = (jnp.arange(n) == 0)[:, None, None] & (jnp.arange(2 * W) < W)[None, None, :]
    mask = band[None] & ~first
    logits = jnp.where(mask[None, :, None, None, :, :], logits, -jnp.inf)
    sink = sinks.astype(jnp.float32).reshape(1, 1, N_KV_HEADS, GROUP, 1, 1)
    m = jnp.maximum(jnp.max(logits, axis=-1, keepdims=True), sink)
    e = jnp.exp(logits - m)
    probs = e / (jnp.sum(e, axis=-1, keepdims=True) + jnp.exp(sink - m))
    out = jnp.einsum('bnkgqj,bnjkd->bnqkgd', probs.astype(v.dtype), vv)
    return out.reshape(B, S, H, Dh)

def swiglu(x, w_gate, w_up, w_down):
    return (jax.nn.silu(x @ w_gate) * (x @ w_up)) @ w_down

def moe_swiglu(x, w_router, w_gate, w_up, w_down):
    logits = (x @ w_router).astype(jnp.float32)
    top_v, top_i = lax.top_k(logits, TOP_K)
    top_w = jax.nn.softmax(top_v, axis=-1)
    gates = jnp.sum(jax.nn.one_hot(top_i, N_EXPERTS, dtype=jnp.float32) * top_w[..., None], axis=-2)
    out = jnp.zeros_like(x)
    for e in range(N_EXPERTS):
        out = out + gates[..., e:e + 1].astype(x.dtype) * swiglu(x, w_gate[e], w_up[e], w_down[e])
    return out

def first_inputs(seed: int = 0) -> dict:
    key = jax.random.key(seed)
    ks = jax.random.split(key, 20)
    f32 = jnp.float32
    beta = (8.0 * DEPTH) ** -0.25

    def nrm(k, shape, fan_in, scale=1.0):
        return jax.random.normal(k, shape, f32) * (scale * fan_in ** -0.5)

    x = jax.random.normal(ks[0], (BATCH, SEQ, D_MODEL), f32)
    p = jax.random.normal(ks[1], (DEPTH, BATCH, SEQ, PLE_DIM), f32)
    positions = jnp.broadcast_to(jnp.arange(SEQ, dtype=jnp.int32)[None, :], (BATCH, SEQ))
    w_qkv = nrm(ks[2], (DEPTH, D_MODEL, QKV_DIM), D_MODEL)
    w_o = nrm(ks[3], (DEPTH, N_HEADS * HEAD_DIM, D_MODEL), N_HEADS * HEAD_DIM, beta)
    ln_mix_g = 1.0 + 0.05 * jax.random.normal(ks[4], (DEPTH, D_MODEL), f32)
    ln_mix_b = 0.02 * jax.random.normal(ks[5], (DEPTH, D_MODEL), f32)
    ln_ffn_g = 1.0 + 0.05 * jax.random.normal(ks[6], (DEPTH, D_MODEL), f32)
    ln_ffn_b = 0.02 * jax.random.normal(ks[7], (DEPTH, D_MODEL), f32)
    sinks = 0.5 * jax.random.normal(ks[8], (N_ODD, N_HEADS), f32)
    w_ffn_gate = nrm(ks[9], (N_EVEN, D_MODEL, D_FF), D_MODEL)
    w_ffn_up = nrm(ks[10], (N_EVEN, D_MODEL, D_FF), D_MODEL)
    w_ffn_down = nrm(ks[11], (N_EVEN, D_FF, D_MODEL), D_FF, beta)
    w_router = nrm(ks[12], (N_ODD, D_MODEL, N_EXPERTS), D_MODEL)
    w_exp_gate = nrm(ks[13], (N_ODD, N_EXPERTS, D_MODEL, D_FF), D_MODEL)
    w_exp_up = nrm(ks[14], (N_ODD, N_EXPERTS, D_MODEL, D_FF), D_MODEL)
    w_exp_down = nrm(ks[15], (N_ODD, N_EXPERTS, D_FF, D_MODEL), D_FF, beta)
    w_ple_proj = nrm(ks[16], (DEPTH, PLE_DIM, D_MODEL), PLE_DIM, 0.5)
    w_ple_gate = nrm(ks[17], (DEPTH, D_MODEL, D_MODEL), D_MODEL)
    return {"x": x, "p": p, "positions": positions, "w_qkv": w_qkv, "w_o": w_o,
            "ln_mix_g": ln_mix_g, "ln_mix_b": ln_mix_b, "ln_ffn_g": ln_ffn_g, "ln_ffn_b": ln_ffn_b,
            "sinks": sinks, "w_ffn_gate": w_ffn_gate, "w_ffn_up": w_ffn_up, "w_ffn_down": w_ffn_down,
            "w_router": w_router, "w_exp_gate": w_exp_gate, "w_exp_up": w_exp_up, "w_exp_down": w_exp_down,
            "w_ple_proj": w_ple_proj, "w_ple_gate": w_ple_gate}

def first_block(x, p, positions, w_qkv, w_o, ln_mix_g, ln_mix_b, ln_ffn_g, ln_ffn_b, sinks,
              w_ffn_gate, w_ffn_up, w_ffn_down, w_router, w_exp_gate, w_exp_up, w_exp_down,
              w_ple_proj, w_ple_gate):
    alpha = (2.0 * DEPTH) ** 0.25
    B, S, _ = x.shape
    cos, sin = rope_tables(positions)
    for i in range(DEPTH):
        j = i // 2
        q, k, v = project_qkv(x, w_qkv[i], cos, sin)
        if i % 2 == 0:
            a = moba_attention(q, k, v)
        else:
            a = sliding_window_attention(q, k, v, sinks[j])
        x = layer_norm(alpha * x + a.reshape(B, S, N_HEADS * HEAD_DIM) @ w_o[i], ln_mix_g[i], ln_mix_b[i])
        if i % 2 == 0:
            f = swiglu(x, w_ffn_gate[j], w_ffn_up[j], w_ffn_down[j])
        else:
            f = moe_swiglu(x, w_router[j], w_exp_gate[j], w_exp_up[j], w_exp_down[j])
        x = layer_norm(alpha * x + f, ln_ffn_g[i], ln_ffn_b[i])
        x = x + (p[i] @ w_ple_proj[i]) * jax.nn.sigmoid(x @ w_ple_gate[i])
    return x


DN_HEADS = 4
DN_HEAD_DIM = 128
DN_WIDTH = DN_HEADS * DN_HEAD_DIM
DN_CONV = 4
DN_CHUNK = 64
SWA_HEADS = 8
SWA_HEAD_DIM = 64
SWA_WIDTH = SWA_HEADS * SWA_HEAD_DIM
DILATED_CONFIGS = ((128, 1), (512, 4), (2048, 16))
ATTN_BLOCK = 128
ROPE_DIM = SWA_HEAD_DIM // 4
D_MIX = DN_WIDTH + SWA_WIDTH
IN_SPLITS = (3 * DN_WIDTH, DN_WIDTH, DN_HEADS, DN_HEADS, SWA_WIDTH, SWA_WIDTH, SWA_WIDTH)
IN_WIDTH = sum(IN_SPLITS)
D_FF_2 = 2816
FFN_CONV = 3
NORM_EPS = 1e-6


def _rmsnorm(x, w):
    xf = x.astype(jnp.float32)
    y = xf * lax.rsqrt(jnp.mean(xf * xf, axis=-1, keepdims=True) + NORM_EPS)
    return (y * w.astype(jnp.float32)).astype(x.dtype)

def _l2norm(x):
    xf = x.astype(jnp.float32)
    return xf * lax.rsqrt(jnp.sum(xf * xf, axis=-1, keepdims=True) + NORM_EPS)

def _causal_dwconv(x, w):
    K = w.shape[0]
    S = x.shape[1]
    xp = jnp.pad(x, ((0, 0), (K - 1, 0), (0, 0)))
    y = xp[:, 0:S] * w[0]
    for j in range(1, K):
        y = y + xp[:, j:j + S] * w[j]
    return y

def _rope_tables(S):
    pos = jnp.arange(S, dtype=jnp.float32)
    inv_freq = ROPE_THETA ** (-jnp.arange(0, ROPE_DIM, 2, dtype=jnp.float32) / ROPE_DIM)
    ang = pos[:, None] * inv_freq[None, :]
    return jnp.cos(ang), jnp.sin(ang)

def _partial_rope(x, cos, sin):
    half = ROPE_DIM // 2
    c = cos[None, :, None, :].astype(x.dtype)
    s = sin[None, :, None, :].astype(x.dtype)
    x1, x2, rest = x[..., :half], x[..., half:ROPE_DIM], x[..., ROPE_DIM:]
    return jnp.concatenate([x1 * c - x2 * s, x2 * c + x1 * s, rest], axis=-1)

def _gated_delta_rule(q, k, v, g, beta):
    B, S, H, Dk = q.shape
    Dv = v.shape[-1]
    C = DN_CHUNK
    n = S // C
    f32 = jnp.float32

    def chunks(t):
        return t.astype(f32).reshape(B, n, C, H, -1).transpose(0, 3, 1, 2, 4)

    q = chunks(q) * (Dk ** -0.5)
    k = chunks(k)
    v = chunks(v)
    g = g.astype(f32).reshape(B, n, C, H).transpose(0, 3, 1, 2)
    beta = beta.astype(f32).reshape(B, n, C, H).transpose(0, 3, 1, 2)
    G = jnp.cumsum(g, axis=-1)
    idx = jnp.arange(C)
    incl = idx[:, None] >= idx[None, :]
    strict = idx[:, None] > idx[None, :]
    gamma = jnp.exp(jnp.where(incl, G[..., :, None] - G[..., None, :], -jnp.inf))
    kb = k * beta[..., None]
    a_kk = jnp.where(strict, jnp.einsum('bhnid,bhnjd->bhnij', kb, k) * gamma, 0.0)
    tri = a_kk + jnp.eye(C, dtype=f32)
    rhs = jnp.concatenate([v * beta[..., None], kb * jnp.exp(G)[..., None]], axis=-1)
    sol = lax.linalg.triangular_solve(tri, rhs, left_side=True, lower=True, unit_diagonal=True)
    u, w = sol[..., :Dv], sol[..., Dv:]
    qk = jnp.einsum('bhnid,bhnjd->bhnij', q, k) * gamma
    qg = q * jnp.exp(G)[..., None]
    kd = k * jnp.exp(G[..., -1:] - G)[..., None]
    dc = jnp.exp(G[..., -1])

    def step(state, xs):
        u_c, w_c, qk_c, qg_c, kd_c, dc_c = xs
        v_new = u_c - jnp.einsum('bhcd,bhde->bhce', w_c, state)
        o_c = jnp.einsum('bhcd,bhde->bhce', qg_c, state) + jnp.einsum('bhij,bhje->bhie', qk_c, v_new)
        state = state * dc_c[..., None, None] + jnp.einsum('bhcd,bhce->bhde', kd_c, v_new)
        return state, o_c

    xs = tuple(jnp.moveaxis(t, 2, 0) for t in (u, w, qk, qg, kd, dc))
    state0 = jnp.zeros((B, H, Dk, Dv), f32)
    _, o = lax.scan(step, state0, xs)
    return o.transpose(1, 0, 3, 2, 4).reshape(B, S, H, Dv)

def _causal_window_attention(q, k, v, span):
    N, L, H, Dh = q.shape
    nb = -(-L // ATTN_BLOCK)
    pad = nb * ATTN_BLOCK - L
    qb = jnp.pad(q, ((0, 0), (0, pad), (0, 0), (0, 0))).reshape(N, nb, ATTN_BLOCK, H, Dh)

    def kv_blocks(t):
        t = jnp.pad(t, ((0, 0), (ATTN_BLOCK, pad), (0, 0), (0, 0))).reshape(N, nb + 1, ATTN_BLOCK, H, Dh)
        return jnp.concatenate([t[:, :-1], t[:, 1:]], axis=2)

    kw, vw = kv_blocks(k), kv_blocks(v)
    s = jnp.einsum('nbqhd,nbkhd->nbhqk', qb, kw, preferred_element_type=jnp.float32)
    qi = jnp.arange(ATTN_BLOCK)[:, None]
    ki = jnp.arange(2 * ATTN_BLOCK)[None, :]
    dist = qi + ATTN_BLOCK - ki
    key_pos = jnp.arange(nb)[:, None, None] * ATTN_BLOCK - ATTN_BLOCK + ki[None]
    valid = (dist >= 0) & (dist <= span) & (key_pos >= 0)
    s = jnp.where(valid[None, :, None], s, -jnp.inf)
    lse = jax.nn.logsumexp(s, axis=-1)
    p = jnp.exp(s - lse[..., None])
    o = jnp.einsum('nbhqk,nbkhd->nbqhd', p, vw.astype(jnp.float32))
    o = o.reshape(N, nb * ATTN_BLOCK, H, Dh)[:, :L]
    lse = lse.transpose(0, 1, 3, 2).reshape(N, nb * ATTN_BLOCK, H)[:, :L]
    return o, lse

def _dilated_attention(q, k, v):
    B, S, H, Dh = q.shape
    q = q * (Dh ** -0.5)
    outs, lses = [], []
    for window, dil in DILATED_CONFIGS:
        L = S // dil

        def by_residue(t):
            return t.reshape(B, L, dil, H, Dh).transpose(0, 2, 1, 3, 4).reshape(B * dil, L, H, Dh)

        o, lse = _causal_window_attention(by_residue(q), by_residue(k), by_residue(v), window // dil)
        outs.append(o.reshape(B, dil, L, H, Dh).transpose(0, 2, 1, 3, 4).reshape(B, S, H, Dh))
        lses.append(lse.reshape(B, dil, L, H).transpose(0, 2, 1, 3).reshape(B, S, H))
    wts = jax.nn.softmax(jnp.stack(lses), axis=0)
    o = jnp.einsum('gbsh,gbshd->bshd', wts, jnp.stack(outs))
    return o.astype(v.dtype)

def _hybrid_mixer(h, cos, sin, w_in, dn_conv, dn_a_log, dn_dt_bias, dn_out_norm, w_out):
    B, S, _ = h.shape
    proj = h @ w_in
    a_qkv, a_z, a_b, a_a, b_q, b_k, b_v = jnp.split(proj, np.cumsum(IN_SPLITS)[:-1], axis=-1)
    a_qkv = jax.nn.silu(_causal_dwconv(a_qkv, dn_conv))
    aq, ak, av = jnp.split(a_qkv, 3, axis=-1)
    heads_a = lambda t: t.reshape(B, S, DN_HEADS, DN_HEAD_DIM)
    aq, ak, av = _l2norm(heads_a(aq)), _l2norm(heads_a(ak)), heads_a(av)
    beta = jax.nn.sigmoid(a_b.astype(jnp.float32))
    g = -jnp.exp(dn_a_log.astype(jnp.float32)) * jax.nn.softplus(a_a.astype(jnp.float32) + dn_dt_bias.astype(jnp.float32))
    o_a = _gated_delta_rule(aq, ak, av, g, beta).astype(h.dtype)
    o_a = _rmsnorm(o_a, dn_out_norm) * jax.nn.silu(heads_a(a_z))
    heads_b = lambda t: t.reshape(B, S, SWA_HEADS, SWA_HEAD_DIM)
    bq = _partial_rope(heads_b(b_q), cos, sin)
    bk = _partial_rope(heads_b(b_k), cos, sin)
    o_b = _dilated_attention(bq, bk, heads_b(b_v))
    mixed = jnp.concatenate([o_a.reshape(B, S, DN_WIDTH), o_b.reshape(B, S, SWA_WIDTH)], axis=-1)
    return mixed @ w_out

def _conv_glu_ffn(h, ffn_up, ffn_conv, ffn_conv_bias, ffn_down):
    u = _causal_dwconv(h @ ffn_up, ffn_conv) + ffn_conv_bias
    gate, val = jnp.split(u, 2, axis=-1)
    return (jax.nn.gelu(gate, approximate=True) * val) @ ffn_down

def second_inputs(seed: int = 0) -> dict:
    key = jax.random.key(seed)
    ks = jax.random.split(key, 16)
    f32 = jnp.float32

    def normal(k, shape, scale):
        return jax.random.normal(k, shape, f32) * scale

    def gain(k, shape):
        return 1.0 + 0.02 * jax.random.normal(k, shape, f32)

    x = normal(ks[0], (BATCH, SEQ, D_MODEL), 1.0)
    pre_mix_norm = gain(ks[1], (DEPTH, D_MODEL))
    w_in = normal(ks[2], (DEPTH, D_MODEL, IN_WIDTH), D_MODEL ** -0.5)
    dn_conv = normal(ks[3], (DEPTH, DN_CONV, 3 * DN_WIDTH), DN_CONV ** -0.5)
    dn_a_log = jnp.log(jax.random.uniform(ks[4], (DEPTH, DN_HEADS), f32, 1.0, 16.0))
    dt = jnp.exp(jax.random.uniform(ks[5], (DEPTH, DN_HEADS), f32, math.log(1e-3), math.log(1e-1)))
    dn_dt_bias = dt + jnp.log(-jnp.expm1(-dt))
    dn_out_norm = gain(ks[6], (DEPTH, DN_HEAD_DIM))
    w_out = normal(ks[7], (DEPTH, D_MIX, D_MODEL), D_MIX ** -0.5)
    post_mix_norm = gain(ks[8], (DEPTH, D_MODEL))
    pre_ffn_norm = gain(ks[9], (DEPTH, D_MODEL))
    ffn_up = normal(ks[10], (DEPTH, D_MODEL, 2 * D_FF_2), D_MODEL ** -0.5)
    ffn_conv = normal(ks[11], (DEPTH, FFN_CONV, 2 * D_FF_2), FFN_CONV ** -0.5)
    ffn_conv_bias = normal(ks[12], (DEPTH, 2 * D_FF_2), 0.02)
    ffn_down = normal(ks[13], (DEPTH, D_FF_2, D_MODEL), D_FF_2 ** -0.5)
    post_ffn_norm = gain(ks[14], (DEPTH, D_MODEL))
    return {"x": x, "pre_mix_norm": pre_mix_norm, "w_in": w_in, "dn_conv": dn_conv,
            "dn_a_log": dn_a_log, "dn_dt_bias": dn_dt_bias, "dn_out_norm": dn_out_norm,
            "w_out": w_out, "post_mix_norm": post_mix_norm, "pre_ffn_norm": pre_ffn_norm,
            "ffn_up": ffn_up, "ffn_conv": ffn_conv, "ffn_conv_bias": ffn_conv_bias,
            "ffn_down": ffn_down, "post_ffn_norm": post_ffn_norm}

def second_block(x, pre_mix_norm, w_in, dn_conv, dn_a_log, dn_dt_bias, dn_out_norm, w_out,
              post_mix_norm, pre_ffn_norm, ffn_up, ffn_conv, ffn_conv_bias, ffn_down, post_ffn_norm):
    S = x.shape[1]
    cos, sin = _rope_tables(S)
    for l in range(DEPTH):
        h = _rmsnorm(x, pre_mix_norm[l])
        h = _hybrid_mixer(h, cos, sin, w_in[l], dn_conv[l], dn_a_log[l], dn_dt_bias[l], dn_out_norm[l], w_out[l])
        x = x + _rmsnorm(h, post_mix_norm[l])
        h = _rmsnorm(x, pre_ffn_norm[l])
        h = _conv_glu_ffn(h, ffn_up[l], ffn_conv[l], ffn_conv_bias[l], ffn_down[l])
        x = x + _rmsnorm(h, post_ffn_norm[l])
    return x


def setup_inputs(seed=0):
    out = dict(first_inputs(seed))
    for name, value in second_inputs(seed + 1).items():
        if name != "x":
            out[name + "_2"] = value
    return out


def reference(
    x, p, positions, w_qkv, w_o, ln_mix_g, ln_mix_b, ln_ffn_g, ln_ffn_b, sinks, w_ffn_gate,
    w_ffn_up, w_ffn_down, w_router, w_exp_gate, w_exp_up, w_exp_down, w_ple_proj, w_ple_gate,
    pre_mix_norm_2, w_in_2, dn_conv_2, dn_a_log_2, dn_dt_bias_2, dn_out_norm_2, w_out_2,
    post_mix_norm_2, pre_ffn_norm_2, ffn_up_2, ffn_conv_2, ffn_conv_bias_2, ffn_down_2,
    post_ffn_norm_2,
):
    x = first_block(
        x, p, positions, w_qkv, w_o, ln_mix_g, ln_mix_b, ln_ffn_g, ln_ffn_b, sinks, w_ffn_gate,
        w_ffn_up, w_ffn_down, w_router, w_exp_gate, w_exp_up, w_exp_down, w_ple_proj,
        w_ple_gate,
    )
    return second_block(
        x, pre_mix_norm_2, w_in_2, dn_conv_2, dn_a_log_2, dn_dt_bias_2, dn_out_norm_2, w_out_2,
        post_mix_norm_2, pre_ffn_norm_2, ffn_up_2, ffn_conv_2, ffn_conv_bias_2, ffn_down_2,
        post_ffn_norm_2,
    )


_drawn_inputs = setup_inputs


def setup_inputs(seed=0):
    import zlib

    import numpy as np

    out = dict(_drawn_inputs(seed))
    spreads = {}
    factors = {'sinks': 5.671, 'post_ffn_norm_2': 3.32}
    for name, (base, spread) in spreads.items():
        noise = np.random.default_rng([zlib.crc32(name.encode()), seed]).standard_normal(out[name].shape)
        drawn = base * np.exp(spread * noise) if base else spread * noise
        out[name] = __import__('jax').numpy.asarray(drawn.astype(out[name].dtype))
    for name, factor in factors.items():
        out[name] = (out[name] * factor).astype(out[name].dtype)
    return out
```

```python
from contextlib import ExitStack

import numpy as np
import concourse.bass as bass
from concourse import mybir

F32 = mybir.dt.float32
I32 = mybir.dt.int32
ALU = mybir.AluOpType
ACT = mybir.ActivationFunctionType
AXX = mybir.AxisListType.X

P = 128
S = 256
NT = S // P
DM = 1024
KC = DM // P
NHEAD = 16
DH = 64
FF1 = 3584
FF2 = 2816
NE = 8
UNIT = 2048
RING = 7
NEG = -1.0e30
ALPHA = float((2.0 * 2) ** 0.25)
LN_EPS = 1e-5
RMS_EPS = 1e-6
DN_H = 4
N_DN = DN_H * NT
LEVELS = 7
MAGIC = 12582912.0
NVEC = 12
VSLOTS = 4

FFN_STEPS = {0: FF1 // 256, 2: FF2 // 256, 3: FF2 // 256}
EXP_STEPS = FF1 // 512


def constants():
    p = np.arange(P)[:, None]
    f = np.arange(P)[None, :]
    parts = {}
    parts["ident"] = (p == f)
    parts["ones"] = np.ones((P, P))
    parts["upto"] = (p <= f)
    parts["before"] = (p < f)
    q0, q1 = np.arange(P)[:, None], P + np.arange(P)[:, None]
    k0, k1 = np.arange(P)[None, :], np.arange(S)[None, :]

    def both(rule):
        return np.concatenate([rule(q0 - k0), rule(q1 - k1)], axis=1)
    parts["mask_causal"] = both(lambda d: np.where(d >= 0, 0.0, NEG))
    parts["mask_window"] = both(lambda d: np.where((d >= 0) & (d < 128), 0.0, NEG))

    def dilated(d):
        n = ((d >= 0) & (d <= 128)).astype(np.float64)
        n = n + ((d >= 0) & (d % 4 == 0)) + ((d >= 0) & (d % 16 == 0))
        return np.where(n > 0, np.log(np.maximum(n, 1.0)), NEG)
    parts["mask_dilated"] = both(dilated)
    parts["mask_gamma"] = np.where(f >= p, 0.0, NEG)
    for n in range(LEVELS):
        b = 1 << n
        same = (p // (2 * b)) == (f // (2 * b))
        parts[f"level{n}"] = same & ((f // b) % 2 == 1) & ((p // b) % 2 == 0)
    parts["iota"] = np.broadcast_to(np.arange(S)[None, :], (P, S))
    parts["rank"] = np.broadcast_to(8.0 - np.arange(NE)[None, :], (P, NE))
    inv = (1.0 / (np.float32(500000.0) ** (np.arange(0, 16, 2, dtype=np.float32) / np.float32(16)))).astype(np.float32)
    parts["inv"] = np.broadcast_to(inv[None, :], (P, 8))
    inv2 = (np.float32(500000.0) ** (-np.arange(0, 16, 2, dtype=np.float32) / np.float32(16))).astype(np.float32)
    ang = np.arange(S, dtype=np.float32)[:, None] * inv2[None, :]
    tab = ang.reshape(NT, P, 8).transpose(1, 0, 2).reshape(P, NT * 8).astype(np.float64)
    parts["cos2"] = np.cos(tab)
    parts["sin2"] = np.sin(tab)
    parts["ln_eps"] = np.full((P, 1), LN_EPS)
    parts["rms_eps"] = np.full((P, 1), RMS_EPS)
    at, cols, n = {}, [], 0
    for name, a in parts.items():
        a = np.asarray(a, dtype=np.float32)
        at[name] = (n, a.shape[1])
        n += a.shape[1]
        cols.append(a)
    return np.ascontiguousarray(np.concatenate(cols, axis=1)), at


class Plan:

    def __init__(self):
        self.value, self.per, self.in_loop, self.opens = {}, {}, set(), {}


class Events:

    def __init__(self, nc, ctx, plan, tag):
        self.nc, self.ctx, self.plan, self.tag = nc, ctx, plan, tag
        self.turn, self.marked, self.seen = None, None, 0

    def new(self, name, step=1):
        return Event(self, name, step)

    def loop(self, turn):
        return Turns(self, turn)


class Turns:

    def __init__(self, events, turn):
        self.events, self.turn = events, turn

    def __enter__(self):
        self.events.turn, self.events.marked = self.turn, {}

    def __exit__(self, *_):
        ev = self.events
        for event, n in ev.marked.items():
            ev.plan.per[event.name] = n
            event.n += (NE - 1) * n
        ev.turn = ev.marked = None


class Event:
    counts = False

    def __init__(self, events, name, step):
        self.ev, self.name, self.step, self.n = events, events.tag + name, step, 0
        self.sem = events.ctx.enter_context(events.nc.semaphore(self.name)) if step else None

    def _turns(self):
        per = self.ev.plan.per.get(self.name, 0)
        return self.ev.turn * per if self.ev.turn is not None and per else 0

    def mark(self, *key):
        self.n += self.step or 1
        if self.ev.marked is not None:
            self.ev.marked[self] = self.ev.marked.get(self, 0) + (self.step or 1)
            self.ev.plan.in_loop.add((self.name, key))
        self.ev.plan.value[self.name, key] = self.n
        return self.sem, self.step

    def at(self, *key):
        v = self.ev.plan.value.get((self.name, key), 1)
        if self.counts:
            self.ev.seen = max(self.ev.seen, v + (self.ev.turn is None and (self.name, key) in self.ev.plan.in_loop)
                               * (NE - 1) * self.ev.plan.per.get(self.name, 0))
        if self.ev.turn is not None:
            return self.sem, v + self._turns()
        if (self.name, key) in self.ev.plan.in_loop:
            v += (NE - 1) * self.ev.plan.per.get(self.name, 0)
        return self.sem, v

    def last(self):
        return self.sem, self.n + self._turns()


class Groups(Event):
    counts = True


class Free(Event):

    def opened(self, groups):
        opens = self.ev.plan.opens.setdefault(self.name, [])
        turns = self._turns()
        n = self.n
        self.n += 1
        if self.ev.marked is not None:
            self.ev.marked[self] = self.ev.marked.get(self, 0) + 1
        opens.append((groups.n, self.n))
        return n, n + turns

    def mark(self, *key):
        use = 1
        for before, n in self.ev.plan.opens.get(self.name, ()):
            if before < self.ev.seen:
                use = max(use, n)
        self.ev.plan.value[self.name, key] = use
        if self.ev.marked is not None:
            self.ev.plan.in_loop.add((self.name, key))
        return self.sem, 1


def build_program(nc, A, plan, debug=None):
    cst_np, cst_at = constants()
    NC = cst_np.shape[1]
    with ExitStack() as ctx:
        def sb(name, shape, dt=F32):
            return ctx.enter_context(nc.sbuf_tensor(name, shape, dt))

        ring = sb("ring", [P, RING, UNIT])
        cst = sb("cst", [P, NC])
        X = sb("X", [P, NT, DM])
        R = sb("R", [P, NT, DM])
        xT = sb("xT", [P, KC, S])
        aT = sb("aT", [P, KC, S])
        vec = sb("vec", [P, VSLOTS, DM])
        small = sb("small", [P, 640])
        pos_i = sb("pos_i", [P, NT], I32)
        flag_i = sb("flag_i", [P, 1], I32)
        ARENA = 14400
        arena = sb("arena", [P, ARENA])

        def carve(start, shapes):
            out, at = {}, start
            for name, shape in shapes:
                n = int(np.prod(shape))
                ap = arena[:, at:at + n]
                if len(shape) > 1:
                    letters = "abcd"[:len(shape)]
                    ap = ap.rearrange("p (" + " ".join(letters) + ") -> p " + " ".join(letters),
                                      **{c: s for c, s in zip(letters[1:], shape[1:])})
                out[name] = ap
                at += n
            assert at <= ARENA, at
            return out

        att = carve(0, [("qn", (NT, 1536)), ("kd", (NT, 4, 2, DH)), ("qT", (8, S)), ("kT", (4, S)),
                        ("s", (2, 384)), ("pr", (2, 384)), ("pt", (2, 384)), ("tmp", (4, 24, 8)),
                        ("sg", (4, 512))])
        dn = carve(0, [("cv", (12, S)), ("z", (NT, 512)), ("gB", (N_DN, P)), ("bB", (N_DN, P)),
                       ("gam", (N_DN, P)), ("kb", (DN_H, S)), ("LT", (N_DN, P)), ("D", (N_DN, P)),
                       ("DT", (N_DN, P)), ("Xl", (N_DN, P)), ("vb", (N_DN, P)), ("kbg", (DN_H, P)),
                       ("kdec", (DN_H, P))])
        dn["AT"] = dn["gB"]
        dn["qk"] = dn["bB"]
        dn["u"] = dn["LT"]
        dn["wT"] = dn["Xl"][:, 0:DN_H, :]
        dn["state"] = dn["Xl"][:, DN_H:, :]
        dn["vn"] = dn["kdec"]
        dn["o"] = dn["D"]
        dn["sq"] = dn["gam"]
        ffn = carve(0, [("hT", (2, 2, S)), ("sg", (2, 2, S)), ("cbg", (2, 2, S)), ("cbv", (2, 2, S)),
                        ("gg", (2, 2, S))])
        moe = carve(0, [("xe", (KC, P)), ("sel", (NT, P)), ("selg", (NT, P)), ("sgT", (S,)),
                        ("sg", (2, 512)), ("h", (2, 512)), ("hTe", (2, 4, P)), ("ye", (DM,))])

        bank = [ctx.enter_context(nc.psum_tensor(f"bank{b}", [P, 512], F32)) for b in range(8)]

        def C(name, a=0, b=None):
            at, n = cst_at[name]
            return cst[:, at + a:at + (n if b is None else b)]

        ident, ones = C("ident"), C("ones")
        used = [0]

        def sm(*shape):
            n = int(np.prod(shape))
            ap = small[:, used[0]:used[0] + n]
            used[0] += n
            if len(shape) > 1:
                letters = "abcd"[:len(shape)]
                ap = ap.rearrange("p (" + " ".join(letters) + ") -> p " + " ".join(letters),
                                  **{c: s for c, s in zip(letters[1:], shape[1:])})
            return ap
        cos1, sin1 = sm(NT, 8), sm(NT, 8)
        ang, red, rnd = sm(NT, 8), sm(NT, 8), sm(NT, 8)
        pos_f = sm(NT)
        sinks = sm(NHEAD)
        nmax, rsum, esink, rden = sm(2, 2), sm(2, 2), sm(2, 2), sm(2, 2)
        st6, mv, sd, rstd = sm(NT, 2, 6), sm(NT, 2), sm(NT), sm(NT)
        ss = sm(NT, DN_H)
        lg, lg2, oh1, oh2, sc8 = sm(NT, NE), sm(NT, NE), sm(NT, NE), sm(NT, NE), sm(NT, NE)
        m1, m2, w1, w2 = sm(NT), sm(NT), sm(NT), sm(NT)
        memb, gates, posx = sm(NT, NE), sm(NT, NE), sm(NT, NE)
        pcol, gcol = sm(NT), sm(NT)
        flag_f = sm(1)
        tick = sm(9)
        ba, beta, sp1, sp2, gl = sm(NT, 8), sm(NT, DN_H), sm(NT, DN_H), sm(NT, DN_H), sm(NT, DN_H)
        alog, dtb = sm(2, DN_H), sm(2, DN_H)
        ngc, expg, kdsc, bexp = sm(NT, DN_H), sm(NT, DN_H), sm(DN_H), sm(DN_H)
        rn8 = sm(NT, DN_H)
        nsink = sm(NHEAD)
        junk = sb("junk", [P, NT, DM])[:, :, :]
        wr = sb("wr", [P, KC, NE])
        wba = sb("wba", [P, KC, 8])
        pT = sb("pT", [P, 2, S])
        cw = sb("cw", [P, 12, 4])
        fcw = sb("fcw", [P, 44, 4])
        prew = sb("prew", [P, 2, KC])
        onorm = sb("onorm", [P, P])

        def events(tag):
            ev = Events(nc, ctx, plan, tag)

            class E:
                pass
            E.ev = ev
            E.groups = Groups(ev, "groups", 1)
            E.free = [Free(ev, f"free{b}", 1) for b in range(8)]
            E.dve = ev.new("dve_step")
            E.act = ev.new("act_step")
            E.loaded = [ev.new(f"loaded{s}", 16) for s in range(RING)]
            return E
        M = events("")
        V = events("ovf_")
        for event in V.free + [V.groups]:
            event.n = 1
        ev = M.ev
        x_ready = ev.new("x_ready")
        params = ev.new("params_loaded", 16)
        consts = ev.new("consts_loaded", 16)
        vecs = [ev.new(f"vec_loaded{s}", 16) for s in range(VSLOTS)]
        vec_used = ev.new("vec_used")
        stored = ev.new("stored", 16)
        probs, roped, maxed, exped = ev.new("probs"), ev.new("roped"), ev.new("maxed"), ev.new("exped")
        stats, rooted, prenorm, hidden = ev.new("stats"), ev.new("rooted"), ev.new("prenorm"), ev.new("hidden")
        member, decided, flag_done = ev.new("member"), ev.new("decided"), ev.new("flag_done")
        angles, angles_done = ev.new("angles"), ev.new("angles_done")
        squares, decay, normed, inverse, gated = (ev.new("squares"), ev.new("decay"), ev.new("normed"), ev.new("inverse"),
                                                  ev.new("gated"))

        def hidden_at(L, s):
            return M.free[5 + 2 * (s % 2)].at("h", L, s) if L == 0 else hidden.at(L, s)

        def overflow_done():
            return V.free[3].at("ovf", "sc", 1, 1)

        def stream_order():
            for L in range(4):
                if L < 2:
                    yield from [(("qkv", L, i), "wu_qkv", (L, i)) for i in range(6)]
                    yield from [(("wo", L, i), "wu_o", (L, i)) for i in range(4)]
                else:
                    yield from [(("in", L, i), "wu_in", (L - 2, i)) for i in range(14)]
                    yield from [(("wo", L, i), "wu_out", (L - 2, i)) for i in range(4)]
                if L == 1:
                    yield (("experts",), None, None)
                else:
                    n = FFN_STEPS[L]
                    gu, dw, pre = ("wu_ffn_gu", "wu_ffn_d", ()) if L == 0 else ("wu_up", "wu_down", (L - 2,))
                    for s in range(n):
                        yield (("gu", L, s, 0), gu, pre + (s, 0))
                        yield (("gu", L, s, 1), gu, pre + (s, 1))
                        if s:
                            yield (("dn", L, s - 1), dw, pre + (s - 1,))
                    yield (("dn", L, n - 1), dw, pre + (n - 1,))
                if L < 2:
                    yield (("pp", L), "wu_pp", (L,))
                    yield from [(("pg", L, i), "wu_pg", (L, i)) for i in range(4)]

        def expert_order():
            def gu(f):
                return [(("gu", f, h, i), ("wu_eg", "wu_eu")[h], (f, i)) for h in range(2) for i in range(2)]

            def down(f):
                return [(("dn", f, i), "wu_ed", (f, i)) for i in range(2)]
            out = gu(0)
            for f in range(EXP_STEPS):
                if f + 1 < EXP_STEPS:
                    out += gu(f + 1)
                if f:
                    out += down(f - 1)
            return out + down(EXP_STEPS - 1)
        EXPERT = expert_order()
        assert len(EXPERT) % RING == 0
        unit_at, n = {}, 0
        for key, arr, idx in stream_order():
            if key == ("experts",):
                expert_base = n
                n += NE * len(EXPERT)
            else:
                unit_at[key] = n
                n += 1
        last_read = plan.value.setdefault("last_read", {})

        def unit(E, eng, key, base=None):
            i = unit_at[key] if base is None else base + [k for k, _, _ in EXPERT].index(key)
            slot, n = i % RING, 16 * (i // RING + 1)
            if base is not None:
                n = n + E.ev.turn * (16 * len(EXPERT) // RING)
            eng.wait_ge(E.loaded[slot].sem, n)
            return ring[:, slot, :]

        def released(E, i, *key):
            last_read[E.ev.tag, i] = key

        block = ctx.enter_context(nc.Block())

        @block.sync
        def _(sp):
            for key, arr, idx in stream_order():
                if key == ("experts",):
                    sp.wait_ge(*M.groups.at(*last_read.get(("", expert_base - 1), ("none",))))
                    with sp.Fori(0, NE) as e:
                        with ev.loop(e):
                            for j, (ekey, earr, eidx) in enumerate(EXPERT):
                                i = expert_base + j
                                before = (j - RING) % len(EXPERT)
                                sem, v = M.groups.at(*last_read.get(("", expert_base + before), ("none",)))
                                sp.wait_ge(sem, v - plan.per.get("groups", 0) if j < RING else v)
                                sp.dma_start(ring[:, i % RING, :], A[earr][e, eidx[0], eidx[1]]) \
                                    .then_inc(*M.loaded[i % RING].mark())
                    sp.wait_ge(*flag_done.at())
                    r = sp.value_load(flag_i[0:1, 0:1], min_val=0, max_val=1)
                    with sp.If(r > 0):
                        sp.wait_ge(*M.free[3].at("moe", "sc", 1, 1))
                        with sp.Fori(0, NE) as e:
                            with V.ev.loop(e):
                                sp.wait_ge(V.groups.sem, e * plan.per.get("ovf_groups", 0) + 1)
                                for j, (ekey, earr, eidx) in enumerate(EXPERT):
                                    if j >= RING:
                                        sp.wait_ge(*V.groups.at(*last_read.get(("ovf_", j - RING), ("none",))))
                                    sp.dma_start(ring[:, j % RING, :], A[earr][e, eidx[0], eidx[1]]) \
                                        .then_inc(*V.loaded[j % RING].mark())
                        sp.wait_ge(*overflow_done())
                    continue
                i = unit_at[key]
                if i >= RING:
                    old = i - RING
                    if expert_base <= old < expert_base + NE * len(EXPERT):
                        old = expert_base + (old - expert_base) % len(EXPERT)
                    sp.wait_ge(*M.groups.at(*last_read.get(("", old), ("none",))))
                src = A[arr][idx] if len(idx) > 1 else A[arr][idx[0]]
                sp.dma_start(ring[:, i % RING, :], src).then_inc(*M.loaded[i % RING].mark())
            sp.wait_ge(*x_ready.at(3, "ffn", 1))
            sp.dma_start(A["out"].rearrange("(t p) d -> p t d", p=P), X[:, :, :]).then_inc(*stored.mark())
            sp.wait_ge(*stored.at())

        @block.gpsimd
        def _(gp):
            def load(*loads):
                for dst, src, key in loads:
                    gp.dma_start(dst, src).then_inc(*params.mark())
                for dst, src, key in loads:
                    plan.value[params.name, key] = params.n

            def load_vec(v):
                s = v % VSLOTS
                if v >= VSLOTS:
                    old = v - VSLOTS
                    if old % 2 == 0:
                        gp.wait_ge(*vec_used.at(old))
                    else:
                        gp.wait_ge(*x_ready.at(old // 4, "mix" if old % 4 == 1 else "ffn", 1))
                gp.dma_start(vec[:, s, :], A["vecs"][v]).then_inc(*vecs[s].mark())
            gp.dma_start(cst[:, :], A["cst"]).then_inc(*consts.mark())
            load((pos_i[:, :], A["positions"], ("pos",)), (sinks, A["sinks"], ("sinks",)),
                 (X[:, :, :], A["x"].rearrange("(t p) d -> p t d", p=P), ("X",)), (xT[:, :, :], A["xT"], ("xT",)),
                 (alog, A["alog"], ("alog",)), (dtb, A["dtb"], ("dtb",)), (wr[:, :, :], A["wr"], ("wr",)),
                 (pT[:, :, :], A["pT"][0], ("pT", 0)))
            for v in range(8):
                load_vec(v)
            gp.wait_ge(*M.groups.at("pp", 0, 1, 1))
            gp.wait_ge(*params.last())
            load((pT[:, :, :], A["pT"][1], ("pT", 1)))
            for L in (2, 3):
                for v in (4 + 2 * L, 5 + 2 * L):
                    load_vec(v)
                if L == 3:
                    gp.wait_ge(*x_ready.at(2, "ffn", 1))
                gp.wait_ge(*params.last())
                load((wba[:, :, :], A["wba"][L - 2], ("wba", L)), (cw[:, :, :], A["cw"][L - 2], ("cw", L)),
                     (fcw[:, :, :], A["fcw"][L - 2], ("fcw", L)), (prew[:, :, :], A["prew"][L - 2], ("prew", L)),
                     (onorm[:, :], A["onorm"][L - 2], ("onorm", L)))
            if debug:
                k = 0
                for L, w in debug["dump"]:
                    gp.wait_ge(*x_ready.at(L, w, 1))
                    gp.dma_start(A["dbg"][k].rearrange("(t p) d -> p t d", p=P), X[:, :, :]).then_inc(*stored.mark("dbg", k))
                    k += 1

        @block.tensor
        def _(pe):
            def open_bank(E, b):
                before, n = E.free[b].opened(E.groups)
                if before:
                    pe.wait_ge(E.free[b].sem, n)
                return bank[b]

            def transposes(stage, src, ready):
                for t in range(NT):
                    pe.wait_ge(*ready(t))
                    for g in range(2):
                        o = open_bank(M, 2 * t + g)
                        for c in range(4):
                            mm = nc.tensor.transpose(o[:, c * P:(c + 1) * P],
                                                     src[:, t, (4 * g + c) * P:(4 * g + c + 1) * P], ident)
                        mm.then_inc(*M.groups.mark("tx", stage, t, g))

            def linear(name, L, blocks, units, lhs, first=0):
                for nb in range(blocks):
                    u = [unit(M, pe, (units, L, 2 * (first + nb) + i)) for i in range(2)]
                    for t in range(NT):
                        o = open_bank(M, (2 * nb + t) % 4)
                        for kc in range(KC):
                            mm = nc.tensor.matmul(o[:, :], lhs[:, kc, t * P:(t + 1) * P],
                                                  u[kc // 4][:, (kc % 4) * 512:(kc % 4 + 1) * 512],
                                                  start=(kc == 0), stop=(kc == KC - 1))
                        mm.then_inc(*M.groups.mark(name, L, nb, t))
                    for i in range(2):
                        released(M, unit_at[units, L, 2 * (first + nb) + i], name, L, nb, 1)

            def attention(L, heads, kchunk, out0):
                def scores(h):
                    j, lo = h // 2, DH * (h % 2)
                    o = open_bank(M, 4 + h % 2)
                    q = att["qT"][lo:lo + DH, j, :]
                    k = att["kT"][lo:lo + DH, kchunk(h), :]
                    nc.tensor.matmul(o[:, 0:P], q[:, 0:P], k[:, 0:P], start=True, stop=True)
                    nc.tensor.matmul(o[:, P:3 * P], q[:, P:S], k[:, :], start=True, stop=True) \
                        .then_inc(*M.groups.mark("sc", L, h))

                def turn(h):
                    pe.wait_ge(*probs.at(L, h))
                    o = open_bank(M, 6 + h % 2)
                    for c in range(3):
                        mm = nc.tensor.transpose(o[:, c * P:(c + 1) * P], att["pr"][:, h % 2, c * P:(c + 1) * P], ident)
                    mm.then_inc(*M.groups.mark("pt", L, h))

                def values(h):
                    j, lo = h // 2, DH * (h % 2)
                    o = bank[2 + j % 2] if h % 2 else open_bank(M, 2 + j % 2)
                    pe.wait_ge(*M.free[6 + h % 2].at("pt", L, h))
                    vcol = 1280 + DH * (h // 4) if L < 2 else 1024 + DH * h
                    nc.tensor.matmul(o[lo:lo + DH, 0:S], att["qn"][:, 0, vcol:vcol + DH], att["pt"][:, h % 2, 0:S],
                                     start=True, stop=False)
                    nc.tensor.matmul(o[lo:lo + DH, P:S], att["qn"][:, 1, vcol:vcol + DH], att["pt"][:, h % 2, S:S + P],
                                     start=False, stop=True).then_inc(*M.groups.mark("pv", L, h))
                for i in range(heads + 2):
                    if i < heads:
                        scores(i)
                    if 0 <= i - 1 < heads:
                        turn(i - 1)
                    if i >= 2:
                        values(i - 2)

            def turn_qk(L, nq):
                for t in range(NT):
                    pe.wait_ge(*roped.at(L, t))
                    for g in range(nq // 4 + 1):
                        o = open_bank(M, (3 * t + g) % 4)
                        for c in range(4):
                            if g < nq // 4:
                                src = att["qn"][:, t, (4 * g + c) * P:(4 * g + c + 1) * P]
                            elif L < 2:
                                src = att["kd"][:, t, c, :, :].rearrange("p a b -> p (a b)")
                            else:
                                src = att["qn"][:, t, 512 + c * P:512 + (c + 1) * P]
                            mm = nc.tensor.transpose(o[:, c * P:(c + 1) * P], src, ident)
                        mm.then_inc(*M.groups.mark("qkT", L, t, g))
                for t in range(NT):
                    for g in range(nq // 4 + 1):
                        pe.wait_ge(*M.free[(3 * t + g) % 4].at("qkT", L, t, g))

            def xT_ready(stage):
                for t in range(NT):
                    for g in range(2):
                        pe.wait_ge(*M.free[2 * t + g].at("xT", stage, t, g))

            def dense_ffn(L):
                n = FFN_STEPS[L]

                def gate_up(s):
                    u = [unit(M, pe, ("gu", L, s, i)) for i in range(2)]
                    for half in range(2):
                        o = open_bank(M, 4 + 2 * (s % 2) + half)
                        for m in range(2):
                            for kc in range(KC):
                                c0 = (kc % 4) * 512 + half * 256 + m * P
                                mm = nc.tensor.matmul(o[:, m * S:(m + 1) * S], u[kc // 4][:, c0:c0 + P], xT[:, kc, :],
                                                      start=(kc == 0), stop=(kc == KC - 1))
                        mm.then_inc(*M.groups.mark("gu", L, s, half))
                    for i in range(2):
                        released(M, unit_at["gu", L, s, i], "gu", L, s, 1)

                def down(s):
                    d = unit(M, pe, ("dn", L, s))
                    pe.wait_ge(*hidden_at(L, s))
                    for t in range(NT):
                        for nb in range(2):
                            o = open_bank(M, 2 * t + nb) if s == 0 else bank[2 * t + nb]
                            for m in range(2):
                                mm = nc.tensor.matmul(o[:, :], ffn["hT"][:, s % 2, m, t * P:(t + 1) * P],
                                                      d[:, m * DM + nb * 512:m * DM + (nb + 1) * 512],
                                                      start=(s == 0 and m == 0), stop=(s == n - 1 and m == 1))
                    mm.then_inc(*M.groups.mark("down", L, s))
                    released(M, unit_at["dn", L, s], "down", L, s)
                gate_up(0)
                for s in range(n):
                    if s + 1 < n:
                        gate_up(s + 1)
                    down(s)

            def router():
                for t in range(NT):
                    o = open_bank(M, t)
                    for kc in range(KC):
                        mm = nc.tensor.matmul(o[:, 0:NE], xT[:, kc, t * P:(t + 1) * P], wr[:, kc, :],
                                              start=(kc == 0), stop=(kc == KC - 1))
                    mm.then_inc(*M.groups.mark("router", t))
                pe.wait_ge(*member.at())
                o = open_bank(M, 2)
                nc.tensor.matmul(o[:, 0:NE], C("before"), memb[:, 0, :], start=True, stop=True)
                nc.tensor.matmul(o[:, NE:2 * NE], ones, memb[:, 0, :], start=True, stop=False)
                nc.tensor.matmul(o[:, NE:2 * NE], C("before"), memb[:, 1, :], start=False, stop=True)
                nc.tensor.matmul(o[:, 2 * NE:3 * NE], ones, memb[:, 0, :], start=True, stop=False)
                nc.tensor.matmul(o[:, 2 * NE:3 * NE], ones, memb[:, 1, :], start=False, stop=True) \
                    .then_inc(*M.groups.mark("ranks"))

            def experts(E, tag, base):
                pe.wait_ge(*E.dve.at(tag, "sel"))
                for g in range(2):
                    o = open_bank(E, 2 + g)
                    for c in range(4):
                        for t in range(NT):
                            mm = nc.tensor.matmul(o[:, c * P:(c + 1) * P], X[:, t, (4 * g + c) * P:(4 * g + c + 1) * P],
                                                  moe["sel"][:, t, :], start=(t == 0), stop=(t == NT - 1))
                    mm.then_inc(*E.groups.mark(tag, "ga", g))
                o = open_bank(E, 2)
                for t in range(NT):
                    mm = nc.tensor.transpose(o[:, t * P:(t + 1) * P], moe["selg"][:, t, :], ident)
                mm.then_inc(*E.groups.mark(tag, "tg"))
                for g in range(2):
                    pe.wait_ge(*E.free[2 + g].at(tag, "xe", g))

                def gate_up(f):
                    for half in range(2):
                        u = [unit(E, pe, ("gu", f, half, i), base) for i in range(2)]
                        o = open_bank(E, 4 + 2 * (f % 2) + half)
                        for kc in range(KC):
                            mm = nc.tensor.matmul(o[:, :], moe["xe"][:, kc, :], u[kc // 4][:, (kc % 4) * 512:(kc % 4 + 1) * 512],
                                                  start=(kc == 0), stop=(kc == KC - 1))
                        mm.then_inc(*E.groups.mark(tag, "gu", f, half))
                        for i in range(2):
                            released(E, base + order.index(("gu", f, half, i)), tag, "gu", f, half)

                def turn(f):
                    pe.wait_ge(*E.free[5 + 2 * (f % 2)].at(tag, "h", f))
                    o = open_bank(E, 2 + f % 2)
                    for c in range(4):
                        mm = nc.tensor.transpose(o[:, c * P:(c + 1) * P], moe["h"][:, f % 2, c * P:(c + 1) * P], ident)
                    mm.then_inc(*E.groups.mark(tag, "tr", f))

                def down(f):
                    d = [unit(E, pe, ("dn", f, i), base) for i in range(2)]
                    pe.wait_ge(*E.free[2 + f % 2].at(tag, "hTe", f))
                    for nb in range(2):
                        o = open_bank(E, nb) if f == 0 else bank[nb]
                        for c in range(4):
                            mm = nc.tensor.matmul(o[:, :], moe["hTe"][:, f % 2, c, :],
                                                  d[c // 2][:, (c % 2) * DM + nb * 512:(c % 2) * DM + (nb + 1) * 512],
                                                  start=(f == 0 and c == 0), stop=(f == EXP_STEPS - 1 and c == 3))
                    mm.then_inc(*E.groups.mark(tag, "dn", f))
                    for i in range(2):
                        released(E, base + order.index(("dn", f, i)), tag, "dn", f)
                order = [k for k, _, _ in EXPERT]
                gate_up(0)
                for f in range(EXP_STEPS):
                    if f + 1 < EXP_STEPS:
                        gate_up(f + 1)
                    turn(f)
                    if f:
                        down(f - 1)
                down(EXP_STEPS - 1)
                pe.wait_ge(*E.free[0].at(tag, "ye", 0))
                pe.wait_ge(*E.free[1].at(tag, "ye", 1))
                for t in range(NT):
                    for nb in range(2):
                        o = open_bank(E, 2 + nb)
                        nc.tensor.matmul(o[:, :], moe["sgT"][:, t * P:(t + 1) * P], moe["ye"][:, nb * 512:(nb + 1) * 512],
                                         start=True, stop=True).then_inc(*E.groups.mark(tag, "sc", t, nb))

            def delta(L):
                for nb in range(3):
                    u = [unit(M, pe, ("in", L, 2 * nb + i)) for i in range(2)]
                    for j in range(2):
                        o = open_bank(M, 2 * (nb % 2) + j)
                        for m in range(2):
                            for kc in range(KC):
                                c0 = (kc % 4) * 512 + (2 * j + m) * P
                                mm = nc.tensor.matmul(o[:, m * S:(m + 1) * S], u[kc // 4][:, c0:c0 + P], xT[:, kc, :],
                                                      start=(kc == 0), stop=(kc == KC - 1))
                        mm.then_inc(*M.groups.mark("cv", L, 2 * nb + j))
                    for i in range(2):
                        released(M, unit_at["in", L, 2 * nb + i], "cv", L, 2 * nb + 1)
                linear("z", L, 1, "in", xT, first=3)
                pe.wait_ge(*params.at("wba", L))
                o = open_bank(M, 2)
                for t in range(NT):
                    for kc in range(KC):
                        mm = nc.tensor.matmul(o[:, t * 8:t * 8 + 8], xT[:, kc, t * P:(t + 1) * P], wba[:, kc, :],
                                              start=(kc == 0), stop=(kc == KC - 1))
                mm.then_inc(*M.groups.mark("ba", L))
                for g in range(4):
                    pe.wait_ge(*squares.at(L, g))
                    o = open_bank(M, 4 + g)
                    nc.tensor.matmul(o[:, :], ones, dn["sq"][:, 4 * (g % 2):4 * (g % 2) + 4, :].rearrange("p a b -> p (a b)"),
                                     start=True, stop=True).then_inc(*M.groups.mark("ssq", L, g))
                pe.wait_ge(*decay.at(L, "g"))
                o = open_bank(M, 6)
                for t in range(NT):
                    mm = nc.tensor.matmul(o[:, t * DN_H:(t + 1) * DN_H], C("upto"), gl[:, t, :], start=True, stop=True)
                mm.then_inc(*M.groups.mark("gcol", L))
                pe.wait_ge(*decay.at(L, "rows"))
                for name, src, rhs, b0 in (("grow", dn["gB"], C("upto"), 0), ("brow", dn["bB"], ident, 2)):
                    for t in range(NT):
                        o = open_bank(M, b0 + t)
                        for h in range(DN_H):
                            mm = nc.tensor.matmul(o[:, h * P:(h + 1) * P], src[:, t * DN_H + h, :], rhs, start=True, stop=True)
                        mm.then_inc(*M.groups.mark(name, L, t))
                pe.wait_ge(*normed.at(L, 3))
                for name, c0, b0 in (("kn", DN_H, 4), ("vn", 2 * DN_H, 6)):
                    for t in range(NT):
                        o = open_bank(M, b0 + t)
                        for h in range(DN_H):
                            mm = nc.tensor.transpose(o[:, h * P:(h + 1) * P], dn["cv"][:, c0 + h, t * P:(t + 1) * P], ident)
                        mm.then_inc(*M.groups.mark(name, L, t))
                for name, b0 in (("kk", 0), ("kq", 2)):
                    for t in range(NT):
                        if name == "kk":
                            pe.wait_ge(*M.free[2 + t].at("brow", L, t))
                        o = open_bank(M, b0 + t)
                        for h in range(DN_H):
                            rhs = dn["kb"][:, h, t * P:(t + 1) * P] if name == "kk" else dn["cv"][:, h, t * P:(t + 1) * P]
                            mm = nc.tensor.matmul(o[:, h * P:(h + 1) * P], dn["cv"][:, DN_H + h, t * P:(t + 1) * P], rhs,
                                                  start=True, stop=True)
                        mm.then_inc(*M.groups.mark(name, L, t))
                for n in range(LEVELS):
                    for t in range(NT):
                        pe.wait_ge(*inverse.at(L, n, "LT", t))
                        o = open_bank(M, t)
                        for h in range(DN_H):
                            i = t * DN_H + h
                            if n == 0:
                                mm = nc.tensor.transpose(o[:, h * P:(h + 1) * P], dn["LT"][:, i, :], ident)
                            else:
                                mm = nc.tensor.matmul(o[:, h * P:(h + 1) * P], dn["LT"][:, i, :], dn["D"][:, i, :], start=True, stop=True)
                        mm.then_inc(*M.groups.mark("lv", L, n, "X", t))
                    if n == 0:
                        continue
                    for t in range(NT):
                        pe.wait_ge(*M.free[t].at("lv", L, n, "X", t))
                        for which, b in ((0, 2 + t), (1, 4 + t)):
                            if which == 0 and n == LEVELS - 1:
                                continue
                            o = open_bank(M, b)
                            for h in range(DN_H):
                                i = t * DN_H + h
                                a, r = (dn["DT"], dn["Xl"]) if which == 0 else (dn["Xl"], dn["DT"])
                                mm = nc.tensor.matmul(o[:, h * P:(h + 1) * P], a[:, i, :], r[:, i, :], start=True, stop=True)
                            mm.then_inc(*M.groups.mark("lv", L, n, "D" if which == 0 else "DT", t))
                for t in range(NT):
                    pe.wait_ge(*M.free[4 + t].at("lv", L, LEVELS - 1, "DT", t))
                for t in range(NT):
                    pe.wait_ge(*M.free[4 + t].at("kn", L, t))
                    pe.wait_ge(*M.free[6 + t].at("vn", L, t))
                for t in range(NT):
                    o = open_bank(M, t)
                    for h in range(DN_H):
                        i = t * DN_H + h
                        mm = nc.tensor.matmul(o[:, h * P:(h + 1) * P], dn["DT"][:, i, :], dn["vb"][:, i, :], start=True, stop=True)
                    mm.then_inc(*M.groups.mark("u", L, t))
                o = open_bank(M, 2)
                for h in range(DN_H):
                    mm = nc.tensor.matmul(o[:, h * P:(h + 1) * P], dn["kbg"][:, h, :], dn["DT"][:, DN_H + h, :], start=True, stop=True)
                mm.then_inc(*M.groups.mark("wT", L))
                pe.wait_ge(*M.free[0].at("u", L, 0))
                o = open_bank(M, 3)
                for h in range(DN_H):
                    mm = nc.tensor.matmul(o[:, h * P:(h + 1) * P], dn["kdec"][:, h, :], dn["u"][:, h, :], start=True, stop=True)
                mm.then_inc(*M.groups.mark("state", L))
                o = open_bank(M, 4)
                for h in range(DN_H):
                    mm = nc.tensor.matmul(o[:, h * P:(h + 1) * P], dn["qk"][:, h, :], dn["u"][:, h, :], start=True, stop=True)
                mm.then_inc(*M.groups.mark("o0", L))
                pe.wait_ge(*M.free[3].at("state", L))
                pe.wait_ge(*M.free[2].at("wT", L))
                o = open_bank(M, 5)
                for h in range(DN_H):
                    mm = nc.tensor.matmul(o[:, h * P:(h + 1) * P], dn["wT"][:, h, :], dn["state"][:, h, :], start=True, stop=True)
                mm.then_inc(*M.groups.mark("ws", L))
                o = open_bank(M, 6)
                for h in range(DN_H):
                    mm = nc.tensor.matmul(o[:, h * P:(h + 1) * P], dn["cv"][:, h, P:S], dn["state"][:, h, :], start=True, stop=True)
                mm.then_inc(*M.groups.mark("qs", L))
                pe.wait_ge(*M.free[5].at("ws", L))
                o = open_bank(M, 7)
                for h in range(DN_H):
                    mm = nc.tensor.matmul(o[:, h * P:(h + 1) * P], dn["qk"][:, DN_H + h, :], dn["vn"][:, h, :], start=True, stop=True)
                mm.then_inc(*M.groups.mark("o1", L))
                for t in range(NT):
                    pe.wait_ge(*gated.at(L, t))
                    o = open_bank(M, t)
                    for h in range(DN_H):
                        mm = nc.tensor.transpose(o[:, h * P:(h + 1) * P], dn["o"][:, t * DN_H + h, :], ident)
                    mm.then_inc(*M.groups.mark("oT", L, t))

            pe.wait_ge(*consts.at())
            for L in range(2):
                if L == 0:
                    pe.wait_ge(*params.at("xT"))
                else:
                    transposes((L, "in"), X, lambda t: x_ready.at(0, "ple", t))
                    xT_ready((L, "in"))
                linear("qkv", L, 3, "qkv", xT)
                turn_qk(L, 8)
                attention(L, NHEAD, lambda h: h // 4, 0)
                for j in range(8):
                    pe.wait_ge(*M.free[2 + j % 2].at("pv", L, j))
                linear("wo", L, 2, "wo", aT)
                transposes((L, "mix"), X, lambda t: x_ready.at(L, "mix", t))
                xT_ready((L, "mix"))
                if L == 0:
                    dense_ffn(0)
                else:
                    router()
                    with pe.Fori(0, NE) as e:
                        with ev.loop(e):
                            experts(M, "moe", expert_base)
                    pe.wait_ge(*flag_done.at())
                    r = pe.value_load(flag_i[0:1, 0:1], min_val=0, max_val=1)
                    with pe.If(r > 0):
                        with pe.Fori(0, NE) as e:
                            with V.ev.loop(e):
                                experts(V, "ovf", 0)
                        pe.wait_ge(*overflow_done())
                u = unit(M, pe, ("pp", L))
                pe.wait_ge(*params.at("pT", L))
                for nb in range(2):
                    for t in range(NT):
                        o = open_bank(M, 4 + 2 * nb + t)
                        for kc in range(2):
                            mm = nc.tensor.matmul(o[:, :], pT[:, kc, t * P:(t + 1) * P],
                                                  u[:, kc * DM + nb * 512:kc * DM + (nb + 1) * 512],
                                                  start=(kc == 0), stop=(kc == 1))
                        mm.then_inc(*M.groups.mark("pp", L, nb, t))
                released(M, unit_at["pp", L], "pp", L, 1, 1)
                transposes((L, "ffn"), X, lambda t: x_ready.at(L, "ffn", t))
                xT_ready((L, "ffn"))
                linear("pg", L, 2, "pg", xT)
            for L in range(2, 4):
                transposes((L, "in"), R, lambda t: prenorm.at(L, "in", t))
                xT_ready((L, "in"))
                delta(L)
                linear("bqkv", L, 3, "in", xT, first=4)
                turn_qk(L, 4)
                attention(L, 8, lambda h: h // 2, 4)
                for t in range(NT):
                    pe.wait_ge(*M.free[t].at("oT", L, t))
                for j in range(4):
                    pe.wait_ge(*M.free[2 + j % 2].at("pv", L, j))
                linear("wo", L, 2, "wo", aT)
                transposes((L, "mix"), R, lambda t: prenorm.at(L, "mix", t))
                xT_ready((L, "mix"))
                dense_ffn(L)

        @block.scalar
        def _(ac):
            def wait_self(E=M):
                ac.wait_ge(*E.act.last())

            def copy_T(stage, L):
                for t in range(NT):
                    for g in range(2):
                        ac.wait_ge(*M.groups.at("tx", stage, t, g))
                        nc.scalar.copy(xT[:, 4 * g:4 * g + 4, t * P:(t + 1) * P],
                                       bank[2 * t + g][:, :].rearrange("p (c n) -> p c n", n=P)) \
                            .then_inc(*M.free[2 * t + g].mark("xT", stage, t, g))

            def qkv_out(name, L, nq):
                for nb in range(3):
                    for t in range(NT):
                        ac.wait_ge(*M.groups.at(name, L, nb, t))
                        b = (2 * nb + t) % 4
                        nc.scalar.activation(att["qn"][:, t, nb * 512:(nb + 1) * 512], bank[b][:, :], ACT.Copy,
                                             scale=(DH ** -0.5 if nb < nq else 1.0)).then_inc(*M.free[b].mark(name, L, nb, t))

            def copy_qkT(L, nq):
                for t in range(NT):
                    for g in range(nq // 4 + 1):
                        b = (3 * t + g) % 4
                        ac.wait_ge(*M.groups.at("qkT", L, t, g))
                        dst = att["qT"][:, 4 * g:4 * g + 4, t * P:(t + 1) * P] if g < nq // 4 \
                            else att["kT"][:, :, t * P:(t + 1) * P]
                        nc.scalar.copy(dst, bank[b][:, :].rearrange("p (c n) -> p c n", n=P)) \
                            .then_inc(*M.free[b].mark("qkT", L, t, g))

            def attention(L, heads, out0):
                def exps(h):
                    i = h % 2
                    ac.wait_ge(*maxed.at(L, h))
                    if h >= 2:
                        ac.wait_ge(*M.groups.at("pt", L, h - 2))
                    for q, (a, b) in enumerate(((0, P), (P, 3 * P))):
                        ins = nc.scalar.activation(att["pr"][:, i, a:b], att["s"][:, i, a:b], ACT.Exp,
                                                   bias=nmax[:, i, q:q + 1], accum_out=rsum[:, i, q:q + 1])
                    if L == 1:
                        ins = nc.scalar.activation(esink[:, i, :], nmax[:, i, :], ACT.Exp, bias=sinks[:, h:h + 1])
                    ins.then_inc(*exped.mark(L, h))

                def turned(h):
                    ac.wait_ge(*M.groups.at("pt", L, h))
                    if h >= 2:
                        ac.wait_ge(*M.groups.at("pv", L, h - 2))
                    nc.scalar.copy(att["pt"][:, h % 2, :], bank[6 + h % 2][:, 0:384]).then_inc(*M.free[6 + h % 2].mark("pt", L, h))

                def out(j):
                    ac.wait_ge(*M.groups.at("pv", L, 2 * j + 1))
                    nc.scalar.copy(aT[:, out0 + j, :], bank[2 + j % 2][:, 0:S]).then_inc(*M.free[2 + j % 2].mark("pv", L, j))
                for i in range(heads + 2):
                    if i < heads:
                        exps(i)
                    if 0 <= i - 1 < heads:
                        turned(i - 1)
                    if i >= 2 and i % 2 == 1:
                        out((i - 3) // 2)

            def root(L, which, src, scale, eps):
                ac.wait_ge(*stats.at(L, which))
                nc.scalar.activation(sd, src, ACT.Sqrt, bias=eps, scale=scale).then_inc(*rooted.mark(L, which))

            def sum_squares(L, which, src, ready):
                if M.act.n:
                    wait_self()
                for t in range(NT):
                    ac.wait_ge(*ready(t))
                    ins = nc.scalar.activation(junk[:, t, :], src[:, t, :], ACT.Square, accum_out=ss[:, t, 0:1])
                ins.then_inc(*M.act.mark("ss", L, which))
                wait_self()
                nc.scalar.activation(sd, ss[:, :, 0], ACT.Sqrt, bias=C("rms_eps"), scale=1.0 / DM) \
                    .then_inc(*rooted.mark(L, which))

            def dense_act(L):
                n = FFN_STEPS[L]
                for s in range(n):
                    b = 4 + 2 * (s % 2)
                    if L == 0:
                        ac.wait_ge(*M.groups.at("gu", L, s, 0))
                        if s >= 2:
                            ac.wait_ge(*hidden_at(L, s - 2))
                        nc.scalar.activation(ffn["sg"][:, s % 2, :, :].rearrange("p a b -> p (a b)"), bank[b][:, :], ACT.Silu) \
                            .then_inc(*M.free[b].mark("sg", L, s))
                        continue
                    if s >= 2:
                        ac.wait_ge(*hidden_at(L, s - 2))
                    for half, buf in enumerate((ffn["cbg"], ffn["cbv"])):
                        ac.wait_ge(*M.groups.at("gu", L, s, half))
                        for m in range(2):
                            c = half * 22 + 2 * s + m
                            ins = nc.scalar.activation(buf[:, s % 2, m, :], bank[b + half][:, m * S:(m + 1) * S], ACT.Identity,
                                                       bias=fcw[:, c, 3:4], scale=fcw[:, c, 2:3])
                        ins.then_inc(*M.act.mark("tap", L, s, half))
                    if s:
                        gelu(L, s - 1)
                if L:
                    gelu(L, n - 1)

            def gelu(L, s):
                ac.wait_ge(*M.free[4 + 2 * (s % 2)].at("cb", L, s, 0))
                nc.scalar.activation(ffn["gg"][:, s % 2, :, :].rearrange("p a b -> p (a b)"),
                                     ffn["cbg"][:, s % 2, :, :].rearrange("p a b -> p (a b)"), ACT.Gelu_apprx_tanh) \
                    .then_inc(*M.act.mark("gelu", L, s))

            def experts(E, tag):
                for g in range(2):
                    ac.wait_ge(*E.groups.at(tag, "ga", g))
                    nc.scalar.copy(moe["xe"][:, 4 * g:4 * g + 4, :].rearrange("p a b -> p (a b)"), bank[2 + g][:, :]) \
                        .then_inc(*E.free[2 + g].mark(tag, "xe", g))
                ac.wait_ge(*E.groups.at(tag, "tg"))
                nc.scalar.copy(moe["sgT"], bank[2][:, 0:S]).then_inc(*E.free[2].mark(tag, "sgT"))

                def silu(f):
                    b = 4 + 2 * (f % 2)
                    ac.wait_ge(*E.groups.at(tag, "gu", f, 0))
                    if f >= 2:
                        ac.wait_ge(*E.free[b + 1].at(tag, "h", f - 2))
                    nc.scalar.activation(moe["sg"][:, f % 2, :], bank[b][:, :], ACT.Silu).then_inc(*E.free[b].mark(tag, "sg", f))

                def turned(f):
                    ac.wait_ge(*E.groups.at(tag, "tr", f))
                    if f >= 2:
                        ac.wait_ge(*E.groups.at(tag, "dn", f - 2))
                    nc.scalar.copy(moe["hTe"][:, f % 2, :, :].rearrange("p a b -> p (a b)"), bank[2 + f % 2][:, :]) \
                        .then_inc(*E.free[2 + f % 2].mark(tag, "hTe", f))
                silu(0)
                for f in range(EXP_STEPS):
                    if f + 1 < EXP_STEPS:
                        silu(f + 1)
                    turned(f)
                ac.wait_ge(*E.groups.at(tag, "dn", EXP_STEPS - 1))
                nc.scalar.copy(moe["ye"][:, 0:512], bank[0][:, :]).then_inc(*E.free[0].mark(tag, "ye", 0))

            def delta(L):
                ac.wait_ge(*params.at("cw", L))
                for j in range(6):
                    b = 2 * ((j // 2) % 2) + j % 2
                    ac.wait_ge(*M.groups.at("cv", L, j))
                    for m in range(2):
                        ins = nc.scalar.activation(dn["cv"][:, 2 * j + m, :], bank[b][:, m * S:(m + 1) * S], ACT.Identity,
                                                   scale=cw[:, 2 * j + m, 3:4])
                    ins.then_inc(*M.act.mark("tap", L, j))
                for t in range(NT):
                    ac.wait_ge(*M.groups.at("z", L, 0, t))
                    nc.scalar.copy(dn["z"][:, t, :], bank[t][:, :]).then_inc(*M.free[t].mark("z", L, 0, t))
                ac.wait_ge(*M.groups.at("ba", L))
                nc.scalar.copy(ba.rearrange("p a b -> p (a b)"), bank[2][:, 0:16]).then_inc(*M.free[2].mark("ba", L))
                for j in range(6):
                    ac.wait_ge(*M.free[2 * ((j // 2) % 2) + j % 2].at("cv", L, j))
                    v = dn["cv"][:, 2 * j:2 * j + 2, :].rearrange("p a b -> p (a b)")
                    nc.scalar.activation(v, v, ACT.Silu).then_inc(*M.act.mark("silu", L, j))
                for t in range(NT):
                    ac.wait_ge(*M.free[t].at("z", L, 0, t))
                    nc.scalar.activation(dn["z"][:, t, :], dn["z"][:, t, :], ACT.Silu).then_inc(*M.act.mark("zs", L, t))
                ac.wait_ge(*M.free[2].at("ba", L))
                nc.scalar.activation(beta, ba[:, :, 0:DN_H], ACT.Sigmoid).then_inc(*M.act.mark("beta", L))
                ac.wait_ge(*decay.at(L, "y"))
                nc.scalar.activation(sp1, sp1, ACT.Abs).then_inc(*M.act.mark())
                wait_self()
                nc.scalar.activation(sp1, sp1, ACT.Exp, scale=-1.0).then_inc(*M.act.mark())
                wait_self()
                nc.scalar.activation(sp1, sp1, ACT.Ln, bias=1.0).then_inc(*M.act.mark())
                nc.scalar.activation(gl, alog[:, L - 2:L - 1, :].to_broadcast([P, NT, DN_H]), ACT.Exp).then_inc(*M.act.mark("sp", L))
                for g in range(4):
                    if g >= 2:
                        ac.wait_ge(*M.groups.at("ssq", L, g - 2))
                    ac.wait_ge(*M.act.at("silu", L, g))
                    nc.scalar.activation(dn["sq"][:, 4 * (g % 2):4 * (g % 2) + 4, :].rearrange("p a b -> p (a b)"),
                                         dn["cv"][:, 2 * g:2 * g + 2, :].rearrange("p a b -> p (a b)"), ACT.Square) \
                        .then_inc(*squares.mark(L, g))
                for g in range(4):
                    ac.wait_ge(*M.groups.at("ssq", L, g))
                    ac.wait_ge(*M.groups.at("ssq", L, 3))
                    if g >= 2:
                        ac.wait_ge(*normed.at(L, g - 2))
                    nc.scalar.activation(dn["sq"][:, 4 * (g % 2):4 * (g % 2) + 4, :].rearrange("p a b -> p (a b)"),
                                         bank[4 + g][:, :], ACT.Sqrt, bias=C("rms_eps")) \
                        .then_inc(*M.free[4 + g].mark("len", L, g))
                ac.wait_ge(*M.groups.at("gcol", L))
                nc.scalar.activation(ngc.rearrange("p a b -> p (a b)"), bank[6][:, 0:N_DN], ACT.Copy, scale=-1.0) \
                    .then_inc(*M.free[6].mark("gcol", L))
                ac.wait_ge(*M.free[6].at("gcol", L))
                nc.scalar.activation(expg, ngc, ACT.Exp, scale=-1.0).then_inc(*M.act.mark("expg", L))
                ac.wait_ge(*decay.at(L, "last"))
                nc.scalar.activation(kdsc, kdsc, ACT.Exp).then_inc(*M.act.mark("kdsc", L))
                for t in range(NT):
                    ac.wait_ge(*M.free[t].at("grow", L, t))
                    for h in range(DN_H):
                        ins = nc.scalar.activation(dn["gam"][:, t * DN_H + h, :], dn["gam"][:, t * DN_H + h, :], ACT.Exp,
                                                   bias=ngc[:, t, h:h + 1])
                    ins.then_inc(*M.act.mark("gam", L, t))
                ac.wait_ge(*M.groups.at("u", L, 0))
                nc.scalar.copy(dn["u"][:, 0:DN_H, :].rearrange("p a b -> p (a b)"), bank[0][:, :]).then_inc(*M.free[0].mark("u", L, 0))
                ac.wait_ge(*M.groups.at("u", L, 1))
                nc.scalar.copy(dn["u"][:, DN_H:, :].rearrange("p a b -> p (a b)"), bank[1][:, :]).then_inc(*M.free[1].mark("u", L, 1))
                ac.wait_ge(*M.groups.at("wT", L))
                nc.scalar.copy(dn["wT"].rearrange("p a b -> p (a b)"), bank[2][:, :]).then_inc(*M.free[2].mark("wT", L))
                ac.wait_ge(*M.groups.at("state", L))
                nc.scalar.copy(dn["state"].rearrange("p a b -> p (a b)"), bank[3][:, :]).then_inc(*M.free[3].mark("state", L))
                for t in range(NT):
                    ac.wait_ge(*(M.free[4].at("o0", L) if t == 0 else M.free[7].at("o1", L)))
                    for h in range(DN_H):
                        ins = nc.scalar.activation(junk[:, t, h * P:(h + 1) * P], dn["o"][:, t * DN_H + h, :], ACT.Square, accum_out=ss[:, t, h:h + 1])
                ins.then_inc(*M.act.mark("oss", L))
                wait_self()
                nc.scalar.activation(rn8, ss, ACT.Sqrt, bias=C("rms_eps"), scale=1.0 / P).then_inc(*M.act.mark("ort", L))
                for t in range(NT):
                    ac.wait_ge(*M.groups.at("oT", L, t))
                    nc.scalar.copy(aT[:, 0:4, t * P:(t + 1) * P], bank[t][:, :].rearrange("p (c n) -> p c n", n=P)) \
                        .then_inc(*M.free[t].mark("oT", L, t))

            M.ev.seen = V.ev.seen = 0
            ac.wait_ge(*consts.at())
            ac.wait_ge(*angles.at("sin"))
            nc.scalar.activation(sin1, red, ACT.Sin).then_inc(*angles_done.mark("sin"))
            ac.wait_ge(*angles.at("cos"))
            nc.scalar.activation(cos1, ang, ACT.Sin).then_inc(*angles_done.mark("cos"))
            ac.wait_ge(*params.at("sinks"))
            for L in range(2):
                if L:
                    copy_T((L, "in"), L)
                qkv_out("qkv", L, 2)
                copy_qkT(L, 8)
                attention(L, NHEAD, 0)
                root(L, "mix", mv[:, :, 1], 1.0, C("ln_eps"))
                copy_T((L, "mix"), L)
                if L == 0:
                    dense_act(0)
                else:
                    ac.wait_ge(*decided.at("m"))
                    nc.scalar.activation(w2, w2, ACT.Exp).then_inc(*M.act.mark("w2"))
                    with ac.Fori(0, NE) as e:
                        with ev.loop(e):
                            experts(M, "moe")
                    ac.wait_ge(*flag_done.at())
                    r = ac.value_load(flag_i[0:1, 0:1], min_val=0, max_val=1)
                    with ac.If(r > 0):
                        with ac.Fori(0, NE) as e:
                            with V.ev.loop(e):
                                experts(V, "ovf")
                        ac.wait_ge(*overflow_done())
                root(L, "ffn", mv[:, :, 1], 1.0, C("ln_eps"))
                copy_T((L, "ffn"), L)
                for nb in range(2):
                    for t in range(NT):
                        b = (2 * nb + t) % 4
                        ac.wait_ge(*M.groups.at("pg", L, nb, t))
                        nc.scalar.activation(att["sg"][:, 2 * nb + t, :], bank[b][:, :], ACT.Sigmoid).then_inc(*M.free[b].mark("pg", L, nb, t))
            for L in range(2, 4):
                sum_squares(L, "in", X, lambda t: x_ready.at(*((1, "ple", t) if L == 2 else (2, "ffn", t))))
                delta(L)
                qkv_out("bqkv", L, 1)
                copy_qkT(L, 4)
                attention(L, 8, 4)
                for nb in range(2):
                    for t in range(NT):
                        b = (2 * nb + t) % 4
                        ac.wait_ge(*M.groups.at("wo", L, nb, t))
                        nc.scalar.copy(R[:, t, nb * 512:(nb + 1) * 512], bank[b][:, :]).then_inc(*M.free[b].mark("wo", L, nb, t))
                sum_squares(L, "mix", R, lambda t: M.free[(2 + t) % 4].at("wo", L, 1, t))
                sum_squares(L, "pre", X, lambda t: x_ready.at(L, "mix", t))
                dense_act(L)
                for t in range(NT):
                    for nb in range(2):
                        b = 2 * t + nb
                        ac.wait_ge(*M.groups.at("down", L, FFN_STEPS[L] - 1))
                        nc.scalar.copy(R[:, t, nb * 512:(nb + 1) * 512], bank[b][:, :]).then_inc(*M.free[b].mark("y", L, t, nb))
                sum_squares(L, "ffn", R, lambda t: M.free[2 * t + 1].at("y", L, t, 1))

        @block.vector
        def _(ve):
            V_ = nc.vector

            def sync(E=M):
                ve.wait_ge(*E.dve.last())

            def step(ins, E=M, *key):
                ins.then_inc(*E.dve.mark(*key))

            def chain(ins, E=M, *key):
                step(ins, E, *key)
                sync(E)

            def vec_row(v):
                s = v % VSLOTS
                ve.wait_ge(vecs[s].sem, 16 * (v // VSLOTS + 1))
                return vec[:, s, :]

            def rope(L, heads, cos, sin):
                for t in range(NT):
                    for nb in range(3):
                        ve.wait_ge(*M.free[(2 * nb + t) % 4].at("qkv" if L < 2 else "bqkv", L, nb, t))
                    q = att["qn"][:, t, 0:heads * DH].rearrange("p (h d) -> p h d", d=DH)
                    x1, x2 = q[:, :, 0:8], q[:, :, 8:16]
                    c = cos[:, t, :].unsqueeze(1).to_broadcast([P, heads, 8])
                    s = sin[:, t, :].unsqueeze(1).to_broadcast([P, heads, 8])
                    tm = [att["tmp"][:, i, 0:heads, :] for i in range(4)]
                    step(V_.tensor_tensor(tm[0], x1, c, ALU.mult))
                    step(V_.tensor_tensor(tm[1], x2, s, ALU.mult))
                    step(V_.tensor_tensor(tm[2], x2, c, ALU.mult))
                    chain(V_.tensor_tensor(tm[3], x1, s, ALU.mult))
                    step(V_.tensor_tensor(x1, tm[0], tm[1], ALU.subtract))
                    last = V_.tensor_tensor(x2, tm[2], tm[3], ALU.add)
                    if L < 2:
                        chain(last)
                        k = att["qn"][:, t, 1024:1280].rearrange("p (h d) -> p h d", d=DH)
                        V_.tensor_copy(att["kd"][:, t, :, 0, :], k)
                        last = V_.tensor_copy(att["kd"][:, t, :, 1, :], k)
                    last.then_inc(*roped.mark(L, t))
                    ve.wait_ge(*roped.at(L, t))

            def attention(L, heads, mask):
                def scores(h):
                    i, b = h % 2, 4 + h % 2
                    ve.wait_ge(*M.groups.at("sc", L, h))
                    if h >= 2:
                        ve.wait_ge(*exped.at(L, h - 2))
                    V_.tensor_tensor(att["s"][:, i, :], bank[b][:, 0:384], C(mask), ALU.add).then_inc(*M.free[b].mark("sc", L, h))
                    ve.wait_ge(*M.free[b].at("sc", L, h))
                    for q, (a, c) in enumerate(((0, P), (P, 3 * P))):
                        ins = V_.tensor_reduce(nmax[:, i, q:q + 1], att["s"][:, i, a:c], AXX, ALU.max, negate=True)
                    if L == 1:
                        chain(ins)
                        ins = V_.tensor_scalar(nmax[:, i, :], nmax[:, i, :], nsink[:, h:h + 1], None, ALU.min)
                    ins.then_inc(*maxed.mark(L, h))

                def normalise(h):
                    i = h % 2
                    ve.wait_ge(*exped.at(L, h))
                    if L == 1:
                        chain(V_.tensor_tensor(rsum[:, i, :], rsum[:, i, :], esink[:, i, :], ALU.add))
                    chain(V_.reciprocal(rden[:, i, :], rsum[:, i, :]))
                    for q, (a, c) in enumerate(((0, P), (P, 3 * P))):
                        ins = V_.tensor_scalar(att["pr"][:, i, a:c], att["pr"][:, i, a:c], rden[:, i, q:q + 1], None, ALU.mult)
                    ins.then_inc(*probs.mark(L, h))
                for i in range(heads + 1):
                    if i < heads:
                        scores(i)
                    if i >= 1:
                        normalise(i - 1)

            def layer_norm(L, which, v, take):
                for t in range(NT):
                    take(t)
                sync()
                for t in range(NT):
                    for i in range(2):
                        step(V_.bn_stats(st6[:, t, i, :], R[:, t, i * 512:(i + 1) * 512]))
                sync()
                for t in range(NT):
                    ins = V_.bn_aggr(mv[:, t, :], st6[:, t, :, :].rearrange("p a b -> p (a b)"))
                    if t == 0:
                        step(ins)
                ins.then_inc(*stats.mark(L, which))
                ve.wait_ge(*rooted.at(L, which))
                chain(V_.reciprocal(rstd, sd))
                g, b = vec_row(v), vec_row(v + 1)
                for t in range(NT):
                    step(V_.tensor_scalar(R[:, t, :], R[:, t, :], mv[:, t, 0:1], rstd[:, t:t + 1], ALU.subtract, ALU.mult))
                sync()
                for t in range(NT):
                    ins = V_.tensor_tensor(R[:, t, :], R[:, t, :], g, ALU.mult)
                    if t == 0:
                        step(ins)
                ins.then_inc(*vec_used.mark(v))
                ve.wait_ge(*vec_used.at(v))
                sync()
                for t in range(NT):
                    V_.tensor_tensor(X[:, t, :], R[:, t, :], b, ALU.add).then_inc(*x_ready.mark(L, which, t))

            def post_norm(L, which, v):
                ve.wait_ge(*rooted.at(L, which))
                chain(V_.reciprocal(rstd, sd))
                w = vec_row(v)
                for t in range(NT):
                    ins = V_.scalar_tensor_tensor(R[:, t, :], R[:, t, :], rstd[:, t:t + 1], w, ALU.mult, ALU.mult)
                    if t == 0:
                        step(ins)
                ins.then_inc(*vec_used.mark(v))
                ve.wait_ge(*vec_used.at(v))
                sync()
                for t in range(NT):
                    V_.tensor_tensor(X[:, t, :], X[:, t, :], R[:, t, :], ALU.add).then_inc(*x_ready.mark(L, which, t))

            def pre_norm(L, which, rt):
                ve.wait_ge(*rooted.at(L, rt))
                ve.wait_ge(*x_ready.at(*((L, "mix", 1) if which == "mix" else (1, "ple", 1) if L == 2 else (2, "ffn", 1))))
                chain(V_.reciprocal(rstd, sd))
                for t in range(NT):
                    V_.tensor_scalar(R[:, t, :], X[:, t, :], rstd[:, t:t + 1], None, ALU.mult).then_inc(*prenorm.mark(L, which, t))
                w = prew[:, 0 if which == "in" else 1, :]
                ve.wait_ge(*params.at("prew", L))
                for t in range(NT):
                    for g in range(2):
                        ve.wait_ge(*M.groups.at("tx", (L, which), t, g))
                        V_.tensor_tensor(xT[:, 4 * g:4 * g + 4, t * P:(t + 1) * P],
                                         bank[2 * t + g][:, :].rearrange("p (c n) -> p c n", n=P),
                                         w[:, 4 * g:4 * g + 4].unsqueeze(2).to_broadcast([P, 4, P]), ALU.mult) \
                            .then_inc(*M.free[2 * t + g].mark("xT", (L, which), t, g))

            def dense_dve(L):
                n = FFN_STEPS[L]
                for s in range(n):
                    b = 4 + 2 * (s % 2)
                    if L == 0:
                        ve.wait_ge(*M.free[b].at("sg", L, s))
                        ve.wait_ge(*M.groups.at("gu", L, s, 1))
                        if s >= 2:
                            ve.wait_ge(*M.groups.at("down", L, s - 2))
                        V_.tensor_tensor(ffn["hT"][:, s % 2, :, :].rearrange("p a b -> p (a b)"),
                                         ffn["sg"][:, s % 2, :, :].rearrange("p a b -> p (a b)"), bank[b + 1][:, :], ALU.mult) \
                            .then_inc(*M.free[b + 1].mark("h", L, s))
                        continue
                    for half, buf in enumerate((ffn["cbg"], ffn["cbv"])):
                        ve.wait_ge(*M.groups.at("gu", L, s, half))
                        ve.wait_ge(*M.act.at("tap", L, s, half))
                        o = bank[b + half]
                        for m in range(2):
                            c = half * 22 + 2 * s + m
                            step(V_.scalar_tensor_tensor(buf[:, s % 2, m, 1:S], o[:, m * S:m * S + S - 1], fcw[:, c, 1:2],
                                                         buf[:, s % 2, m, 1:S], ALU.mult, ALU.add))
                        sync()
                        for m in range(2):
                            c = half * 22 + 2 * s + m
                            ins = V_.scalar_tensor_tensor(buf[:, s % 2, m, 2:S], o[:, m * S:m * S + S - 2], fcw[:, c, 0:1],
                                                          buf[:, s % 2, m, 2:S], ALU.mult, ALU.add)
                        ins.then_inc(*M.free[b + half].mark("cb", L, s, half))
                    if s:
                        gated_mul(L, s - 1)
                if L:
                    gated_mul(L, n - 1)

            def gated_mul(L, s):
                ve.wait_ge(*M.act.at("gelu", L, s))
                ve.wait_ge(*M.free[5 + 2 * (s % 2)].at("cb", L, s, 1))
                if s >= 2:
                    ve.wait_ge(*M.groups.at("down", L, s - 2))
                V_.tensor_tensor(ffn["hT"][:, s % 2, :, :], ffn["gg"][:, s % 2, :, :], ffn["cbv"][:, s % 2, :, :], ALU.mult) \
                    .then_inc(*hidden.mark(L, s))

            def route():
                for t in range(NT):
                    ve.wait_ge(*M.groups.at("router", t))
                    V_.tensor_copy(lg[:, t, :], bank[t][:, 0:NE]).then_inc(*M.free[t].mark("router", t))
                    ve.wait_ge(*M.free[t].at("router", t))
                rank = C("rank").unsqueeze(1).to_broadcast([P, NT, NE])

                def pick(src, top, hot):
                    chain(V_.tensor_reduce(top, src, AXX, ALU.max))
                    chain(V_.tensor_tensor(sc8, src, top.unsqueeze(2).to_broadcast([P, NT, NE]), ALU.is_equal))
                    chain(V_.tensor_tensor(sc8, sc8, rank, ALU.mult))
                    chain(V_.tensor_reduce(w1, sc8, AXX, ALU.max))
                    chain(V_.tensor_tensor(hot, sc8, w1.unsqueeze(2).to_broadcast([P, NT, NE]), ALU.is_equal))
                pick(lg, m1, oh1)
                chain(V_.scalar_tensor_tensor(lg2.rearrange("p a b -> p (a b)"), oh1.rearrange("p a b -> p (a b)"), -3.0e38,
                                              lg.rearrange("p a b -> p (a b)"), ALU.mult, ALU.add))
                pick(lg2, m2, oh2)
                V_.tensor_tensor(memb, oh1, oh2, ALU.add).then_inc(*member.mark())
                V_.tensor_tensor(w2, m2, m1, ALU.subtract).then_inc(*decided.mark("m"))
                ve.wait_ge(*M.act.at("w2"))
                chain(V_.tensor_scalar(w1, w2, 1.0, None, ALU.add))
                chain(V_.reciprocal(w1, w1))
                chain(V_.tensor_tensor(w2, w2, w1, ALU.mult))
                chain(V_.tensor_tensor(gates, oh1, w1.unsqueeze(2).to_broadcast([P, NT, NE]), ALU.mult))
                chain(V_.tensor_tensor(sc8, oh2, w2.unsqueeze(2).to_broadcast([P, NT, NE]), ALU.mult))
                chain(V_.tensor_tensor(gates, gates, sc8, ALU.add))
                ve.wait_ge(*M.groups.at("ranks"))
                r = bank[2][:, 0:2 * NE].rearrange("p (a b) -> p a b", b=NE)
                chain(V_.scalar_tensor_tensor(posx.rearrange("p a b -> p (a b)"), r.rearrange("p a b -> p (a b)"), 1.0,
                                              memb.rearrange("p a b -> p (a b)"), ALU.add, ALU.mult))
                chain(V_.tensor_scalar(posx, posx, -1.0, None, ALU.add))
                V_.tensor_reduce(flag_f, bank[2][:, 2 * NE:3 * NE], AXX, ALU.max).then_inc(*M.free[2].mark("ranks"))
                ve.wait_ge(*M.free[2].at("ranks"))
                chain(V_.tensor_scalar(flag_f, flag_f, float(P) + 0.5, None, ALU.is_gt))
                V_.tensor_copy(flag_i[:, :], flag_f).then_inc(*flag_done.mark())
                ve.wait_ge(*flag_done.at())
                for t in range(NT):
                    step(V_.tensor_scalar(R[:, t, :], X[:, t, :], ALPHA, None, ALU.mult))
                sync()

            def experts(E, tag, e, tile):
                step(V_.tensor_copy(pcol, posx[:, :, e]), E)
                chain(V_.tensor_copy(gcol, gates[:, :, e]), E)
                for t in range(NT):
                    io = C("iota", tile * P, (tile + 1) * P)
                    step(V_.tensor_scalar(moe["sel"][:, t, :], io, pcol[:, t:t + 1], None, ALU.is_equal), E)
                    step(V_.tensor_scalar(moe["selg"][:, t, :], io, pcol[:, t:t + 1], gcol[:, t:t + 1], ALU.is_equal, ALU.mult),
                         E, tag, "sel")
                for f in range(EXP_STEPS):
                    b = 4 + 2 * (f % 2)
                    ve.wait_ge(*E.free[b].at(tag, "sg", f))
                    ve.wait_ge(*E.groups.at(tag, "gu", f, 1))
                    if f >= 2:
                        ve.wait_ge(*E.groups.at(tag, "tr", f - 2))
                    V_.tensor_tensor(moe["h"][:, f % 2, :], moe["sg"][:, f % 2, :], bank[b + 1][:, :], ALU.mult) \
                        .then_inc(*E.free[b + 1].mark(tag, "h", f))
                ve.wait_ge(*E.groups.at(tag, "dn", EXP_STEPS - 1))
                V_.tensor_copy(moe["ye"][:, 512:1024], bank[1][:, :]).then_inc(*E.free[1].mark(tag, "ye", 1))
                for t in range(NT):
                    for nb in range(2):
                        ve.wait_ge(*E.groups.at(tag, "sc", t, nb))
                        r = R[:, t, nb * 512:(nb + 1) * 512]
                        V_.tensor_tensor(r, r, bank[2 + nb][:, :], ALU.add).then_inc(*E.free[2 + nb].mark(tag, "sc", t, nb))
                for nb in range(2):
                    ve.wait_ge(*E.free[2 + nb].at(tag, "sc", 1, nb))

            def delta(L):
                for j in range(6):
                    b = 2 * ((j // 2) % 2) + j % 2
                    ve.wait_ge(*M.groups.at("cv", L, j))
                    ve.wait_ge(*M.act.at("tap", L, j))
                    for tap in (2, 1, 0):
                        d = 3 - tap
                        for m in range(2):
                            c = 2 * j + m
                            ins = V_.scalar_tensor_tensor(dn["cv"][:, c, d:S], bank[b][:, m * S:m * S + S - d], cw[:, c, tap:tap + 1],
                                                          dn["cv"][:, c, d:S], ALU.mult, ALU.add)
                            if tap or not m:
                                step(ins)
                        if tap:
                            sync()
                    ins.then_inc(*M.free[b].mark("cv", L, j))
                ve.wait_ge(*M.free[2].at("ba", L))
                chain(V_.tensor_tensor(sp1, ba[:, :, DN_H:8], dtb[:, L - 2:L - 1, :].to_broadcast([P, NT, DN_H]), ALU.add))
                V_.tensor_scalar(sp2, sp1, 0.0, None, ALU.max).then_inc(*decay.mark(L, "y"))
                ve.wait_ge(*M.act.at("sp", L))
                ve.wait_ge(*decay.at(L, "y"))
                chain(V_.tensor_tensor(sp2, sp2, sp1, ALU.add))
                V_.scalar_tensor_tensor(gl.rearrange("p a b -> p (a b)"), sp2.rearrange("p a b -> p (a b)"), -1.0,
                                        gl.rearrange("p a b -> p (a b)"), ALU.mult, ALU.mult).then_inc(*decay.mark(L, "g"))
                ve.wait_ge(*decay.at(L, "g"))
                ve.wait_ge(*M.act.at("beta", L))
                step(V_.tensor_copy(dn["gB"], gl.rearrange("p a b -> p (a b)").unsqueeze(2).to_broadcast([P, N_DN, P])))
                V_.tensor_copy(dn["bB"], beta.rearrange("p a b -> p (a b)").unsqueeze(2).to_broadcast([P, N_DN, P])) \
                    .then_inc(*decay.mark(L, "rows"))
                for g in range(4):
                    ve.wait_ge(*M.free[4 + g].at("len", L, g))
                    v = dn["cv"][:, 2 * g:2 * g + 2, :].rearrange("p a b -> p (a b)")
                    ln = dn["sq"][:, 4 * (g % 2):4 * (g % 2) + 4, :].rearrange("p a b -> p (a b)")
                    chain(V_.reciprocal(ln, ln))
                    V_.scalar_tensor_tensor(v, v, (float(P) ** -0.5 if g < 2 else 1.0), ln, ALU.mult, ALU.mult) \
                        .then_inc(*normed.mark(L, g))
                ve.wait_ge(*normed.at(L, 3))
                ve.wait_ge(*M.free[6].at("gcol", L))
                for t in range(NT):
                    ve.wait_ge(*M.groups.at("grow", L, t))
                    gr = bank[t][:, :].rearrange("p (h n) -> p h n", n=P)
                    if t == 0:
                        V_.tensor_tensor(kdsc, gr[:, :, P - 1], ngc[:, 0, :], ALU.add).then_inc(*decay.mark(L, "last"))
                    V_.tensor_tensor(dn["gam"][:, t * DN_H:(t + 1) * DN_H, :], gr,
                                     C("mask_gamma").unsqueeze(1).to_broadcast([P, DN_H, P]), ALU.add) \
                        .then_inc(*M.free[t].mark("grow", L, t))
                for t in range(NT):
                    ve.wait_ge(*M.groups.at("brow", L, t))
                    V_.tensor_tensor(dn["kb"][:, :, t * P:(t + 1) * P], dn["cv"][:, DN_H:2 * DN_H, t * P:(t + 1) * P],
                                     bank[2 + t][:, :].rearrange("p (h n) -> p h n", n=P), ALU.mult) \
                        .then_inc(*M.free[2 + t].mark("brow", L, t))
                ve.wait_ge(*M.act.at("kdsc", L))
                chain(V_.tensor_tensor(bexp, beta[:, 1, :], expg[:, 1, :], ALU.mult))
                for t in range(NT):
                    ve.wait_ge(*M.groups.at("kn", L, t))
                    for h in range(DN_H):
                        dst, sc = (dn["kdec"], kdsc) if t == 0 else (dn["kbg"], bexp)
                        ins = V_.tensor_scalar(dst[:, h, :], bank[4 + t][:, h * P:(h + 1) * P], sc[:, h:h + 1], None, ALU.mult)
                    ins.then_inc(*M.free[4 + t].mark("kn", L, t))
                for t in range(NT):
                    ve.wait_ge(*M.groups.at("vn", L, t))
                    for h in range(DN_H):
                        ins = V_.tensor_scalar(dn["vb"][:, t * DN_H + h, :], bank[6 + t][:, h * P:(h + 1) * P],
                                               beta[:, t, h:h + 1], None, ALU.mult)
                    ins.then_inc(*M.free[6 + t].mark("vn", L, t))
                for name, b0, dst in (("kk", 0, dn["AT"]), ("kq", 2, dn["qk"])):
                    for t in range(NT):
                        ve.wait_ge(*M.groups.at(name, L, t))
                        ve.wait_ge(*M.act.at("gam", L, t))
                        V_.tensor_tensor(dst[:, t * DN_H:(t + 1) * DN_H, :], bank[b0 + t][:, :].rearrange("p (h n) -> p h n", n=P),
                                         dn["gam"][:, t * DN_H:(t + 1) * DN_H, :], ALU.mult).then_inc(*M.free[b0 + t].mark(name, L, t))
                ve.wait_ge(*M.free[1].at("kk", L, 1))
                for n in range(LEVELS):
                    half = [slice(t * DN_H, (t + 1) * DN_H) for t in range(NT)]
                    for t in range(NT):
                        V_.tensor_tensor(dn["LT"][:, half[t], :], dn["AT"][:, half[t], :],
                                         C(f"level{n}").unsqueeze(1).to_broadcast([P, DN_H, P]), ALU.mult).then_inc(*inverse.mark(L, n, "LT", t))
                        ve.wait_ge(*inverse.at(L, n, "LT", t))
                    for t in range(NT):
                        ve.wait_ge(*M.groups.at("lv", L, n, "X", t))
                        px = bank[t][:, :].rearrange("p (h n) -> p h n", n=P)
                        idb = ident.unsqueeze(1).to_broadcast([P, DN_H, P])
                        if n == 0:
                            step(V_.tensor_tensor(dn["DT"][:, half[t], :], idb, dn["LT"][:, half[t], :], ALU.subtract))
                            V_.tensor_tensor(dn["D"][:, half[t], :], idb, px, ALU.subtract).then_inc(*M.free[t].mark("lv", L, n, "X", t))
                            ve.wait_ge(*M.free[t].at("lv", L, n, "X", t))
                            sync()
                        else:
                            V_.tensor_copy(dn["Xl"][:, half[t], :], px).then_inc(*M.free[t].mark("lv", L, n, "X", t))
                    if n == 0:
                        continue
                    for t in range(NT):
                        for which, b, dst in (("D", 2 + t, dn["D"]), ("DT", 4 + t, dn["DT"])):
                            if which == "D" and n == LEVELS - 1:
                                continue
                            ve.wait_ge(*M.groups.at("lv", L, n, "DT", t))
                            V_.tensor_tensor(dst[:, half[t], :], dst[:, half[t], :], bank[b][:, :].rearrange("p (h n) -> p h n", n=P),
                                             ALU.subtract).then_inc(*M.free[b].mark("lv", L, n, which, t))
                            ve.wait_ge(*M.free[b].at("lv", L, n, which, t))
                ve.wait_ge(*M.groups.at("o0", L))
                V_.tensor_copy(dn["o"][:, 0:DN_H, :].rearrange("p a b -> p (a b)"), bank[4][:, :]).then_inc(*M.free[4].mark("o0", L))
                ve.wait_ge(*M.groups.at("ws", L))
                ve.wait_ge(*M.free[1].at("u", L, 1))
                V_.tensor_tensor(dn["vn"].rearrange("p a b -> p (a b)"), dn["u"][:, DN_H:, :].rearrange("p a b -> p (a b)"),
                                 bank[5][:, :], ALU.subtract).then_inc(*M.free[5].mark("ws", L))
                ve.wait_ge(*M.groups.at("qs", L))
                for h in range(DN_H):
                    ins = V_.tensor_scalar(dn["o"][:, DN_H + h, :], bank[6][:, h * P:(h + 1) * P], expg[:, 1, h:h + 1], None, ALU.mult)
                ins.then_inc(*M.free[6].mark("qs", L))
                ve.wait_ge(*M.free[6].at("qs", L))
                ve.wait_ge(*M.groups.at("o1", L))
                o1 = dn["o"][:, DN_H:, :].rearrange("p a b -> p (a b)")
                V_.tensor_tensor(o1, o1, bank[7][:, :], ALU.add).then_inc(*M.free[7].mark("o1", L))
                ve.wait_ge(*M.act.at("ort", L))
                chain(V_.reciprocal(rn8, rn8))
                ve.wait_ge(*params.at("onorm", L))
                for t in range(NT):
                    for h in range(DN_H):
                        o = dn["o"][:, t * DN_H + h, :]
                        step(V_.scalar_tensor_tensor(o, o, rn8[:, t, h:h + 1], onorm[:, :], ALU.mult, ALU.mult))
                sync()
                for t in range(NT):
                    ve.wait_ge(*M.act.at("zs", L, t))
                    o = dn["o"][:, t * DN_H:(t + 1) * DN_H, :].rearrange("p a b -> p (a b)")
                    V_.tensor_tensor(o, o, dn["z"][:, t, :], ALU.mult).then_inc(*gated.mark(L, t))

            M.ev.seen = V.ev.seen = 0
            ve.wait_ge(*consts.at())
            ve.wait_ge(*params.at("pos"))
            chain(V_.tensor_copy(pos_f, pos_i[:, :]))
            for t in range(NT):
                step(V_.tensor_scalar(ang[:, t, :], C("inv"), pos_f[:, t:t + 1], None, ALU.mult))
            sync()
            chain(V_.tensor_scalar(rnd, ang, float(1.0 / (2 * np.pi)), MAGIC, ALU.mult, ALU.add))
            chain(V_.tensor_scalar(rnd, rnd, -MAGIC, None, ALU.add))
            c1 = 6.28125
            c2 = float(np.float32(np.round((2 * np.pi - c1) * 2 ** 20) / 2 ** 20))
            c3 = float(2 * np.pi - c1 - c2)

            def flat(a):
                return a.rearrange("p a b -> p (a b)")
            for c in (c1, c2, c3):
                chain(V_.scalar_tensor_tensor(flat(ang), flat(rnd), -c, flat(ang), ALU.mult, ALU.add))
            PI = 3.1415925
            V_.tensor_scalar(red, ang, PI, -PI, ALU.min, ALU.max).then_inc(*angles.mark("sin"))
            chain(V_.tensor_scalar(ang, ang, float(np.pi / 2), None, ALU.add))
            chain(V_.tensor_scalar(rnd, ang, float(np.pi), float(2 * np.pi), ALU.is_gt, ALU.mult))
            chain(V_.tensor_tensor(ang, ang, rnd, ALU.subtract))
            V_.tensor_scalar(ang, ang, PI, -PI, ALU.min, ALU.max).then_inc(*angles.mark("cos"))
            ve.wait_ge(*params.at("sinks"))
            chain(V_.tensor_scalar(nsink, sinks, -1.0, None, ALU.mult))
            ve.wait_ge(*angles_done.at("cos"))
            for L in range(2):
                rope(L, 20, cos1, sin1)
                attention(L, NHEAD, "mask_causal" if L == 0 else "mask_window")

                def take_wo(t):
                    if L == 0:
                        ve.wait_ge(*params.at("X"))
                    for nb in range(2):
                        b = (2 * nb + t) % 4
                        ve.wait_ge(*M.groups.at("wo", L, nb, t))
                        V_.scalar_tensor_tensor(R[:, t, nb * 512:(nb + 1) * 512], X[:, t, nb * 512:(nb + 1) * 512], ALPHA,
                                                bank[b][:, :], ALU.mult, ALU.add).then_inc(*M.free[b].mark("wo", L, nb, t))
                        ve.wait_ge(*M.free[b].at("wo", L, nb, t))
                layer_norm(L, "mix", 4 * L, take_wo)

                def take_y(t):
                    for nb in range(2):
                        b = 2 * t + nb
                        ve.wait_ge(*M.groups.at("down", 0, FFN_STEPS[0] - 1))
                        V_.scalar_tensor_tensor(R[:, t, nb * 512:(nb + 1) * 512], X[:, t, nb * 512:(nb + 1) * 512], ALPHA,
                                                bank[b][:, :], ALU.mult, ALU.add).then_inc(*M.free[b].mark("y", L, t, nb))
                        ve.wait_ge(*M.free[b].at("y", L, t, nb))
                if L == 0:
                    dense_dve(0)
                    layer_norm(L, "ffn", 4 * L + 2, take_y)
                else:
                    route()
                    with ve.Fori(0, NE) as e:
                        with ev.loop(e):
                            experts(M, "moe", e, 0)
                    r = ve.value_load(flag_i[0:1, 0:1], min_val=0, max_val=1)
                    with ve.If(r > 0):
                        for n, event in enumerate(V.free + [V.groups]):
                            V_.memset(tick[:, n:n + 1], 0.0).then_inc(event.sem, 1)
                        with ve.Fori(0, NE) as e:
                            with V.ev.loop(e):
                                experts(V, "ovf", e, 1)
                    layer_norm(L, "ffn", 4 * L + 2, lambda t: None)
                for nb in range(2):
                    for t in range(NT):
                        b = (2 * nb + t) % 4
                        ve.wait_ge(*M.free[b].at("pg", L, nb, t))
                        ve.wait_ge(*M.groups.at("pp", L, nb, t))
                        V_.tensor_tensor(att["sg"][:, 2 * nb + t, :], att["sg"][:, 2 * nb + t, :], bank[4 + 2 * nb + t][:, :], ALU.mult) \
                            .then_inc(*M.free[4 + 2 * nb + t].mark("pp", L, nb, t))
                        ve.wait_ge(*M.free[4 + 2 * nb + t].at("pp", L, nb, t))
                for t in range(NT):
                    for nb in range(2):
                        x = X[:, t, nb * 512:(nb + 1) * 512]
                        ins = V_.tensor_tensor(x, x, att["sg"][:, 2 * nb + t, :], ALU.add)
                        if nb == 0:
                            step(ins)
                    ins.then_inc(*x_ready.mark(L, "ple", t))
            for L in range(2, 4):
                pre_norm(L, "in", "in")
                delta(L)
                rope(L, 16, C("cos2").rearrange("p (a b) -> p a b", b=8), C("sin2").rearrange("p (a b) -> p a b", b=8))
                attention(L, 8, "mask_dilated")
                post_norm(L, "mix", 4 + 2 * L)
                pre_norm(L, "mix", "pre")
                dense_dve(L)
                post_norm(L, "ffn", 5 + 2 * L)


_OUT = (S, DM)


def layout(a):
    def np32(name):
        return np.asarray(a[name])

    def natural(w):
        lead, n = w.shape[:-2], w.shape[-1] // 512
        w = w.reshape(lead + (2, 4, P, n, 512))
        k = len(lead)
        w = w.transpose(tuple(range(k)) + (k + 3, k, k + 2, k + 1, k + 4))
        return np.ascontiguousarray(w).reshape(lead + (2 * n, P, UNIT))

    def paired(g, u):
        lead, n = g.shape[:-2], g.shape[-1] // 256
        k = len(lead)
        both = np.stack([w.reshape(lead + (2, 4, P, n, 256)) for w in (g, u)], axis=-2)
        both = both.transpose(tuple(range(k)) + (k + 3, k, k + 2, k + 1, k + 4, k + 5))
        return np.ascontiguousarray(both).reshape(lead + (n, 2, P, UNIT))

    def rows(w):
        lead, n = w.shape[:-2], w.shape[-2] // 256
        k = len(lead)
        w = w.reshape(lead + (n, 2, P, DM)).transpose(tuple(range(k)) + (k, k + 2, k + 1, k + 3))
        return np.ascontiguousarray(w).reshape(lead + (n, P, UNIT))

    def per_channel(w):
        return w.reshape(2, -1, P).transpose(0, 2, 1)

    def every(v):
        return np.broadcast_to(np.asarray(v)[..., None, :], np.asarray(v).shape[:-1] + (P, np.asarray(v).shape[-1]))
    out = {}
    x = np32("x")[0]
    out["x"] = x
    out["xT"] = x.T.reshape(KC, P, S).transpose(1, 0, 2)
    out["pT"] = np32("p")[:, 0].transpose(0, 2, 1).reshape(2, 2, P, S).transpose(0, 2, 1, 3)
    out["positions"] = np32("positions")[0].reshape(NT, P).T
    out["sinks"] = every(np32("sinks")[0])
    out["alog"] = np.broadcast_to(np32("dn_a_log_2")[None], (P, 2, DN_H))
    out["dtb"] = np.broadcast_to(np32("dn_dt_bias_2")[None], (P, 2, DN_H))
    out["wr"] = np32("w_router")[0].reshape(KC, P, NE).transpose(1, 0, 2)
    rowsv = []
    for L in range(2):
        rowsv += [np32("ln_mix_g")[L], np32("ln_mix_b")[L], np32("ln_ffn_g")[L], np32("ln_ffn_b")[L]]
    for L in range(2):
        rowsv += [np32("post_mix_norm_2")[L], np32("post_ffn_norm_2")[L]]
    out["vecs"] = every(np.stack(rowsv))
    out["wu_qkv"] = natural(np32("w_qkv"))
    out["wu_o"] = natural(np32("w_o"))
    out["wu_ffn_gu"] = paired(np32("w_ffn_gate")[0], np32("w_ffn_up")[0])
    out["wu_ffn_d"] = rows(np32("w_ffn_down")[0])
    out["wu_pp"] = rows(np32("w_ple_proj"))[:, 0]
    out["wu_pg"] = natural(np32("w_ple_gate"))
    for name, src in (("wu_eg", "w_exp_gate"), ("wu_eu", "w_exp_up")):
        out[name] = natural(np32(src)[0]).reshape(NE, EXP_STEPS, 2, P, UNIT)
    out["wu_ed"] = rows(np32("w_exp_down")[0]).reshape(NE, EXP_STEPS, 2, P, UNIT)
    w_in = np32("w_in_2")
    out["wu_in"] = natural(np.concatenate([w_in[:, :, :2048], w_in[:, :, 2056:]], axis=2))
    out["wba"] = w_in[:, :, 2048:2056].reshape(2, KC, P, 8).transpose(0, 2, 1, 3)
    out["wu_out"] = natural(np32("w_out_2"))
    up = np32("ffn_up_2")
    out["wu_up"] = paired(up[:, :, :FF2], up[:, :, FF2:])
    out["wu_down"] = rows(np32("ffn_down_2"))
    out["cw"] = np32("dn_conv_2").reshape(2, 4, 12, P).transpose(0, 3, 2, 1)
    out["fcw"] = np.concatenate([np32("ffn_conv_2"), np32("ffn_conv_bias_2")[:, None]], axis=1) \
        .reshape(2, 4, 44, P).transpose(0, 3, 2, 1)
    out["prew"] = np.stack([per_channel(np32("pre_mix_norm_2")), per_channel(np32("pre_ffn_norm_2"))], axis=2)
    out["onorm"] = every(np32("dn_out_norm_2"))
    out["cst"] = constants()[0]
    return {k: np.ascontiguousarray(v) for k, v in out.items()}


def kernel(_debug=None, **inputs):
    import concourse.bacc as bacc
    from concourse.bass_utils import run_bass_kernel_spmd

    arrays = layout(inputs)
    plan = Plan()
    for _ in range(2):
        plan.opens.clear()
        nc = bacc.Bacc("TRN2", target_bir_lowering=False, num_devices=1)
        aps = {n: nc.dram_tensor(f"in_{n}", list(v.shape), mybir.dt.from_np(v.dtype), kind="ExternalInput").ap()
               for n, v in arrays.items()}
        aps["out"] = nc.dram_tensor("out_x", list(_OUT), F32, kind="ExternalOutput").ap()
        if _debug:
            aps["dbg"] = nc.dram_tensor("dbg", [len(_debug["dump"]), S, DM], F32, kind="ExternalOutput").ap()
        build_program(nc, aps, plan, _debug)
    r = run_bass_kernel_spmd(nc, [{f"in_{n}": v for n, v in arrays.items()}], core_ids=[0])
    if _debug:
        return r
    return r.results[0]["out_x"].reshape(1, S, DM)
```

```python
from contextlib import ExitStack

import numpy as np
import concourse.bass as bass
from concourse import mybir

F32R = mybir.dt.float32r
F32 = mybir.dt.float32
I32 = mybir.dt.int32
ALU = mybir.AluOpType
ACT = mybir.ActivationFunctionType
AXX = mybir.AxisListType.X

P = 128
S = 256
NT = S // P
DM = 1024
KC = DM // P
NHEAD = 16
DH = 64
FF1 = 3584
FF2 = 2816
NE = 8
UNIT = 2048
RAW = 6
SPLIT = 3
NEG = -1.0e30
ALPHA = float((2.0 * 2) ** 0.25)
LN_EPS = 1e-5
RMS_EPS = 1e-6
DN_H = 4
N_DN = DN_H * NT
LEVELS = 7
MAGIC = 12582912.0
VSLOTS = 2

FFN_STEPS = {0: FF1 // 256, 2: FF2 // 256, 3: FF2 // 256}
EXP_STEPS = FF1 // 512


def masks():
    p, f = np.arange(P)[:, None], np.arange(P)[None, :]
    q0, q1 = np.arange(P)[:, None], P + np.arange(P)[:, None]
    k0, k1 = np.arange(P)[None, :], np.arange(S)[None, :]
    out = np.zeros((4, P, 1024), np.float32)

    def both(rule):
        return np.concatenate([rule(q0 - k0), rule(q1 - k1)], axis=1)

    def dilated(d):
        n = ((d >= 0) & (d <= 128)).astype(np.float64)
        n = n + ((d >= 0) & (d % 4 == 0)) + ((d >= 0) & (d % 16 == 0))
        return np.where(n > 0, np.log(np.maximum(n, 1.0)), NEG)
    out[0, :, :384] = both(lambda d: np.where(d >= 0, 0.0, NEG))
    out[1, :, :384] = both(lambda d: np.where((d >= 0) & (d < 128), 0.0, NEG))
    out[2, :, :384] = both(dilated)
    for n in range(LEVELS):
        b = 1 << n
        same = (p // (2 * b)) == (f // (2 * b))
        out[3, :, n * P:(n + 1) * P] = same & ((f // b) % 2 == 1) & ((p // b) % 2 == 0)
    out[3, :, LEVELS * P:(LEVELS + 1) * P] = np.where(f >= p, 0.0, NEG)
    return out


def constants():
    p = np.arange(P)[:, None]
    f = np.arange(P)[None, :]
    parts = {}
    parts["ident"] = (p == f)
    parts["ones"] = np.ones((P, P))
    parts["upto"] = (p <= f)
    parts["before"] = (p < f)
    parts["iota"] = np.broadcast_to(np.arange(S)[None, :], (P, S))
    parts["rank"] = np.broadcast_to(8.0 - np.arange(NE)[None, :], (P, NE))
    inv = (1.0 / (np.float32(500000.0) ** (np.arange(0, 16, 2, dtype=np.float32) / np.float32(16)))).astype(np.float32)
    parts["inv"] = np.broadcast_to(inv[None, :], (P, 8))
    inv2 = (np.float32(500000.0) ** (-np.arange(0, 16, 2, dtype=np.float32) / np.float32(16))).astype(np.float32)
    ang = np.arange(S, dtype=np.float32)[:, None] * inv2[None, :]
    tab = ang.reshape(NT, P, 8).transpose(1, 0, 2).reshape(P, NT * 8).astype(np.float64)
    parts["cos2"] = np.cos(tab)
    parts["sin2"] = np.sin(tab)
    parts["ln_eps"] = np.full((P, 1), LN_EPS)
    parts["rms_eps"] = np.full((P, 1), RMS_EPS)
    at, cols, n = {}, [], 0
    for name, a in parts.items():
        a = np.asarray(a, dtype=np.float32)
        at[name] = (n, a.shape[1])
        n += a.shape[1]
        cols.append(a)
    return np.ascontiguousarray(np.concatenate(cols, axis=1)), at


class Plan:

    def __init__(self):
        self.value, self.per, self.in_loop, self.opens = {}, {}, set(), {}


class Events:

    def __init__(self, nc, ctx, plan, tag):
        self.nc, self.ctx, self.plan, self.tag = nc, ctx, plan, tag
        self.turn, self.marked, self.seen = None, None, 0

    def new(self, name, step=1):
        return Event(self, name, step)

    def loop(self, turn):
        return Turns(self, turn)


class Turns:

    def __init__(self, events, turn):
        self.events, self.turn = events, turn

    def __enter__(self):
        self.events.turn, self.events.marked = self.turn, {}

    def __exit__(self, *_):
        ev = self.events
        for event, n in ev.marked.items():
            ev.plan.per[event.name] = n
            event.n += (NE - 1) * n
        ev.turn = ev.marked = None


class Event:
    counts = False

    def __init__(self, events, name, step):
        self.ev, self.name, self.step, self.n = events, events.tag + name, step, 0
        self.sem = events.ctx.enter_context(events.nc.semaphore(self.name)) if step else None

    def _turns(self):
        per = self.ev.plan.per.get(self.name, 0)
        return self.ev.turn * per if self.ev.turn is not None and per else 0

    def mark(self, *key):
        self.n += self.step or 1
        if self.ev.marked is not None:
            self.ev.marked[self] = self.ev.marked.get(self, 0) + (self.step or 1)
            self.ev.plan.in_loop.add((self.name, key))
        self.ev.plan.value[self.name, key] = self.n
        return self.sem, self.step

    def at(self, *key):
        v = self.ev.plan.value.get((self.name, key), 1)
        if self.counts:
            self.ev.seen = max(self.ev.seen, v + (self.ev.turn is None and (self.name, key) in self.ev.plan.in_loop)
                               * (NE - 1) * self.ev.plan.per.get(self.name, 0))
        if self.ev.turn is not None:
            return self.sem, v + self._turns()
        if (self.name, key) in self.ev.plan.in_loop:
            v += (NE - 1) * self.ev.plan.per.get(self.name, 0)
        return self.sem, v

    def last(self):
        return self.sem, self.n + self._turns()


class Groups(Event):
    counts = True


class Free(Event):

    def opened(self, groups):
        opens = self.ev.plan.opens.setdefault(self.name, [])
        turns = self._turns()
        n = self.n
        self.n += 1
        if self.ev.marked is not None:
            self.ev.marked[self] = self.ev.marked.get(self, 0) + 1
        opens.append((groups.n, self.n))
        return n, n + turns

    def mark(self, *key):
        use = 1
        for before, n in self.ev.plan.opens.get(self.name, ()):
            if before < self.ev.seen:
                use = max(use, n)
        self.ev.plan.value[self.name, key] = use
        if self.ev.marked is not None:
            self.ev.plan.in_loop.add((self.name, key))
        return self.sem, 1


def build_program(nc, A, plan, debug=None):
    cst_np, cst_at = constants()
    NC = cst_np.shape[1]
    with ExitStack() as ctx:
        def sb(name, shape, dt=F32):
            return ctx.enter_context(nc.sbuf_tensor(name, shape, dt))

        raw = sb("raw", [P, RAW, UNIT])
        w_hi = sb("w_hi", [P, SPLIT, UNIT], F32R)
        w_lo = sb("w_lo", [P, SPLIT, UNIT], F32R)
        cst = sb("cst", [P, NC])
        X = sb("X", [P, NT, DM])
        R = sb("R", [P, NT, DM])
        xT = [sb(f"xT_{part}", [P, KC, S], F32R) for part in ("hi", "lo")]
        aT = [sb(f"aT_{part}", [P, KC, S], F32R) for part in ("hi", "lo")]
        hT = [a[:, 0:4, :].rearrange("p (i m) n -> p i m n", m=2) for a in aT]
        hTe = [a[:, 4:8, :].rearrange("p (i m) n -> p i (m n)", m=2) for a in aT]
        xe = [a[:, 0:4, :].rearrange("p c n -> p (c n)").rearrange("p (c n) -> p c n", n=P) for a in xT]
        msk = sb("msk", [P, 1024])
        vec = sb("vec", [P, VSLOTS, DM])
        small = sb("small", [P, 640])
        pos_i = sb("pos_i", [P, NT], I32)
        flag_i = sb("flag_i", [P, 1], I32)
        ARENA = 10240
        arena = sb("arena", [P, ARENA])

        def carve(start, shapes):
            out, at = {}, start
            for name, shape in shapes:
                n = int(np.prod(shape))
                ap = arena[:, at:at + n]
                if len(shape) > 1:
                    letters = "abcd"[:len(shape)]
                    ap = ap.rearrange("p (" + " ".join(letters) + ") -> p " + " ".join(letters),
                                      **{c: s for c, s in zip(letters[1:], shape[1:])})
                out[name] = ap
                at += n
            assert at <= ARENA, at
            return out

        att = carve(0, [("qn", (NT, 1536)), ("kd", (NT, 4, 2, DH)), ("qT", (8, S)), ("kT", (4, S)),
                        ("pt", (2, 384)), ("tmp", (4, 20, 8))])
        for name, t in (("s", 0), ("pr", 1)):
            att[name] = att["qn"][:, t, 0:768].rearrange("p (i n) -> p i n", i=2)
        Rf = R[:, :, :].rearrange("p t d -> p (t d)")
        att["sg"] = Rf.rearrange("p (a n) -> p a n", n=512)
        dn = carve(0, [("cv", (12, S)), ("z", (NT, 512)), ("gB", (N_DN, P)), ("bB", (N_DN, P)),
                       ("gam", (N_DN, P)), ("kb", (DN_H, S)), ("DT", (N_DN, P)), ("Xl", (N_DN, P))])
        dn["vb"] = Rf[:, 0:1024].rearrange("p (a n) -> p a n", n=P)
        dn["kbg"] = Rf[:, 1024:1536].rearrange("p (a n) -> p a n", n=P)
        dn["kdec"] = Rf[:, 1536:2048].rearrange("p (a n) -> p a n", n=P)
        dn["LT"] = dn["kb"].rearrange("p a b -> p (a b)").rearrange("p (a n) -> p a n", n=P)
        dn["D"] = dn["gam"]
        dn["AT"] = dn["gB"]
        dn["qk"] = dn["bB"]
        dn["u"] = dn["LT"]
        dn["wT"] = dn["Xl"][:, 0:DN_H, :]
        dn["state"] = dn["Xl"][:, DN_H:, :]
        dn["vn"] = dn["kdec"]
        dn["o"] = dn["D"]
        dn["sq"] = dn["gam"]
        ffn = carve(0, [("sg", (2, 2, S)), ("cbg", (2, 2, S)), ("cbv", (2, 2, S)), ("gg", (2, 2, S)), ("h", (2, 2, S))])
        moe = carve(0, [("sel", (NT, P)), ("selg", (NT, P)), ("sgT", (S,)), ("sg", (2, 512)), ("h", (2, 512)),
                        ("ye", (DM,))])
        turned_in = carve(0, [("w", (4, 4, P))])["w"]
        junk = arena[:, 7680:9728].rearrange("p (t d) -> p t d", t=NT)
        pT = arena[:, 9728:10240].rearrange("p (c n) -> p c n", c=2)

        bank = [ctx.enter_context(nc.psum_tensor(f"bank{b}", [P, 512], F32)) for b in range(8)]

        def C(name, a=0, b=None):
            at, n = cst_at[name]
            return cst[:, at + a:at + (n if b is None else b)]

        ident, ones = C("ident"), C("ones")
        used = [0]

        def sm(*shape):
            n = int(np.prod(shape))
            ap = small[:, used[0]:used[0] + n]
            used[0] += n
            if len(shape) > 1:
                letters = "abcd"[:len(shape)]
                ap = ap.rearrange("p (" + " ".join(letters) + ") -> p " + " ".join(letters),
                                  **{c: s for c, s in zip(letters[1:], shape[1:])})
            return ap
        cos1, sin1 = sm(NT, 8), sm(NT, 8)
        ang, red, rnd = sm(NT, 8), sm(NT, 8), sm(NT, 8)
        pos_f = sm(NT)
        sinks = sm(NHEAD)
        nmax, rsum, esink, rden = sm(2, 2), sm(2, 2), sm(2, 2), sm(2, 2)
        st6, mv, sd, rstd = sm(NT, 2, 6), sm(NT, 2), sm(NT), sm(NT)
        ss = sm(NT, DN_H)
        lg, lg2, oh1, oh2, sc8 = sm(NT, NE), sm(NT, NE), sm(NT, NE), sm(NT, NE), sm(NT, NE)
        m1, m2, w1, w2 = sm(NT), sm(NT), sm(NT), sm(NT)
        memb, gates, posx = sm(NT, NE), sm(NT, NE), sm(NT, NE + 1)
        pcol, pcol2, gcol = sm(NT), sm(NT), sm(NT)
        flag_f = sm(1)
        tick = sm(9)
        ba, beta, sp1, sp2, gl = sm(NT, 8), sm(NT, DN_H), sm(NT, DN_H), sm(NT, DN_H), sm(NT, DN_H)
        alog, dtb = sm(2, DN_H), sm(2, DN_H)
        ngc, expg, kdsc, bexp = sm(NT, DN_H), sm(NT, DN_H), sm(DN_H), sm(DN_H)
        rn8 = sm(NT, DN_H)
        nsink = sm(NHEAD)
        wr = sb("wr", [P, KC, NE])
        wba = sb("wba", [P, KC, 8])
        wr_s = [sb(f"wr_{part}", [P, KC, NE], F32R) for part in ("hi", "lo")]
        wba_s = [sb(f"wba_{part}", [P, KC, 8], F32R) for part in ("hi", "lo")]
        cw = sb("cw", [P, 12, 4])
        fcw = sb("fcw", [P, 44, 4])
        prew = sb("prew", [P, 2, KC])
        onorm = sb("onorm", [P, P])

        def events(tag):
            ev = Events(nc, ctx, plan, tag)

            class E:
                pass
            E.ev = ev
            E.groups = Groups(ev, "groups", 1)
            E.free = [Free(ev, f"free{b}", 1) for b in range(8)]
            E.dve = ev.new("dve_step")
            E.act = ev.new("act_step")
            E.loaded = [ev.new(f"loaded{s}", 16) for s in range(RAW)]
            E.hi = ev.new("hi_ready")
            E.lo = ev.new("lo_ready")
            return E
        M = events("")
        V = events("ovf_")
        for event in V.free + [V.groups]:
            event.n = 1
        ev = M.ev
        x_ready = ev.new("x_ready")
        params = ev.new("params_loaded", 16)
        consts = ev.new("consts_loaded", 16)
        vecs = [ev.new(f"vec_loaded{s}", 16) for s in range(VSLOTS)]
        vec_used = ev.new("vec_used")
        mask_in = ev.new("mask_loaded", 16)
        xs_ready = ev.new("xT_split")
        wsmall = ev.new("small_weights_split")
        stored = ev.new("stored", 16)
        probs, roped, maxed, exped = ev.new("probs"), ev.new("roped"), ev.new("maxed"), ev.new("exped")
        stats, rooted, prenorm, hidden = ev.new("stats"), ev.new("rooted"), ev.new("prenorm"), ev.new("hidden")
        member, decided, flag_done = ev.new("member"), ev.new("decided"), ev.new("flag_done")
        angles, angles_done = ev.new("angles"), ev.new("angles_done")
        squares, decay, normed, inverse, gated = (ev.new("squares"), ev.new("decay"), ev.new("normed"), ev.new("inverse"),
                                                  ev.new("gated"))

        def overflow_done():
            return V.free[3].at("ovf", "sc", 1, 1)

        def stream_order():
            for L in range(4):
                if L < 2:
                    yield from [(("qkv", L, i), "wu_qkv", (L, i)) for i in range(6)]
                    yield from [(("wo", L, i), "wu_o", (L, i)) for i in range(4)]
                else:
                    yield from [(("in", L, i), "wu_in", (L - 2, i)) for i in range(14)]
                    yield from [(("wo", L, i), "wu_out", (L - 2, i)) for i in range(4)]
                if L == 1:
                    yield (("experts",), None, None)
                else:
                    n = FFN_STEPS[L]
                    gu, dw, pre = ("wu_ffn_gu", "wu_ffn_d", ()) if L == 0 else ("wu_up", "wu_down", (L - 2,))
                    for s in range(n):
                        yield (("gu", L, s, 0), gu, pre + (s, 0))
                        yield (("gu", L, s, 1), gu, pre + (s, 1))
                        if s:
                            yield (("dn", L, s - 1), dw, pre + (s - 1,))
                    yield (("dn", L, n - 1), dw, pre + (n - 1,))
                if L < 2:
                    yield from [(("pg", L, i), "wu_pg", (L, i)) for i in range(4)]
                    yield (("pp", L), "wu_pp", (L,))

        def expert_order():
            def gu(f):
                return [(("gu", f, h, i), ("wu_eg", "wu_eu")[h], (f, i)) for h in range(2) for i in range(2)]

            def down(f):
                return [(("dn", f, i), "wu_ed", (f, i)) for i in range(2)]
            out = gu(0)
            for f in range(EXP_STEPS):
                if f + 1 < EXP_STEPS:
                    out += gu(f + 1)
                if f:
                    out += down(f - 1)
            return out + down(EXP_STEPS - 1)
        EXPERT = expert_order()
        TURN = len(EXPERT)
        assert TURN % RAW == 0 and TURN % SPLIT == 0
        unit_at, n = {}, 0
        for key, arr, idx in stream_order():
            if key == ("experts",):
                expert_base = n
                n += NE * len(EXPERT)
            else:
                unit_at[key] = n
                n += 1
        whole = {unit_at["pp", L] for L in range(2)}
        last_read = plan.value.setdefault("last_read", {})
        after = expert_base + NE * TURN

        def split_no(i):
            return i - sum(1 for w in whole if w < i)

        def place(i):
            return split_no(i) % SPLIT

        def key_of(i):
            if i >= after and i - after < SPLIT:
                return expert_base + TURN + i - after
            return i

        def wait_loaded(E, eng, i):
            slot, n = i % RAW, 16 * (i // RAW + 1)
            if E.ev.turn is not None:
                n = n + E.ev.turn * (16 * TURN // RAW)
            eng.wait_ge(E.loaded[slot].sem, n)
            return raw[:, slot, :]

        def index(key, base=None):
            return unit_at[key] if base is None else base + order.index(key)
        order = [k for k, _, _ in EXPERT]

        def unit(E, pe, key, base=None):
            i = index(key, base)
            pe.wait_ge(*E.lo.at("unit", key_of(i)))
            return w_hi[:, place(i), :], w_lo[:, place(i), :]

        def released(E, i, *key):
            last_read[E.ev.tag, i] = key

        def reader(E, i):
            if E is M and expert_base <= i < after:
                i = expert_base + (i - expert_base) % TURN
            return E.groups.at(*last_read.get((E.ev.tag, i), ("none",)))

        def split_hi(E, ac, i):
            src = wait_loaded(E, ac, i)
            back = i - SPLIT - (1 if any(i - SPLIT <= w < i for w in whole) else 0)
            if E is V and i < SPLIT:
                ac.wait_ge(E.groups.sem, 1 + E.ev.turn * plan.per.get("ovf_groups", 0))
            elif back >= 0:
                ac.wait_ge(*reader(E, back))
            nc.scalar.copy(w_hi[:, place(i), :], src).then_inc(*E.hi.mark("unit", i))

        def split_lo(E, ve, i):
            ve.wait_ge(*E.hi.at("unit", i))
            nc.vector.tensor_tensor(w_lo[:, place(i), :], raw[:, i % RAW, :], w_hi[:, place(i), :].bitcast(F32), ALU.subtract) \
                .then_inc(*E.lo.mark("unit", i))

        def ahead(E, split, eng, key, base=None):
            i = index(key, base)
            if i in whole and E is M:
                return
            j = i + SPLIT
            if E is V and j >= TURN:
                return
            if E is M and base is None and i < expert_base <= j:
                return
            if E is M:
                j += sum(1 for w in whole if i < w <= j)
                if j in whole:
                    j += 1
            if j < n_units:
                split(E, eng, j)
        n_units = n

        block = ctx.enter_context(nc.Block())

        @block.sync
        def _(sp):
            for key, arr, idx in stream_order():
                if key == ("experts",):
                    sp.wait_ge(*M.lo.at("unit", expert_base - 1))
                    sp.wait_ge(*flag_done.at())
                    r = sp.value_load(flag_i[0:1, 0:1], min_val=0, max_val=1)
                    with sp.If(r > 0):
                        with sp.Fori(0, NE) as e:
                            with V.ev.loop(e):
                                sp.wait_ge(V.groups.sem, e * plan.per.get("ovf_groups", 0) + 1)
                                for j, (ekey, earr, eidx) in enumerate(EXPERT):
                                    if j >= RAW:
                                        sp.wait_ge(*V.lo.at("unit", j - RAW))
                                    sp.dma_start(raw[:, j % RAW, :], A[earr][e, eidx[0], eidx[1]]) \
                                        .then_inc(*V.loaded[j % RAW].mark())
                        sp.wait_ge(*overflow_done())
                    with sp.Fori(0, NE) as e:
                        with ev.loop(e):
                            for j, (ekey, earr, eidx) in enumerate(EXPERT):
                                i = expert_base + j
                                sem, v = M.lo.at("unit", expert_base + (j - RAW) % TURN)
                                sp.wait_ge(sem, v - plan.per.get("lo_ready", 0) if j < RAW else v)
                                sp.dma_start(raw[:, i % RAW, :], A[earr][e, eidx[0], eidx[1]]) \
                                    .then_inc(*M.loaded[i % RAW].mark())
                    continue
                i = unit_at[key]
                if i >= RAW:
                    old = i - RAW
                    if expert_base <= old < after:
                        old = expert_base + (old - expert_base) % TURN
                    sp.wait_ge(*(reader(M, old) if old in whole else M.lo.at("unit", key_of(old))))
                src = A[arr][idx] if len(idx) > 1 else A[arr][idx[0]]
                sp.dma_start(raw[:, i % RAW, :], src).then_inc(*M.loaded[i % RAW].mark())
            sp.wait_ge(*x_ready.at(3, "ffn", 1))
            sp.dma_start(A["out"].rearrange("(t p) d -> p t d", p=P), X[:, :, :]).then_inc(*stored.mark())
            sp.wait_ge(*stored.at())

        @block.gpsimd
        def _(gp):
            def load(*loads):
                for dst, src, key in loads:
                    gp.dma_start(dst, src).then_inc(*params.mark())
                for dst, src, key in loads:
                    plan.value[params.name, key] = params.n

            def load_vec(v):
                s = v % VSLOTS
                if v >= VSLOTS:
                    old = v - VSLOTS
                    if old % 2 == 0 or old > 8:
                        gp.wait_ge(*vec_used.at(old))
                    else:
                        gp.wait_ge(*x_ready.at(old // 4, "mix" if old % 4 == 1 else "ffn", 1))
                gp.dma_start(vec[:, s, :], A["vecs"][v]).then_inc(*vecs[s].mark())
            def load_mask(n):
                gp.dma_start(msk[:, :], A["masks"][n]).then_inc(*mask_in.mark())

            def load_layer(L):
                gp.wait_ge(*params.last())
                load((wba[:, :, :], A["wba"][L - 2], ("wba", L)), (cw[:, :, :], A["cw"][L - 2], ("cw", L)),
                     (fcw[:, :, :], A["fcw"][L - 2], ("fcw", L)), (prew[:, :, :], A["prew"][L - 2], ("prew", L)),
                     (onorm[:, :], A["onorm"][L - 2], ("onorm", L)))
            gp.dma_start(cst[:, :], A["cst"]).then_inc(*consts.mark())
            load((pos_i[:, :], A["positions"], ("pos",)), (sinks, A["sinks"], ("sinks",)),
                 (Rf, A["xT"].rearrange("p c n -> p (c n)"), ("xT",)),
                 (X[:, :, :], A["x"].rearrange("(t p) d -> p t d", p=P), ("X",)),
                 (alog, A["alog"], ("alog",)), (dtb, A["dtb"], ("dtb",)), (wr[:, :, :], A["wr"], ("wr",)))
            load_mask(0)
            load_vec(0)
            load_vec(1)
            for L in range(2):
                gp.wait_ge(*maxed.at(L, NHEAD - 1))
                load_mask(1 if L == 0 else 3)
                load_vec(4 * L + 2)
                load_vec(4 * L + 3)
                gp.wait_ge(*params.last())
                load((pT, A["pT"][L], ("pT", L)))
                load_vec(4 * L + 4)
                load_vec(4 * L + 5)
            load_layer(2)
            for L in (2, 3):
                gp.wait_ge(*inverse.at(L, LEVELS - 1, "LT", 1))
                load_mask(2)
                if L == 2:
                    gp.wait_ge(*maxed.at(L, 7))
                    load_mask(3)
                    load_vec(10)
                    load_vec(11)
                    gp.wait_ge(*x_ready.at(2, "ffn", 1))
                    load_layer(3)
            if debug:
                k = 0
                for L, w in debug["dump"]:
                    gp.wait_ge(*x_ready.at(L, w, 1))
                    gp.dma_start(A["dbg"][k].rearrange("(t p) d -> p t d", p=P), X[:, :, :]).then_inc(*stored.mark("dbg", k))
                    k += 1

        @block.tensor
        def _(pe):
            def open_bank(E, b):
                before, n = E.free[b].opened(E.groups)
                if before:
                    pe.wait_ge(E.free[b].sem, n)
                return bank[b]

            def transposes(stage, src, ready):
                for t in range(NT):
                    pe.wait_ge(*ready(t))
                    for g in range(2):
                        o = open_bank(M, 2 * t + g)
                        for c in range(4):
                            mm = nc.tensor.transpose(o[:, c * P:(c + 1) * P],
                                                     src[:, t, (4 * g + c) * P:(4 * g + c + 1) * P], ident)
                        mm.then_inc(*M.groups.mark("tx", stage, t, g))

            def mm3(o, l, r, first, last, lone=True, lcols=slice(None), rcols=slice(None)):
                for n, (i, j) in enumerate(((0, 0), (0, 1), (1, 0))):
                    mm = nc.tensor.matmul(o, l[i], r[j], start=(first and n == 0), stop=(last and n == 2),
                                          skip_group_check=not lone)
                return mm

            def linear(name, L, blocks, units, lhs, first=0):
                for nb in range(blocks):
                    o = [None] * NT
                    for i in range(2):
                        key = (units, L, 2 * (first + nb) + i)
                        u = unit(M, pe, key)
                        for t in range(NT):
                            if i == 0:
                                o[t] = open_bank(M, (2 * nb + t) % 4)
                            for kc in range(4 * i, 4 * i + 4):
                                mm = mm3(o[t][:, :], [a[:, kc, t * P:(t + 1) * P] for a in lhs],
                                         [w[:, (kc % 4) * 512:(kc % 4 + 1) * 512] for w in u], kc == 0, kc == KC - 1)
                            if i == 1:
                                mm.then_inc(*M.groups.mark(name, L, nb, t))
                        if i == 0:
                            mm.then_inc(*M.groups.mark("unit", *key))
                            released(M, unit_at[key], "unit", *key)
                        else:
                            released(M, unit_at[key], name, L, nb, 1)

            def features(o, key_a, key_b, cols, name_a, names_b):
                for i, key in enumerate((key_a, key_b)):
                    u = unit(M, pe, key)
                    for half in range(2):
                        for m in range(2):
                            for kc in range(4 * i, 4 * i + 4):
                                c0 = (kc % 4) * 512 + cols(half, m)
                                mm = mm3(o[half][:, m * S:(m + 1) * S], [w[:, c0:c0 + P] for w in u],
                                         [a[:, kc, :] for a in xT], kc == 0 and m == 0, kc == KC - 1, lone=False)
                        if i == 1:
                            mm.then_inc(*M.groups.mark(*names_b[half]))
                    if i == 0:
                        mm.then_inc(*M.groups.mark(*name_a))
                        released(M, unit_at[key], *name_a)
                    else:
                        released(M, unit_at[key], *names_b[1])

            def attention(L, heads, kchunk, out0):
                def scores(h):
                    j, lo = h // 2, DH * (h % 2)
                    o = open_bank(M, 4 + h % 2)
                    q = att["qT"][lo:lo + DH, j, :]
                    k = att["kT"][lo:lo + DH, kchunk(h), :]
                    nc.tensor.matmul(o[:, 0:P], q[:, 0:P], k[:, 0:P], start=True, stop=True)
                    nc.tensor.matmul(o[:, P:3 * P], q[:, P:S], k[:, :], start=True, stop=True) \
                        .then_inc(*M.groups.mark("sc", L, h))

                def turn(h):
                    pe.wait_ge(*probs.at(L, h))
                    o = open_bank(M, 6 + h % 2)
                    for c in range(3):
                        mm = nc.tensor.transpose(o[:, c * P:(c + 1) * P], att["pr"][:, h % 2, c * P:(c + 1) * P], ident)
                    mm.then_inc(*M.groups.mark("pt", L, h))

                def values(h):
                    j, lo = h // 2, DH * (h % 2)
                    o = bank[2 + j % 2] if h % 2 else open_bank(M, 2 + j % 2)
                    pe.wait_ge(*M.free[6 + h % 2].at("pt", L, h))
                    vcol = 1280 + DH * (h // 4) if L < 2 else 1024 + DH * h
                    nc.tensor.matmul(o[lo:lo + DH, 0:S], att["qn"][:, 0, vcol:vcol + DH], att["pt"][:, h % 2, 0:S],
                                     start=True, stop=False)
                    nc.tensor.matmul(o[lo:lo + DH, P:S], att["qn"][:, 1, vcol:vcol + DH], att["pt"][:, h % 2, S:S + P],
                                     start=False, stop=True).then_inc(*M.groups.mark("pv", L, h))
                for i in range(heads + 2):
                    if i < heads:
                        scores(i)
                    if 0 <= i - 1 < heads:
                        turn(i - 1)
                    if i >= 2:
                        values(i - 2)

            def turn_qk(L, nq):
                for t in range(NT):
                    pe.wait_ge(*roped.at(L, t))
                    for g in range(nq // 4 + 1):
                        o = open_bank(M, (3 * t + g) % 4)
                        for c in range(4):
                            if g < nq // 4:
                                src = att["qn"][:, t, (4 * g + c) * P:(4 * g + c + 1) * P]
                            elif L < 2:
                                src = att["kd"][:, t, c, :, :].rearrange("p a b -> p (a b)")
                            else:
                                src = att["qn"][:, t, 512 + c * P:512 + (c + 1) * P]
                            mm = nc.tensor.transpose(o[:, c * P:(c + 1) * P], src, ident)
                        mm.then_inc(*M.groups.mark("qkT", L, t, g))
                for t in range(NT):
                    for g in range(nq // 4 + 1):
                        pe.wait_ge(*M.free[(3 * t + g) % 4].at("qkT", L, t, g))

            def xT_ready(stage):
                for t in range(NT):
                    for g in range(2):
                        if stage[0] < 2:
                            pe.wait_ge(*M.free[2 * t + g].at("xT", stage, t, g))
                        else:
                            pe.wait_ge(*xs_ready.at(stage, t, g))

            def dense_ffn(L):
                n = FFN_STEPS[L]

                def gate_up(s):
                    o = [open_bank(M, 4 + 2 * (s % 2) + half) for half in range(2)]
                    features(o, ("gu", L, s, 0), ("gu", L, s, 1), lambda half, m: half * 256 + m * P,
                             ("unit", "gu", L, s, 0), [("gu", L, s, 0), ("gu", L, s, 1)])

                def down(s):
                    d = unit(M, pe, ("dn", L, s))
                    pe.wait_ge(*hidden.at(L, s))
                    for t in range(NT):
                        for nb in range(2):
                            o = open_bank(M, 2 * t + nb) if s == 0 else bank[2 * t + nb]
                            for m in range(2):
                                c0 = m * DM + nb * 512
                                mm = mm3(o[:, :], [a[:, s % 2, m, t * P:(t + 1) * P] for a in hT],
                                         [w[:, c0:c0 + 512] for w in d], s == 0 and m == 0, s == n - 1 and m == 1)
                    mm.then_inc(*M.groups.mark("down", L, s))
                    released(M, unit_at["dn", L, s], "down", L, s)
                gate_up(0)
                for s in range(n):
                    if s + 1 < n:
                        gate_up(s + 1)
                    down(s)

            def router():
                pe.wait_ge(*wsmall.at("wr"))
                for t in range(NT):
                    o = open_bank(M, t)
                    for kc in range(KC):
                        mm = mm3(o[:, 0:NE], [a[:, kc, t * P:(t + 1) * P] for a in xT], [w[:, kc, :] for w in wr_s],
                                 kc == 0, kc == KC - 1)
                    mm.then_inc(*M.groups.mark("router", t))
                pe.wait_ge(*member.at())
                o = open_bank(M, 2)
                nc.tensor.matmul(o[:, 0:NE], C("before"), memb[:, 0, :], start=True, stop=True)
                nc.tensor.matmul(o[:, NE:2 * NE], ones, memb[:, 0, :], start=True, stop=False)
                nc.tensor.matmul(o[:, NE:2 * NE], C("before"), memb[:, 1, :], start=False, stop=True)
                nc.tensor.matmul(o[:, 2 * NE:3 * NE], ones, memb[:, 0, :], start=True, stop=False)
                nc.tensor.matmul(o[:, 2 * NE:3 * NE], ones, memb[:, 1, :], start=False, stop=True) \
                    .then_inc(*M.groups.mark("ranks"))

            def gather(E, tag, which):
                pe.wait_ge(*E.dve.at(tag, which, "sel"))
                for g in range(2):
                    o = open_bank(E, 2 + g)
                    for c in range(4):
                        for t in range(NT):
                            mm = nc.tensor.matmul(o[:, c * P:(c + 1) * P], X[:, t, (4 * g + c) * P:(4 * g + c + 1) * P],
                                                  moe["sel"][:, t, :], start=(t == 0), stop=(t == NT - 1))
                    mm.then_inc(*E.groups.mark(tag, which, "ga", g))

            def gathered(E, tag, which):
                for g in range(2):
                    pe.wait_ge(*E.free[2 + g].at(tag, which, "xe", g))

            def experts(E, tag, base):
                if E is V:
                    gather(E, tag, "own")
                    gathered(E, tag, "own")
                pe.wait_ge(*E.dve.at(tag, "selg"))
                o = open_bank(E, 2)
                for t in range(NT):
                    mm = nc.tensor.transpose(o[:, t * P:(t + 1) * P], moe["selg"][:, t, :], ident)
                mm.then_inc(*E.groups.mark(tag, "tg"))

                def gate_up(f):
                    for half in range(2):
                        o = open_bank(E, 4 + 2 * (f % 2) + half)
                        for i in range(2):
                            key = ("gu", f, half, i)
                            u = unit(E, pe, key, base)
                            for kc in range(4 * i, 4 * i + 4):
                                mm = mm3(o[:, :], [a[:, kc, :] for a in xe], [w[:, (kc % 4) * 512:(kc % 4 + 1) * 512] for w in u],
                                         kc == 0, kc == KC - 1)
                            name = (tag, "unit") + key if i == 0 else (tag, "gu", f, half)
                            mm.then_inc(*E.groups.mark(*name))
                            released(E, index(key, base), *name)

                def turn(f):
                    pe.wait_ge(*E.free[5 + 2 * (f % 2)].at(tag, "h", f))
                    o = open_bank(E, 2 + f % 2)
                    for c in range(4):
                        mm = nc.tensor.transpose(o[:, c * P:(c + 1) * P], moe["h"][:, f % 2, c * P:(c + 1) * P], ident)
                    mm.then_inc(*E.groups.mark(tag, "tr", f))

                def down(f):
                    o = [open_bank(E, nb) if f == 0 else bank[nb] for nb in range(2)]
                    for i in range(2):
                        key = ("dn", f, i)
                        d = unit(E, pe, key, base)
                        if i == 0:
                            pe.wait_ge(*E.free[2 + f % 2].at(tag, "hTe", f))
                        for nb in range(2):
                            for c in range(2):
                                cc = 2 * i + c
                                c0 = c * DM + nb * 512
                                mm = mm3(o[nb][:, :], [a[:, f % 2, cc * P:(cc + 1) * P] for a in hTe], [w[:, c0:c0 + 512] for w in d],
                                         f == 0 and cc == 0, f == EXP_STEPS - 1 and cc == 3)
                        name = (tag, "unit") + key if i == 0 else (tag, "dn", f)
                        mm.then_inc(*E.groups.mark(*name))
                        released(E, index(key, base), *name)
                gate_up(0)
                for f in range(EXP_STEPS):
                    if f + 1 < EXP_STEPS:
                        gate_up(f + 1)
                    turn(f)
                    if f:
                        down(f - 1)
                    if E is M and f == EXP_STEPS - 1:
                        gather(E, tag, "next")
                down(EXP_STEPS - 1)
                pe.wait_ge(*E.free[0].at(tag, "ye", 0))
                pe.wait_ge(*E.free[1].at(tag, "ye", 1))
                for t in range(NT):
                    for nb in range(2):
                        o = open_bank(E, 2 + nb)
                        nc.tensor.matmul(o[:, :], moe["sgT"][:, t * P:(t + 1) * P], moe["ye"][:, nb * 512:(nb + 1) * 512],
                                         start=True, stop=True).then_inc(*E.groups.mark(tag, "sc", t, nb))
                if E is M:
                    gathered(E, tag, "next")

            def delta(L):
                for nb in range(3):
                    o = [open_bank(M, 2 * (nb % 2) + j) for j in range(2)]
                    features(o, ("in", L, 2 * nb), ("in", L, 2 * nb + 1), lambda j, m: (2 * j + m) * P,
                             ("unit", "in", L, 2 * nb), [("cv", L, 2 * nb), ("cv", L, 2 * nb + 1)])
                linear("z", L, 1, "in", xT, first=3)
                pe.wait_ge(*wsmall.at("wba", L))
                o = open_bank(M, 2)
                for t in range(NT):
                    for kc in range(KC):
                        mm = mm3(o[:, t * 8:t * 8 + 8], [a[:, kc, t * P:(t + 1) * P] for a in xT],
                                 [w[:, kc, :] for w in wba_s], kc == 0, kc == KC - 1)
                mm.then_inc(*M.groups.mark("ba", L))
                for g in range(4):
                    pe.wait_ge(*squares.at(L, g))
                    o = open_bank(M, 4 + g)
                    nc.tensor.matmul(o[:, :], ones, dn["sq"][:, 4 * (g % 2):4 * (g % 2) + 4, :].rearrange("p a b -> p (a b)"),
                                     start=True, stop=True).then_inc(*M.groups.mark("ssq", L, g))
                pe.wait_ge(*decay.at(L, "g"))
                o = open_bank(M, 6)
                for t in range(NT):
                    mm = nc.tensor.matmul(o[:, t * DN_H:(t + 1) * DN_H], C("upto"), gl[:, t, :], start=True, stop=True)
                mm.then_inc(*M.groups.mark("gcol", L))
                pe.wait_ge(*decay.at(L, "rows"))
                for name, src, rhs, b0 in (("grow", dn["gB"], C("upto"), 0), ("brow", dn["bB"], ident, 2)):
                    for t in range(NT):
                        o = open_bank(M, b0 + t)
                        for h in range(DN_H):
                            mm = nc.tensor.matmul(o[:, h * P:(h + 1) * P], src[:, t * DN_H + h, :], rhs, start=True, stop=True)
                        mm.then_inc(*M.groups.mark(name, L, t))
                pe.wait_ge(*normed.at(L, 3))
                for name, c0, b0 in (("kn", DN_H, 4), ("vn", 2 * DN_H, 6)):
                    for t in range(NT):
                        o = open_bank(M, b0 + t)
                        for h in range(DN_H):
                            mm = nc.tensor.transpose(o[:, h * P:(h + 1) * P], dn["cv"][:, c0 + h, t * P:(t + 1) * P], ident)
                        mm.then_inc(*M.groups.mark(name, L, t))
                for name, b0 in (("kk", 0), ("kq", 2)):
                    for t in range(NT):
                        if name == "kk":
                            pe.wait_ge(*M.free[2 + t].at("brow", L, t))
                        o = open_bank(M, b0 + t)
                        for h in range(DN_H):
                            rhs = dn["kb"][:, h, t * P:(t + 1) * P] if name == "kk" else dn["cv"][:, h, t * P:(t + 1) * P]
                            mm = nc.tensor.matmul(o[:, h * P:(h + 1) * P], dn["cv"][:, DN_H + h, t * P:(t + 1) * P], rhs,
                                                  start=True, stop=True)
                        mm.then_inc(*M.groups.mark(name, L, t))
                for n in range(LEVELS):
                    for t in range(NT):
                        pe.wait_ge(*inverse.at(L, n, "LT", t))
                        o = open_bank(M, t)
                        for h in range(DN_H):
                            i = t * DN_H + h
                            if n == 0:
                                mm = nc.tensor.transpose(o[:, h * P:(h + 1) * P], dn["LT"][:, i, :], ident)
                            else:
                                mm = nc.tensor.matmul(o[:, h * P:(h + 1) * P], dn["LT"][:, i, :], dn["D"][:, i, :], start=True, stop=True)
                        mm.then_inc(*M.groups.mark("lv", L, n, "X", t))
                    if n == 0:
                        continue
                    for t in range(NT):
                        pe.wait_ge(*M.free[t].at("lv", L, n, "X", t))
                        for which, b in ((0, 2 + t), (1, 4 + t)):
                            if which == 0 and n == LEVELS - 1:
                                continue
                            o = open_bank(M, b)
                            for h in range(DN_H):
                                i = t * DN_H + h
                                a, r = (dn["DT"], dn["Xl"]) if which == 0 else (dn["Xl"], dn["DT"])
                                mm = nc.tensor.matmul(o[:, h * P:(h + 1) * P], a[:, i, :], r[:, i, :], start=True, stop=True)
                            mm.then_inc(*M.groups.mark("lv", L, n, "D" if which == 0 else "DT", t))
                for t in range(NT):
                    pe.wait_ge(*M.free[4 + t].at("lv", L, LEVELS - 1, "DT", t))
                for t in range(NT):
                    pe.wait_ge(*M.free[4 + t].at("kn", L, t))
                    pe.wait_ge(*M.free[6 + t].at("vn", L, t))
                for t in range(NT):
                    o = open_bank(M, t)
                    for h in range(DN_H):
                        i = t * DN_H + h
                        mm = nc.tensor.matmul(o[:, h * P:(h + 1) * P], dn["DT"][:, i, :], dn["vb"][:, i, :], start=True, stop=True)
                    mm.then_inc(*M.groups.mark("u", L, t))
                o = open_bank(M, 2)
                for h in range(DN_H):
                    mm = nc.tensor.matmul(o[:, h * P:(h + 1) * P], dn["kbg"][:, h, :], dn["DT"][:, DN_H + h, :], start=True, stop=True)
                mm.then_inc(*M.groups.mark("wT", L))
                pe.wait_ge(*M.free[0].at("u", L, 0))
                o = open_bank(M, 3)
                for h in range(DN_H):
                    mm = nc.tensor.matmul(o[:, h * P:(h + 1) * P], dn["kdec"][:, h, :], dn["u"][:, h, :], start=True, stop=True)
                mm.then_inc(*M.groups.mark("state", L))
                o = open_bank(M, 4)
                for h in range(DN_H):
                    mm = nc.tensor.matmul(o[:, h * P:(h + 1) * P], dn["qk"][:, h, :], dn["u"][:, h, :], start=True, stop=True)
                mm.then_inc(*M.groups.mark("o0", L))
                pe.wait_ge(*M.free[3].at("state", L))
                pe.wait_ge(*M.free[2].at("wT", L))
                o = open_bank(M, 5)
                for h in range(DN_H):
                    mm = nc.tensor.matmul(o[:, h * P:(h + 1) * P], dn["wT"][:, h, :], dn["state"][:, h, :], start=True, stop=True)
                mm.then_inc(*M.groups.mark("ws", L))
                o = open_bank(M, 6)
                for h in range(DN_H):
                    mm = nc.tensor.matmul(o[:, h * P:(h + 1) * P], dn["cv"][:, h, P:S], dn["state"][:, h, :], start=True, stop=True)
                mm.then_inc(*M.groups.mark("qs", L))
                pe.wait_ge(*M.free[5].at("ws", L))
                o = open_bank(M, 7)
                for h in range(DN_H):
                    mm = nc.tensor.matmul(o[:, h * P:(h + 1) * P], dn["qk"][:, DN_H + h, :], dn["vn"][:, h, :], start=True, stop=True)
                mm.then_inc(*M.groups.mark("o1", L))
                for t in range(NT):
                    pe.wait_ge(*gated.at(L, t))
                    o = open_bank(M, t)
                    for h in range(DN_H):
                        mm = nc.tensor.transpose(o[:, h * P:(h + 1) * P], dn["o"][:, t * DN_H + h, :], ident)
                    mm.then_inc(*M.groups.mark("oT", L, t))

            pe.wait_ge(*consts.at())
            for L in range(2):
                if L == 0:
                    pe.wait_ge(*xs_ready.at("first"))
                else:
                    transposes((L, "in"), X, lambda t: x_ready.at(0, "ple", t))
                    xT_ready((L, "in"))
                linear("qkv", L, 3, "qkv", xT)
                turn_qk(L, 8)
                attention(L, NHEAD, lambda h: h // 4, 0)
                for j in range(8):
                    pe.wait_ge(*M.free[2 + j % 2].at("pv", L, j))
                linear("wo", L, 2, "wo", aT)
                transposes((L, "mix"), X, lambda t: x_ready.at(L, "mix", t))
                xT_ready((L, "mix"))
                if L == 0:
                    dense_ffn(0)
                else:
                    router()
                    pe.wait_ge(*flag_done.at())
                    r = pe.value_load(flag_i[0:1, 0:1], min_val=0, max_val=1)
                    with pe.If(r > 0):
                        with pe.Fori(0, NE) as e:
                            with V.ev.loop(e):
                                experts(V, "ovf", 0)
                        pe.wait_ge(*overflow_done())
                    gather(M, "moe", "first")
                    gathered(M, "moe", "first")
                    with pe.Fori(0, NE) as e:
                        with ev.loop(e):
                            experts(M, "moe", expert_base)
                transposes((L, "ffn"), X, lambda t: x_ready.at(L, "ffn", t))
                xT_ready((L, "ffn"))
                linear("pg", L, 2, "pg", xT)
                u = wait_loaded(M, pe, unit_at["pp", L])
                pe.wait_ge(*params.at("pT", L))
                for nb in range(2):
                    for t in range(NT):
                        o = open_bank(M, 4 + 2 * nb + t)
                        for kc in range(2):
                            mm = nc.tensor.matmul(o[:, :], pT[:, kc, t * P:(t + 1) * P],
                                                  u[:, kc * DM + nb * 512:kc * DM + (nb + 1) * 512],
                                                  start=(kc == 0), stop=(kc == 1))
                        mm.then_inc(*M.groups.mark("pp", L, nb, t))
                released(M, unit_at["pp", L], "pp", L, 1, 1)
            for L in range(2, 4):
                transposes((L, "in"), R, lambda t: prenorm.at(L, "in", t))
                xT_ready((L, "in"))
                delta(L)
                linear("bqkv", L, 3, "in", xT, first=4)
                turn_qk(L, 4)
                attention(L, 8, lambda h: h // 2, 4)
                for t in range(NT):
                    pe.wait_ge(*M.free[t].at("oT", L, t))
                for j in range(4):
                    pe.wait_ge(*M.free[2 + j % 2].at("pv", L, j))
                linear("wo", L, 2, "wo", aT)
                transposes((L, "mix"), R, lambda t: prenorm.at(L, "mix", t))
                xT_ready((L, "mix"))
                dense_ffn(L)

        @block.scalar
        def _(ac):
            def wait_self(E=M):
                ac.wait_ge(*E.act.last())

            def walk(*key):
                ahead(M, split_hi, ac, key)

            def copy_T(stage, L):
                for t in range(NT):
                    for g in range(2):
                        if L < 2:
                            ac.wait_ge(*M.groups.at("tx", stage, t, g))
                            src = bank[2 * t + g][:, :].rearrange("p (c n) -> p c n", n=P)
                        else:
                            ac.wait_ge(*M.free[2 * t + g].at("xT", stage, t, g))
                            src = turned_in[:, 2 * t + g, :, :]
                        nc.scalar.copy(xT[0][:, 4 * g:4 * g + 4, t * P:(t + 1) * P], src) \
                            .then_inc(*M.act.mark("xT", stage, t, g))

            def qkv_out(name, L, nq):
                units, first = ("qkv", 0) if L < 2 else ("in", 4)
                for nb in range(3):
                    walk(units, L, 2 * (first + nb))
                    for t in range(NT):
                        ac.wait_ge(*M.groups.at(name, L, nb, t))
                        b = (2 * nb + t) % 4
                        nc.scalar.activation(att["qn"][:, t, nb * 512:(nb + 1) * 512], bank[b][:, :], ACT.Copy,
                                             scale=(DH ** -0.5 if nb < nq else 1.0)).then_inc(*M.free[b].mark(name, L, nb, t))
                    walk(units, L, 2 * (first + nb) + 1)

            def copy_qkT(L, nq):
                for t in range(NT):
                    for g in range(nq // 4 + 1):
                        b = (3 * t + g) % 4
                        ac.wait_ge(*M.groups.at("qkT", L, t, g))
                        dst = att["qT"][:, 4 * g:4 * g + 4, t * P:(t + 1) * P] if g < nq // 4 \
                            else att["kT"][:, :, t * P:(t + 1) * P]
                        nc.scalar.copy(dst, bank[b][:, :].rearrange("p (c n) -> p c n", n=P)) \
                            .then_inc(*M.free[b].mark("qkT", L, t, g))

            def attention(L, heads, out0):
                def exps(h):
                    i = h % 2
                    ac.wait_ge(*maxed.at(L, h))
                    if h >= 2:
                        ac.wait_ge(*M.groups.at("pt", L, h - 2))
                    for q, (a, b) in enumerate(((0, P), (P, 3 * P))):
                        ins = nc.scalar.activation(att["pr"][:, i, a:b], att["s"][:, i, a:b], ACT.Exp,
                                                   bias=nmax[:, i, q:q + 1], accum_out=rsum[:, i, q:q + 1])
                    if L == 1:
                        ins = nc.scalar.activation(esink[:, i, :], nmax[:, i, :], ACT.Exp, bias=sinks[:, h:h + 1])
                    ins.then_inc(*exped.mark(L, h))

                def turned(h):
                    ac.wait_ge(*M.groups.at("pt", L, h))
                    if h >= 2:
                        ac.wait_ge(*M.groups.at("pv", L, h - 2))
                    nc.scalar.copy(att["pt"][:, h % 2, :], bank[6 + h % 2][:, 0:384]).then_inc(*M.free[6 + h % 2].mark("pt", L, h))

                def out(j):
                    ac.wait_ge(*M.groups.at("pv", L, 2 * j + 1))
                    nc.scalar.copy(aT[0][:, out0 + j, :], bank[2 + j % 2][:, 0:S]).then_inc(*M.act.mark("aT", L, j))
                for i in range(heads + 2):
                    if i < heads:
                        exps(i)
                    if 0 <= i - 1 < heads:
                        turned(i - 1)
                    if i >= 2 and i % 2 == 1:
                        out((i - 3) // 2)

            def root(L, which, src, scale, eps):
                ac.wait_ge(*stats.at(L, which))
                nc.scalar.activation(sd, src, ACT.Sqrt, bias=eps, scale=scale).then_inc(*rooted.mark(L, which))

            def sum_squares(L, which, src, ready):
                if M.act.n:
                    wait_self()
                for t in range(NT):
                    ac.wait_ge(*ready(t))
                    ins = nc.scalar.activation(junk[:, t, :], src[:, t, :], ACT.Square, accum_out=ss[:, t, 0:1])
                ins.then_inc(*M.act.mark("ss", L, which))
                wait_self()
                nc.scalar.activation(sd, ss[:, :, 0], ACT.Sqrt, bias=C("rms_eps"), scale=1.0 / DM) \
                    .then_inc(*rooted.mark(L, which))

            def dense_act(L):
                n = FFN_STEPS[L]
                for s in range(n):
                    b = 4 + 2 * (s % 2)
                    walk("gu", L, s, 0)
                    if L == 0:
                        ac.wait_ge(*M.groups.at("gu", L, s, 0))
                        if s >= 2:
                            ac.wait_ge(*hidden.at(L, s - 2))
                        nc.scalar.activation(ffn["sg"][:, s % 2, :, :].rearrange("p a b -> p (a b)"), bank[b][:, :], ACT.Silu) \
                            .then_inc(*M.free[b].mark("sg", L, s))
                        walk("gu", L, s, 1)
                        if s:
                            walk("dn", L, s - 1)
                        continue
                    if s >= 2:
                        ac.wait_ge(*hidden.at(L, s - 2))
                    for half, buf in enumerate((ffn["cbg"], ffn["cbv"])):
                        ac.wait_ge(*M.groups.at("gu", L, s, half))
                        for m in range(2):
                            c = half * 22 + 2 * s + m
                            ins = nc.scalar.activation(buf[:, s % 2, m, :], bank[b + half][:, m * S:(m + 1) * S], ACT.Identity,
                                                       bias=fcw[:, c, 3:4], scale=fcw[:, c, 2:3])
                        ins.then_inc(*M.act.mark("tap", L, s, half))
                    walk("gu", L, s, 1)
                    gelu(L, s)
                    if s:
                        walk("dn", L, s - 1)
                walk("dn", L, n - 1)

            def gelu(L, s):
                ac.wait_ge(*M.free[4 + 2 * (s % 2)].at("cb", L, s, 0))
                nc.scalar.activation(ffn["gg"][:, s % 2, :, :].rearrange("p a b -> p (a b)"),
                                     ffn["cbg"][:, s % 2, :, :].rearrange("p a b -> p (a b)"), ACT.Gelu_apprx_tanh) \
                    .then_inc(*M.act.mark("gelu", L, s))

            def gathered(E, tag, which):
                for g in range(2):
                    ac.wait_ge(*E.groups.at(tag, which, "ga", g))
                    nc.scalar.copy(xe[0][:, 4 * g:4 * g + 4, :], bank[2 + g][:, :].rearrange("p (c n) -> p c n", n=P)) \
                        .then_inc(*E.act.mark(tag, which, "xe", g))

            def experts(E, tag, base):
                def walk(*key):
                    ahead(E, split_hi, ac, key, base)
                if E is V:
                    for i in range(SPLIT):
                        split_hi(E, ac, i)
                    gathered(E, tag, "own")
                ac.wait_ge(*E.groups.at(tag, "tg"))
                nc.scalar.copy(moe["sgT"], bank[2][:, 0:S]).then_inc(*E.free[2].mark(tag, "sgT"))

                def silu(f):
                    b = 4 + 2 * (f % 2)
                    walk("gu", f, 0, 0)
                    ac.wait_ge(*E.groups.at(tag, "gu", f, 0))
                    if f >= 2:
                        ac.wait_ge(*E.free[b + 1].at(tag, "h", f - 2))
                    nc.scalar.activation(moe["sg"][:, f % 2, :], bank[b][:, :], ACT.Silu).then_inc(*E.free[b].mark(tag, "sg", f))
                    walk("gu", f, 0, 1)
                    walk("gu", f, 1, 0)
                    walk("gu", f, 1, 1)

                def turned(f):
                    ac.wait_ge(*E.groups.at(tag, "tr", f))
                    if f >= 2:
                        ac.wait_ge(*E.groups.at(tag, "dn", f - 2))
                    nc.scalar.copy(hTe[0][:, f % 2, :], bank[2 + f % 2][:, :]).then_inc(*E.act.mark(tag, "hTe", f))

                def down(f):
                    walk("dn", f, 0)
                    walk("dn", f, 1)
                silu(0)
                for f in range(EXP_STEPS):
                    if f + 1 < EXP_STEPS:
                        silu(f + 1)
                    turned(f)
                    if f:
                        down(f - 1)
                    if E is M and f == EXP_STEPS - 1:
                        gathered(E, tag, "next")
                down(EXP_STEPS - 1)
                ac.wait_ge(*E.groups.at(tag, "dn", EXP_STEPS - 1))
                nc.scalar.copy(moe["ye"][:, 0:512], bank[0][:, :]).then_inc(*E.free[0].mark(tag, "ye", 0))

            def delta(L):
                ac.wait_ge(*params.at("cw", L))
                nc.scalar.copy(wba_s[0][:, :, :], wba[:, :, :]).then_inc(*M.act.mark("wba", L))
                for j in range(6):
                    b = 2 * ((j // 2) % 2) + j % 2
                    if j % 2 == 0:
                        walk("in", L, j)
                    ac.wait_ge(*M.groups.at("cv", L, j))
                    for m in range(2):
                        ins = nc.scalar.activation(dn["cv"][:, 2 * j + m, :], bank[b][:, m * S:(m + 1) * S], ACT.Identity,
                                                   scale=cw[:, 2 * j + m, 3:4])
                    ins.then_inc(*M.act.mark("tap", L, j))
                    if j % 2:
                        walk("in", L, j)
                walk("in", L, 6)
                for t in range(NT):
                    ac.wait_ge(*M.groups.at("z", L, 0, t))
                    nc.scalar.copy(dn["z"][:, t, :], bank[t][:, :]).then_inc(*M.free[t].mark("z", L, 0, t))
                walk("in", L, 7)
                ac.wait_ge(*M.groups.at("ba", L))
                nc.scalar.copy(ba.rearrange("p a b -> p (a b)"), bank[2][:, 0:16]).then_inc(*M.free[2].mark("ba", L))
                for j in range(6):
                    ac.wait_ge(*M.free[2 * ((j // 2) % 2) + j % 2].at("cv", L, j))
                    v = dn["cv"][:, 2 * j:2 * j + 2, :].rearrange("p a b -> p (a b)")
                    nc.scalar.activation(v, v, ACT.Silu).then_inc(*M.act.mark("silu", L, j))
                for t in range(NT):
                    ac.wait_ge(*M.free[t].at("z", L, 0, t))
                    nc.scalar.activation(dn["z"][:, t, :], dn["z"][:, t, :], ACT.Silu).then_inc(*M.act.mark("zs", L, t))
                ac.wait_ge(*M.free[2].at("ba", L))
                nc.scalar.activation(beta, ba[:, :, 0:DN_H], ACT.Sigmoid).then_inc(*M.act.mark("beta", L))
                ac.wait_ge(*decay.at(L, "y"))
                nc.scalar.activation(sp1, sp1, ACT.Abs).then_inc(*M.act.mark())
                wait_self()
                nc.scalar.activation(sp1, sp1, ACT.Exp, scale=-1.0).then_inc(*M.act.mark())
                wait_self()
                nc.scalar.activation(sp1, sp1, ACT.Ln, bias=1.0).then_inc(*M.act.mark())
                nc.scalar.activation(gl, alog[:, L - 2:L - 1, :].to_broadcast([P, NT, DN_H]), ACT.Exp).then_inc(*M.act.mark("sp", L))
                for g in range(4):
                    if g >= 2:
                        ac.wait_ge(*M.groups.at("ssq", L, g - 2))
                    ac.wait_ge(*M.act.at("silu", L, g))
                    nc.scalar.activation(dn["sq"][:, 4 * (g % 2):4 * (g % 2) + 4, :].rearrange("p a b -> p (a b)"),
                                         dn["cv"][:, 2 * g:2 * g + 2, :].rearrange("p a b -> p (a b)"), ACT.Square) \
                        .then_inc(*squares.mark(L, g))
                for g in range(4):
                    ac.wait_ge(*M.groups.at("ssq", L, g))
                    ac.wait_ge(*M.groups.at("ssq", L, 3))
                    if g >= 2:
                        ac.wait_ge(*normed.at(L, g - 2))
                    nc.scalar.activation(dn["sq"][:, 4 * (g % 2):4 * (g % 2) + 4, :].rearrange("p a b -> p (a b)"),
                                         bank[4 + g][:, :], ACT.Sqrt, bias=C("rms_eps")) \
                        .then_inc(*M.free[4 + g].mark("len", L, g))
                ac.wait_ge(*M.groups.at("gcol", L))
                nc.scalar.activation(ngc.rearrange("p a b -> p (a b)"), bank[6][:, 0:N_DN], ACT.Copy, scale=-1.0) \
                    .then_inc(*M.free[6].mark("gcol", L))
                ac.wait_ge(*M.free[6].at("gcol", L))
                nc.scalar.activation(expg, ngc, ACT.Exp, scale=-1.0).then_inc(*M.act.mark("expg", L))
                ac.wait_ge(*decay.at(L, "last"))
                nc.scalar.activation(kdsc, kdsc, ACT.Exp).then_inc(*M.act.mark("kdsc", L))
                for t in range(NT):
                    ac.wait_ge(*M.free[t].at("grow", L, t))
                    for h in range(DN_H):
                        ins = nc.scalar.activation(dn["gam"][:, t * DN_H + h, :], dn["gam"][:, t * DN_H + h, :], ACT.Exp,
                                                   bias=ngc[:, t, h:h + 1])
                    ins.then_inc(*M.act.mark("gam", L, t))
                ac.wait_ge(*M.groups.at("u", L, 0))
                nc.scalar.copy(dn["u"][:, 0:DN_H, :].rearrange("p a b -> p (a b)"), bank[0][:, :]).then_inc(*M.free[0].mark("u", L, 0))
                ac.wait_ge(*M.groups.at("u", L, 1))
                nc.scalar.copy(dn["u"][:, DN_H:, :].rearrange("p a b -> p (a b)"), bank[1][:, :]).then_inc(*M.free[1].mark("u", L, 1))
                ac.wait_ge(*M.groups.at("wT", L))
                nc.scalar.copy(dn["wT"].rearrange("p a b -> p (a b)"), bank[2][:, :]).then_inc(*M.free[2].mark("wT", L))
                ac.wait_ge(*M.groups.at("state", L))
                nc.scalar.copy(dn["state"].rearrange("p a b -> p (a b)"), bank[3][:, :]).then_inc(*M.free[3].mark("state", L))
                for t in range(NT):
                    ac.wait_ge(*(M.free[4].at("o0", L) if t == 0 else M.free[7].at("o1", L)))
                    for h in range(DN_H):
                        ins = nc.scalar.activation(dn["AT"][:, t * DN_H + h, :], dn["o"][:, t * DN_H + h, :], ACT.Square, accum_out=ss[:, t, h:h + 1])
                ins.then_inc(*M.act.mark("oss", L))
                wait_self()
                nc.scalar.activation(rn8, ss, ACT.Sqrt, bias=C("rms_eps"), scale=1.0 / P).then_inc(*M.act.mark("ort", L))
                for t in range(NT):
                    ac.wait_ge(*M.groups.at("oT", L, t))
                    nc.scalar.copy(aT[0][:, 0:4, t * P:(t + 1) * P], bank[t][:, :].rearrange("p (c n) -> p c n", n=P)) \
                        .then_inc(*M.act.mark("oT", L, t))

            M.ev.seen = V.ev.seen = 0
            ac.wait_ge(*consts.at())
            ac.wait_ge(*angles.at("sin"))
            nc.scalar.activation(sin1, red, ACT.Sin).then_inc(*angles_done.mark("sin"))
            ac.wait_ge(*angles.at("cos"))
            nc.scalar.activation(cos1, ang, ACT.Sin).then_inc(*angles_done.mark("cos"))
            ac.wait_ge(*params.at("sinks"))
            ac.wait_ge(*params.at("xT"))
            nc.scalar.copy(xT[0][:, :, :], Rf.rearrange("p (c n) -> p c n", n=S)).then_inc(*M.act.mark("xT", "first"))
            nc.scalar.copy(wr_s[0][:, :, :], wr[:, :, :]).then_inc(*M.act.mark("wr"))
            for i in range(SPLIT):
                split_hi(M, ac, i)
            for L in range(2):
                if L:
                    copy_T((L, "in"), L)
                qkv_out("qkv", L, 2)
                copy_qkT(L, 8)
                attention(L, NHEAD, 0)
                for i in range(4):
                    walk("wo", L, i)
                root(L, "mix", mv[:, :, 1], 1.0, C("ln_eps"))
                copy_T((L, "mix"), L)
                if L == 0:
                    dense_act(0)
                else:
                    ac.wait_ge(*decided.at("m"))
                    nc.scalar.activation(w2, w2, ACT.Exp).then_inc(*M.act.mark("w2"))
                    ac.wait_ge(*flag_done.at())
                    r = ac.value_load(flag_i[0:1, 0:1], min_val=0, max_val=1)
                    with ac.If(r > 0):
                        with ac.Fori(0, NE) as e:
                            with V.ev.loop(e):
                                experts(V, "ovf", 0)
                        ac.wait_ge(*overflow_done())
                    for i in range(SPLIT):
                        split_hi(M, ac, expert_base + i)
                    gathered(M, "moe", "first")
                    with ac.Fori(0, NE) as e:
                        with ev.loop(e):
                            experts(M, "moe", expert_base)
                root(L, "ffn", mv[:, :, 1], 1.0, C("ln_eps"))
                copy_T((L, "ffn"), L)
                for nb in range(2):
                    walk("pg", L, 2 * nb)
                    for t in range(NT):
                        b = (2 * nb + t) % 4
                        ac.wait_ge(*M.groups.at("pg", L, nb, t))
                        nc.scalar.activation(att["sg"][:, 2 * nb + t, :], bank[b][:, :], ACT.Sigmoid).then_inc(*M.free[b].mark("pg", L, nb, t))
                    walk("pg", L, 2 * nb + 1)
            for L in range(2, 4):
                sum_squares(L, "in", X, lambda t: x_ready.at(*((1, "ple", t) if L == 2 else (2, "ffn", t))))
                copy_T((L, "in"), L)
                delta(L)
                qkv_out("bqkv", L, 1)
                copy_qkT(L, 4)
                attention(L, 8, 4)
                for nb in range(2):
                    walk("wo", L, 2 * nb)
                    for t in range(NT):
                        b = (2 * nb + t) % 4
                        ac.wait_ge(*M.groups.at("wo", L, nb, t))
                        nc.scalar.copy(R[:, t, nb * 512:(nb + 1) * 512], bank[b][:, :]).then_inc(*M.free[b].mark("wo", L, nb, t))
                    walk("wo", L, 2 * nb + 1)
                sum_squares(L, "mix", R, lambda t: M.free[(2 + t) % 4].at("wo", L, 1, t))
                sum_squares(L, "pre", X, lambda t: x_ready.at(L, "mix", t))
                copy_T((L, "mix"), L)
                dense_act(L)
                for t in range(NT):
                    for nb in range(2):
                        b = 2 * t + nb
                        ac.wait_ge(*M.groups.at("down", L, FFN_STEPS[L] - 1))
                        nc.scalar.copy(R[:, t, nb * 512:(nb + 1) * 512], bank[b][:, :]).then_inc(*M.free[b].mark("y", L, t, nb))
                sum_squares(L, "ffn", R, lambda t: M.free[2 * t + 1].at("y", L, t, 1))

        @block.vector
        def _(ve):
            V_ = nc.vector

            def sync(E=M):
                ve.wait_ge(*E.dve.last())

            def step(ins, E=M, *key):
                ins.then_inc(*E.dve.mark(*key))

            def chain(ins, E=M, *key):
                step(ins, E, *key)
                sync(E)

            def walk(*key):
                ahead(M, split_lo, ve, key)

            def rest_T(stage, L):
                for t in range(NT):
                    for g in range(2):
                        ve.wait_ge(*M.groups.at("tx", stage, t, g))
                        ve.wait_ge(*M.act.at("xT", stage, t, g))
                        cols = slice(t * P, (t + 1) * P)
                        hi = xT[0][:, 4 * g:4 * g + 4, cols].bitcast(F32)
                        dst = xT[1][:, 4 * g:4 * g + 4, cols]
                        if L < 2:
                            V_.tensor_tensor(dst, bank[2 * t + g][:, :].rearrange("p (c n) -> p c n", n=P), hi, ALU.subtract) \
                                .then_inc(*M.free[2 * t + g].mark("xT", stage, t, g))
                        else:
                            V_.tensor_tensor(dst, turned_in[:, 2 * t + g, :, :], hi, ALU.subtract) \
                                .then_inc(*xs_ready.mark(stage, t, g))

            def vec_row(v):
                s = v % VSLOTS
                ve.wait_ge(vecs[s].sem, 16 * (v // VSLOTS + 1))
                return vec[:, s, :]

            def rope(L, heads, cos, sin):
                for t in range(NT):
                    for nb in range(3):
                        ve.wait_ge(*M.free[(2 * nb + t) % 4].at("qkv" if L < 2 else "bqkv", L, nb, t))
                    q = att["qn"][:, t, 0:heads * DH].rearrange("p (h d) -> p h d", d=DH)
                    x1, x2 = q[:, :, 0:8], q[:, :, 8:16]
                    c = cos[:, t, :].unsqueeze(1).to_broadcast([P, heads, 8])
                    s = sin[:, t, :].unsqueeze(1).to_broadcast([P, heads, 8])
                    tm = [att["tmp"][:, i, 0:heads, :] for i in range(4)]
                    step(V_.tensor_tensor(tm[0], x1, c, ALU.mult))
                    step(V_.tensor_tensor(tm[1], x2, s, ALU.mult))
                    step(V_.tensor_tensor(tm[2], x2, c, ALU.mult))
                    chain(V_.tensor_tensor(tm[3], x1, s, ALU.mult))
                    step(V_.tensor_tensor(x1, tm[0], tm[1], ALU.subtract))
                    last = V_.tensor_tensor(x2, tm[2], tm[3], ALU.add)
                    if L < 2:
                        chain(last)
                        k = att["qn"][:, t, 1024:1280].rearrange("p (h d) -> p h d", d=DH)
                        V_.tensor_copy(att["kd"][:, t, :, 0, :], k)
                        last = V_.tensor_copy(att["kd"][:, t, :, 1, :], k)
                    last.then_inc(*roped.mark(L, t))
                    ve.wait_ge(*roped.at(L, t))

            def attention(L, heads, out0):
                ve.wait_ge(mask_in.sem, 16 * (L + 1 if L < 2 else 2 * L))

                def scores(h):
                    i, b = h % 2, 4 + h % 2
                    ve.wait_ge(*M.groups.at("sc", L, h))
                    if h >= 2:
                        ve.wait_ge(*exped.at(L, h - 2))
                    V_.tensor_tensor(att["s"][:, i, :], bank[b][:, 0:384], msk[:, 0:384], ALU.add).then_inc(*M.free[b].mark("sc", L, h))
                    ve.wait_ge(*M.free[b].at("sc", L, h))
                    for q, (a, c) in enumerate(((0, P), (P, 3 * P))):
                        ins = V_.tensor_reduce(nmax[:, i, q:q + 1], att["s"][:, i, a:c], AXX, ALU.max, negate=True)
                    if L == 1:
                        chain(ins)
                        ins = V_.tensor_scalar(nmax[:, i, :], nmax[:, i, :], nsink[:, h:h + 1], None, ALU.min)
                    ins.then_inc(*maxed.mark(L, h))

                def normalise(h):
                    i = h % 2
                    ve.wait_ge(*exped.at(L, h))
                    if L == 1:
                        chain(V_.tensor_tensor(rsum[:, i, :], rsum[:, i, :], esink[:, i, :], ALU.add))
                    chain(V_.reciprocal(rden[:, i, :], rsum[:, i, :]))
                    for q, (a, c) in enumerate(((0, P), (P, 3 * P))):
                        ins = V_.tensor_scalar(att["pr"][:, i, a:c], att["pr"][:, i, a:c], rden[:, i, q:q + 1], None, ALU.mult)
                    ins.then_inc(*probs.mark(L, h))

                def rest(j):
                    ve.wait_ge(*M.groups.at("pv", L, 2 * j + 1))
                    ve.wait_ge(*M.act.at("aT", L, j))
                    V_.tensor_tensor(aT[1][:, out0 + j, :], bank[2 + j % 2][:, 0:S], aT[0][:, out0 + j, :].bitcast(F32), ALU.subtract) \
                        .then_inc(*M.free[2 + j % 2].mark("pv", L, j))
                for i in range(heads + 2):
                    if i < heads:
                        scores(i)
                    if 1 <= i <= heads:
                        normalise(i - 1)
                    if i >= 2 and i % 2:
                        rest((i - 3) // 2)

            def layer_norm(L, which, v, take):
                for t in range(NT):
                    take(t)
                sync()
                for t in range(NT):
                    for i in range(2):
                        step(V_.bn_stats(st6[:, t, i, :], R[:, t, i * 512:(i + 1) * 512]))
                sync()
                for t in range(NT):
                    ins = V_.bn_aggr(mv[:, t, :], st6[:, t, :, :].rearrange("p a b -> p (a b)"))
                    if t == 0:
                        step(ins)
                ins.then_inc(*stats.mark(L, which))
                ve.wait_ge(*rooted.at(L, which))
                chain(V_.reciprocal(rstd, sd))
                g, b = vec_row(v), vec_row(v + 1)
                for t in range(NT):
                    step(V_.tensor_scalar(R[:, t, :], R[:, t, :], mv[:, t, 0:1], rstd[:, t:t + 1], ALU.subtract, ALU.mult))
                sync()
                for t in range(NT):
                    ins = V_.tensor_tensor(R[:, t, :], R[:, t, :], g, ALU.mult)
                    if t == 0:
                        step(ins)
                ins.then_inc(*vec_used.mark(v))
                ve.wait_ge(*vec_used.at(v))
                sync()
                for t in range(NT):
                    V_.tensor_tensor(X[:, t, :], R[:, t, :], b, ALU.add).then_inc(*x_ready.mark(L, which, t))

            def post_norm(L, which, v):
                ve.wait_ge(*rooted.at(L, which))
                chain(V_.reciprocal(rstd, sd))
                w = vec_row(v)
                for t in range(NT):
                    ins = V_.scalar_tensor_tensor(R[:, t, :], R[:, t, :], rstd[:, t:t + 1], w, ALU.mult, ALU.mult)
                    if t == 0:
                        step(ins)
                ins.then_inc(*vec_used.mark(v))
                ve.wait_ge(*vec_used.at(v))
                sync()
                for t in range(NT):
                    V_.tensor_tensor(X[:, t, :], X[:, t, :], R[:, t, :], ALU.add).then_inc(*x_ready.mark(L, which, t))

            def pre_norm(L, which, rt):
                ve.wait_ge(*rooted.at(L, rt))
                ve.wait_ge(*x_ready.at(*((L, "mix", 1) if which == "mix" else (1, "ple", 1) if L == 2 else (2, "ffn", 1))))
                chain(V_.reciprocal(rstd, sd))
                for t in range(NT):
                    V_.tensor_scalar(R[:, t, :], X[:, t, :], rstd[:, t:t + 1], None, ALU.mult).then_inc(*prenorm.mark(L, which, t))
                w = prew[:, 0 if which == "in" else 1, :]
                ve.wait_ge(*params.at("prew", L))
                for t in range(NT):
                    for g in range(2):
                        ve.wait_ge(*M.groups.at("tx", (L, which), t, g))
                        V_.tensor_tensor(turned_in[:, 2 * t + g, :, :],
                                         bank[2 * t + g][:, :].rearrange("p (c n) -> p c n", n=P),
                                         w[:, 4 * g:4 * g + 4].unsqueeze(2).to_broadcast([P, 4, P]), ALU.mult) \
                            .then_inc(*M.free[2 * t + g].mark("xT", (L, which), t, g))
                rest_T((L, which), L)

            def dense_dve(L):
                n = FFN_STEPS[L]
                for s in range(n):
                    b = 4 + 2 * (s % 2)
                    walk("gu", L, s, 0)
                    if L == 0:
                        ve.wait_ge(*M.free[b].at("sg", L, s))
                        ve.wait_ge(*M.groups.at("gu", L, s, 1))
                        V_.tensor_tensor(ffn["h"][:, s % 2, :, :].rearrange("p a b -> p (a b)"),
                                         ffn["sg"][:, s % 2, :, :].rearrange("p a b -> p (a b)"), bank[b + 1][:, :], ALU.mult) \
                            .then_inc(*M.free[b + 1].mark("h", L, s))
                        walk("gu", L, s, 1)
                        ve.wait_ge(*M.free[b + 1].at("h", L, s))
                        split_hidden(L, s)
                        if s:
                            walk("dn", L, s - 1)
                        continue
                    for half, buf in enumerate((ffn["cbg"], ffn["cbv"])):
                        ve.wait_ge(*M.groups.at("gu", L, s, half))
                        ve.wait_ge(*M.act.at("tap", L, s, half))
                        o = bank[b + half]
                        for m in range(2):
                            c = half * 22 + 2 * s + m
                            step(V_.scalar_tensor_tensor(buf[:, s % 2, m, 1:S], o[:, m * S:m * S + S - 1], fcw[:, c, 1:2],
                                                         buf[:, s % 2, m, 1:S], ALU.mult, ALU.add))
                        sync()
                        for m in range(2):
                            c = half * 22 + 2 * s + m
                            ins = V_.scalar_tensor_tensor(buf[:, s % 2, m, 2:S], o[:, m * S:m * S + S - 2], fcw[:, c, 0:1],
                                                          buf[:, s % 2, m, 2:S], ALU.mult, ALU.add)
                        ins.then_inc(*M.free[b + half].mark("cb", L, s, half))
                    walk("gu", L, s, 1)
                    gated_mul(L, s)
                    if s:
                        walk("dn", L, s - 1)
                walk("dn", L, n - 1)

            def gated_mul(L, s):
                ve.wait_ge(*M.act.at("gelu", L, s))
                ve.wait_ge(*M.free[5 + 2 * (s % 2)].at("cb", L, s, 1))
                chain(V_.tensor_tensor(ffn["h"][:, s % 2, :, :], ffn["gg"][:, s % 2, :, :], ffn["cbv"][:, s % 2, :, :], ALU.mult))
                split_hidden(L, s)

            def split_hidden(L, s):
                if s >= 2:
                    ve.wait_ge(*M.groups.at("down", L, s - 2))
                h = ffn["h"][:, s % 2, :, :]
                chain(V_.tensor_copy(hT[0][:, s % 2, :, :], h))
                V_.tensor_tensor(hT[1][:, s % 2, :, :], h, hT[0][:, s % 2, :, :].bitcast(F32), ALU.subtract) \
                    .then_inc(*hidden.mark(L, s))

            def route():
                for t in range(NT):
                    ve.wait_ge(*M.groups.at("router", t))
                    V_.tensor_copy(lg[:, t, :], bank[t][:, 0:NE]).then_inc(*M.free[t].mark("router", t))
                    ve.wait_ge(*M.free[t].at("router", t))
                rank = C("rank").unsqueeze(1).to_broadcast([P, NT, NE])

                def pick(src, top, hot):
                    chain(V_.tensor_reduce(top, src, AXX, ALU.max))
                    chain(V_.tensor_tensor(sc8, src, top.unsqueeze(2).to_broadcast([P, NT, NE]), ALU.is_equal))
                    chain(V_.tensor_tensor(sc8, sc8, rank, ALU.mult))
                    chain(V_.tensor_reduce(w1, sc8, AXX, ALU.max))
                    chain(V_.tensor_tensor(hot, sc8, w1.unsqueeze(2).to_broadcast([P, NT, NE]), ALU.is_equal))
                pick(lg, m1, oh1)
                chain(V_.scalar_tensor_tensor(lg2.rearrange("p a b -> p (a b)"), oh1.rearrange("p a b -> p (a b)"), -3.0e38,
                                              lg.rearrange("p a b -> p (a b)"), ALU.mult, ALU.add))
                pick(lg2, m2, oh2)
                V_.tensor_tensor(memb, oh1, oh2, ALU.add).then_inc(*member.mark())
                V_.tensor_tensor(w2, m2, m1, ALU.subtract).then_inc(*decided.mark("m"))
                ve.wait_ge(*M.act.at("w2"))
                chain(V_.tensor_scalar(w1, w2, 1.0, None, ALU.add))
                chain(V_.reciprocal(w1, w1))
                chain(V_.tensor_tensor(w2, w2, w1, ALU.mult))
                chain(V_.tensor_tensor(gates, oh1, w1.unsqueeze(2).to_broadcast([P, NT, NE]), ALU.mult))
                chain(V_.tensor_tensor(sc8, oh2, w2.unsqueeze(2).to_broadcast([P, NT, NE]), ALU.mult))
                chain(V_.tensor_tensor(gates, gates, sc8, ALU.add))
                ve.wait_ge(*M.groups.at("ranks"))
                r = bank[2][:, 0:2 * NE].rearrange("p (a b) -> p a b", b=NE)
                chain(V_.memset(posx, 0.0))
                chain(V_.scalar_tensor_tensor(posx[:, :, 0:NE], r, 1.0, memb, ALU.add, ALU.mult))
                chain(V_.tensor_scalar(posx, posx, -1.0, None, ALU.add))
                V_.tensor_reduce(flag_f, bank[2][:, 2 * NE:3 * NE], AXX, ALU.max).then_inc(*M.free[2].mark("ranks"))
                ve.wait_ge(*M.free[2].at("ranks"))
                chain(V_.tensor_scalar(flag_f, flag_f, float(P) + 0.5, None, ALU.is_gt))
                V_.tensor_copy(flag_i[:, :], flag_f).then_inc(*flag_done.mark())
                ve.wait_ge(*flag_done.at())
                for t in range(NT):
                    step(V_.tensor_scalar(R[:, t, :], X[:, t, :], ALPHA, None, ALU.mult))
                sync()

            def select(E, tag, which, e, tile):
                chain(V_.tensor_copy(pcol, posx[:, :, e]), E)
                for t in range(NT):
                    step(V_.tensor_scalar(moe["sel"][:, t, :], C("iota", tile * P, (tile + 1) * P), pcol[:, t:t + 1], None,
                                          ALU.is_equal), E, tag, which, "sel")

            def rest_x(E, tag, which):
                for g in range(2):
                    ve.wait_ge(*E.groups.at(tag, which, "ga", g))
                    ve.wait_ge(*E.act.at(tag, which, "xe", g))
                    V_.tensor_tensor(xe[1][:, 4 * g:4 * g + 4, :], bank[2 + g][:, :].rearrange("p (c n) -> p c n", n=P),
                                     xe[0][:, 4 * g:4 * g + 4, :].bitcast(F32), ALU.subtract) \
                        .then_inc(*E.free[2 + g].mark(tag, which, "xe", g))

            def experts(E, tag, base, e, tile):
                def walk(*key):
                    ahead(E, split_lo, ve, key, base)
                if E is V:
                    select(E, tag, "own", e, tile)
                    for i in range(SPLIT):
                        split_lo(E, ve, i)
                    rest_x(E, tag, "own")
                step(V_.tensor_copy(pcol2, posx[:, :, e]), E)
                chain(V_.tensor_copy(gcol, gates[:, :, e]), E)
                for t in range(NT):
                    step(V_.tensor_scalar(moe["selg"][:, t, :], C("iota", tile * P, (tile + 1) * P), pcol2[:, t:t + 1],
                                          gcol[:, t:t + 1], ALU.is_equal, ALU.mult), E, tag, "selg")

                def hidden_of(f):
                    b = 4 + 2 * (f % 2)
                    for half in range(2):
                        walk("gu", f, half, 0)
                        if half == 0:
                            walk("gu", f, 0, 1)
                    ve.wait_ge(*E.free[b].at(tag, "sg", f))
                    ve.wait_ge(*E.groups.at(tag, "gu", f, 1))
                    if f >= 2:
                        ve.wait_ge(*E.groups.at(tag, "tr", f - 2))
                    V_.tensor_tensor(moe["h"][:, f % 2, :], moe["sg"][:, f % 2, :], bank[b + 1][:, :], ALU.mult) \
                        .then_inc(*E.free[b + 1].mark(tag, "h", f))
                    walk("gu", f, 1, 1)

                def rest_h(f):
                    ve.wait_ge(*E.groups.at(tag, "tr", f))
                    ve.wait_ge(*E.act.at(tag, "hTe", f))
                    V_.tensor_tensor(hTe[1][:, f % 2, :], bank[2 + f % 2][:, :], hTe[0][:, f % 2, :].bitcast(F32), ALU.subtract) \
                        .then_inc(*E.free[2 + f % 2].mark(tag, "hTe", f))
                hidden_of(0)
                for f in range(EXP_STEPS):
                    if f + 1 < EXP_STEPS:
                        hidden_of(f + 1)
                    if E is M and f == 1:
                        select(E, tag, "next", e + 1, tile)
                    rest_h(f)
                    if f:
                        walk("dn", f - 1, 0)
                        walk("dn", f - 1, 1)
                    if E is M and f == EXP_STEPS - 1:
                        rest_x(E, tag, "next")
                walk("dn", EXP_STEPS - 1, 0)
                walk("dn", EXP_STEPS - 1, 1)
                ve.wait_ge(*E.groups.at(tag, "dn", EXP_STEPS - 1))
                V_.tensor_copy(moe["ye"][:, 512:1024], bank[1][:, :]).then_inc(*E.free[1].mark(tag, "ye", 1))
                for t in range(NT):
                    for nb in range(2):
                        ve.wait_ge(*E.groups.at(tag, "sc", t, nb))
                        r = R[:, t, nb * 512:(nb + 1) * 512]
                        V_.tensor_tensor(r, r, bank[2 + nb][:, :], ALU.add).then_inc(*E.free[2 + nb].mark(tag, "sc", t, nb))
                for nb in range(2):
                    ve.wait_ge(*E.free[2 + nb].at(tag, "sc", 1, nb))

            def delta(L):
                ve.wait_ge(*M.act.at("wba", L))
                V_.tensor_tensor(wba_s[1][:, :, :], wba[:, :, :], wba_s[0][:, :, :].bitcast(F32), ALU.subtract) \
                    .then_inc(*wsmall.mark("wba", L))
                for j in range(6):
                    b = 2 * ((j // 2) % 2) + j % 2
                    if j % 2 == 0:
                        walk("in", L, j)
                    ve.wait_ge(*M.groups.at("cv", L, j))
                    ve.wait_ge(*M.act.at("tap", L, j))
                    for tap in (2, 1, 0):
                        d = 3 - tap
                        for m in range(2):
                            c = 2 * j + m
                            ins = V_.scalar_tensor_tensor(dn["cv"][:, c, d:S], bank[b][:, m * S:m * S + S - d], cw[:, c, tap:tap + 1],
                                                          dn["cv"][:, c, d:S], ALU.mult, ALU.add)
                            if tap or not m:
                                step(ins)
                        if tap:
                            sync()
                    ins.then_inc(*M.free[b].mark("cv", L, j))
                    if j % 2:
                        walk("in", L, j)
                walk("in", L, 6)
                walk("in", L, 7)
                ve.wait_ge(*M.free[2].at("ba", L))
                chain(V_.tensor_tensor(sp1, ba[:, :, DN_H:8], dtb[:, L - 2:L - 1, :].to_broadcast([P, NT, DN_H]), ALU.add))
                V_.tensor_scalar(sp2, sp1, 0.0, None, ALU.max).then_inc(*decay.mark(L, "y"))
                ve.wait_ge(*M.act.at("sp", L))
                ve.wait_ge(*decay.at(L, "y"))
                chain(V_.tensor_tensor(sp2, sp2, sp1, ALU.add))
                V_.scalar_tensor_tensor(gl.rearrange("p a b -> p (a b)"), sp2.rearrange("p a b -> p (a b)"), -1.0,
                                        gl.rearrange("p a b -> p (a b)"), ALU.mult, ALU.mult).then_inc(*decay.mark(L, "g"))
                ve.wait_ge(*decay.at(L, "g"))
                ve.wait_ge(*M.act.at("beta", L))
                step(V_.tensor_copy(dn["gB"], gl.rearrange("p a b -> p (a b)").unsqueeze(2).to_broadcast([P, N_DN, P])))
                V_.tensor_copy(dn["bB"], beta.rearrange("p a b -> p (a b)").unsqueeze(2).to_broadcast([P, N_DN, P])) \
                    .then_inc(*decay.mark(L, "rows"))
                for g in range(4):
                    ve.wait_ge(*M.free[4 + g].at("len", L, g))
                    v = dn["cv"][:, 2 * g:2 * g + 2, :].rearrange("p a b -> p (a b)")
                    ln = dn["sq"][:, 4 * (g % 2):4 * (g % 2) + 4, :].rearrange("p a b -> p (a b)")
                    chain(V_.reciprocal(ln, ln))
                    V_.scalar_tensor_tensor(v, v, (float(P) ** -0.5 if g < 2 else 1.0), ln, ALU.mult, ALU.mult) \
                        .then_inc(*normed.mark(L, g))
                ve.wait_ge(*normed.at(L, 3))
                ve.wait_ge(*M.free[6].at("gcol", L))
                ve.wait_ge(mask_in.sem, 16 * (2 * L - 1))
                for t in range(NT):
                    ve.wait_ge(*M.groups.at("grow", L, t))
                    gr = bank[t][:, :].rearrange("p (h n) -> p h n", n=P)
                    if t == 0:
                        V_.tensor_tensor(kdsc, gr[:, :, P - 1], ngc[:, 0, :], ALU.add).then_inc(*decay.mark(L, "last"))
                    V_.tensor_tensor(dn["gam"][:, t * DN_H:(t + 1) * DN_H, :], gr,
                                     msk[:, LEVELS * P:(LEVELS + 1) * P].unsqueeze(1).to_broadcast([P, DN_H, P]), ALU.add) \
                        .then_inc(*M.free[t].mark("grow", L, t))
                for t in range(NT):
                    ve.wait_ge(*M.groups.at("brow", L, t))
                    V_.tensor_tensor(dn["kb"][:, :, t * P:(t + 1) * P], dn["cv"][:, DN_H:2 * DN_H, t * P:(t + 1) * P],
                                     bank[2 + t][:, :].rearrange("p (h n) -> p h n", n=P), ALU.mult) \
                        .then_inc(*M.free[2 + t].mark("brow", L, t))
                ve.wait_ge(*M.act.at("kdsc", L))
                chain(V_.tensor_tensor(bexp, beta[:, 1, :], expg[:, 1, :], ALU.mult))
                for t in range(NT):
                    ve.wait_ge(*M.groups.at("kn", L, t))
                    for h in range(DN_H):
                        dst, sc = (dn["kdec"], kdsc) if t == 0 else (dn["kbg"], bexp)
                        ins = V_.tensor_scalar(dst[:, h, :], bank[4 + t][:, h * P:(h + 1) * P], sc[:, h:h + 1], None, ALU.mult)
                    ins.then_inc(*M.free[4 + t].mark("kn", L, t))
                for t in range(NT):
                    ve.wait_ge(*M.groups.at("vn", L, t))
                    for h in range(DN_H):
                        ins = V_.tensor_scalar(dn["vb"][:, t * DN_H + h, :], bank[6 + t][:, h * P:(h + 1) * P],
                                               beta[:, t, h:h + 1], None, ALU.mult)
                    ins.then_inc(*M.free[6 + t].mark("vn", L, t))
                for name, b0, dst in (("kk", 0, dn["AT"]), ("kq", 2, dn["qk"])):
                    for t in range(NT):
                        ve.wait_ge(*M.groups.at(name, L, t))
                        ve.wait_ge(*M.act.at("gam", L, t))
                        V_.tensor_tensor(dst[:, t * DN_H:(t + 1) * DN_H, :], bank[b0 + t][:, :].rearrange("p (h n) -> p h n", n=P),
                                         dn["gam"][:, t * DN_H:(t + 1) * DN_H, :], ALU.mult).then_inc(*M.free[b0 + t].mark(name, L, t))
                ve.wait_ge(*M.free[1].at("kk", L, 1))
                for n in range(LEVELS):
                    half = [slice(t * DN_H, (t + 1) * DN_H) for t in range(NT)]
                    for t in range(NT):
                        V_.tensor_tensor(dn["LT"][:, half[t], :], dn["AT"][:, half[t], :],
                                         msk[:, n * P:(n + 1) * P].unsqueeze(1).to_broadcast([P, DN_H, P]), ALU.mult).then_inc(*inverse.mark(L, n, "LT", t))
                        ve.wait_ge(*inverse.at(L, n, "LT", t))
                    for t in range(NT):
                        ve.wait_ge(*M.groups.at("lv", L, n, "X", t))
                        px = bank[t][:, :].rearrange("p (h n) -> p h n", n=P)
                        idb = ident.unsqueeze(1).to_broadcast([P, DN_H, P])
                        if n == 0:
                            step(V_.tensor_tensor(dn["DT"][:, half[t], :], idb, dn["LT"][:, half[t], :], ALU.subtract))
                            V_.tensor_tensor(dn["D"][:, half[t], :], idb, px, ALU.subtract).then_inc(*M.free[t].mark("lv", L, n, "X", t))
                            ve.wait_ge(*M.free[t].at("lv", L, n, "X", t))
                            sync()
                        else:
                            V_.tensor_copy(dn["Xl"][:, half[t], :], px).then_inc(*M.free[t].mark("lv", L, n, "X", t))
                    if n == 0:
                        continue
                    for t in range(NT):
                        for which, b, dst in (("D", 2 + t, dn["D"]), ("DT", 4 + t, dn["DT"])):
                            if which == "D" and n == LEVELS - 1:
                                continue
                            ve.wait_ge(*M.groups.at("lv", L, n, "DT", t))
                            V_.tensor_tensor(dst[:, half[t], :], dst[:, half[t], :], bank[b][:, :].rearrange("p (h n) -> p h n", n=P),
                                             ALU.subtract).then_inc(*M.free[b].mark("lv", L, n, which, t))
                            ve.wait_ge(*M.free[b].at("lv", L, n, which, t))
                ve.wait_ge(*M.groups.at("o0", L))
                V_.tensor_copy(dn["o"][:, 0:DN_H, :].rearrange("p a b -> p (a b)"), bank[4][:, :]).then_inc(*M.free[4].mark("o0", L))
                ve.wait_ge(*M.groups.at("ws", L))
                ve.wait_ge(*M.free[1].at("u", L, 1))
                V_.tensor_tensor(dn["vn"].rearrange("p a b -> p (a b)"), dn["u"][:, DN_H:, :].rearrange("p a b -> p (a b)"),
                                 bank[5][:, :], ALU.subtract).then_inc(*M.free[5].mark("ws", L))
                ve.wait_ge(*M.groups.at("qs", L))
                for h in range(DN_H):
                    ins = V_.tensor_scalar(dn["o"][:, DN_H + h, :], bank[6][:, h * P:(h + 1) * P], expg[:, 1, h:h + 1], None, ALU.mult)
                ins.then_inc(*M.free[6].mark("qs", L))
                ve.wait_ge(*M.free[6].at("qs", L))
                ve.wait_ge(*M.groups.at("o1", L))
                o1 = dn["o"][:, DN_H:, :].rearrange("p a b -> p (a b)")
                V_.tensor_tensor(o1, o1, bank[7][:, :], ALU.add).then_inc(*M.free[7].mark("o1", L))
                ve.wait_ge(*M.act.at("ort", L))
                chain(V_.reciprocal(rn8, rn8))
                ve.wait_ge(*params.at("onorm", L))
                for t in range(NT):
                    for h in range(DN_H):
                        o = dn["o"][:, t * DN_H + h, :]
                        step(V_.scalar_tensor_tensor(o, o, rn8[:, t, h:h + 1], onorm[:, :], ALU.mult, ALU.mult))
                sync()
                for t in range(NT):
                    ve.wait_ge(*M.act.at("zs", L, t))
                    o = dn["o"][:, t * DN_H:(t + 1) * DN_H, :].rearrange("p a b -> p (a b)")
                    V_.tensor_tensor(o, o, dn["z"][:, t, :], ALU.mult).then_inc(*gated.mark(L, t))
                for t in range(NT):
                    ve.wait_ge(*M.groups.at("oT", L, t))
                    ve.wait_ge(*M.act.at("oT", L, t))
                    V_.tensor_tensor(aT[1][:, 0:4, t * P:(t + 1) * P], bank[t][:, :].rearrange("p (c n) -> p c n", n=P),
                                     aT[0][:, 0:4, t * P:(t + 1) * P].bitcast(F32), ALU.subtract) \
                        .then_inc(*M.free[t].mark("oT", L, t))

            M.ev.seen = V.ev.seen = 0
            ve.wait_ge(*consts.at())
            ve.wait_ge(*params.at("pos"))
            chain(V_.tensor_copy(pos_f, pos_i[:, :]))
            for t in range(NT):
                step(V_.tensor_scalar(ang[:, t, :], C("inv"), pos_f[:, t:t + 1], None, ALU.mult))
            sync()
            chain(V_.tensor_scalar(rnd, ang, float(1.0 / (2 * np.pi)), MAGIC, ALU.mult, ALU.add))
            chain(V_.tensor_scalar(rnd, rnd, -MAGIC, None, ALU.add))
            c1 = 6.28125
            c2 = float(np.float32(np.round((2 * np.pi - c1) * 2 ** 20) / 2 ** 20))
            c3 = float(2 * np.pi - c1 - c2)

            def flat(a):
                return a.rearrange("p a b -> p (a b)")
            for c in (c1, c2, c3):
                chain(V_.scalar_tensor_tensor(flat(ang), flat(rnd), -c, flat(ang), ALU.mult, ALU.add))
            PI = 3.1415925
            V_.tensor_scalar(red, ang, PI, -PI, ALU.min, ALU.max).then_inc(*angles.mark("sin"))
            chain(V_.tensor_scalar(ang, ang, float(np.pi / 2), None, ALU.add))
            chain(V_.tensor_scalar(rnd, ang, float(np.pi), float(2 * np.pi), ALU.is_gt, ALU.mult))
            chain(V_.tensor_tensor(ang, ang, rnd, ALU.subtract))
            V_.tensor_scalar(ang, ang, PI, -PI, ALU.min, ALU.max).then_inc(*angles.mark("cos"))
            ve.wait_ge(*params.at("sinks"))
            chain(V_.tensor_scalar(nsink, sinks, -1.0, None, ALU.mult))
            ve.wait_ge(*angles_done.at("cos"))
            ve.wait_ge(*M.act.at("xT", "first"))
            V_.tensor_tensor(xT[1][:, :, :], Rf.rearrange("p (c n) -> p c n", n=S), xT[0][:, :, :].bitcast(F32), ALU.subtract) \
                .then_inc(*xs_ready.mark("first"))
            ve.wait_ge(*M.act.at("wr"))
            V_.tensor_tensor(wr_s[1][:, :, :], wr[:, :, :], wr_s[0][:, :, :].bitcast(F32), ALU.subtract).then_inc(*wsmall.mark("wr"))
            for i in range(SPLIT):
                split_lo(M, ve, i)
            for L in range(2):
                if L:
                    rest_T((L, "in"), L)
                for i in range(6):
                    walk("qkv", L, i)
                rope(L, 20, cos1, sin1)
                attention(L, NHEAD, 0)

                def take_wo(t):
                    if L == 0:
                        ve.wait_ge(*params.at("X"))
                    for nb in range(2):
                        b = (2 * nb + t) % 4
                        if t == 0:
                            walk("wo", L, 2 * nb)
                            walk("wo", L, 2 * nb + 1)
                        ve.wait_ge(*M.groups.at("wo", L, nb, t))
                        V_.scalar_tensor_tensor(R[:, t, nb * 512:(nb + 1) * 512], X[:, t, nb * 512:(nb + 1) * 512], ALPHA,
                                                bank[b][:, :], ALU.mult, ALU.add).then_inc(*M.free[b].mark("wo", L, nb, t))
                        ve.wait_ge(*M.free[b].at("wo", L, nb, t))
                layer_norm(L, "mix", 4 * L, take_wo)
                rest_T((L, "mix"), L)

                def take_y(t):
                    for nb in range(2):
                        b = 2 * t + nb
                        ve.wait_ge(*M.groups.at("down", 0, FFN_STEPS[0] - 1))
                        V_.scalar_tensor_tensor(R[:, t, nb * 512:(nb + 1) * 512], X[:, t, nb * 512:(nb + 1) * 512], ALPHA,
                                                bank[b][:, :], ALU.mult, ALU.add).then_inc(*M.free[b].mark("y", L, t, nb))
                        ve.wait_ge(*M.free[b].at("y", L, t, nb))
                if L == 0:
                    dense_dve(0)
                    layer_norm(L, "ffn", 4 * L + 2, take_y)
                else:
                    route()
                    r = ve.value_load(flag_i[0:1, 0:1], min_val=0, max_val=1)
                    with ve.If(r > 0):
                        for n, event in enumerate(V.free + [V.groups]):
                            V_.memset(tick[:, n:n + 1], 0.0).then_inc(event.sem, 1)
                        with ve.Fori(0, NE) as e:
                            with V.ev.loop(e):
                                experts(V, "ovf", 0, e, 1)
                    select(M, "moe", "first", 0, 0)
                    for i in range(SPLIT):
                        split_lo(M, ve, expert_base + i)
                    rest_x(M, "moe", "first")
                    with ve.Fori(0, NE) as e:
                        with ev.loop(e):
                            experts(M, "moe", expert_base, e, 0)
                    layer_norm(L, "ffn", 4 * L + 2, lambda t: None)
                rest_T((L, "ffn"), L)
                for i in range(4):
                    walk("pg", L, i)
                for nb in range(2):
                    for t in range(NT):
                        b = (2 * nb + t) % 4
                        ve.wait_ge(*M.free[b].at("pg", L, nb, t))
                        ve.wait_ge(*M.groups.at("pp", L, nb, t))
                        V_.tensor_tensor(att["sg"][:, 2 * nb + t, :], att["sg"][:, 2 * nb + t, :], bank[4 + 2 * nb + t][:, :], ALU.mult) \
                            .then_inc(*M.free[4 + 2 * nb + t].mark("pp", L, nb, t))
                        ve.wait_ge(*M.free[4 + 2 * nb + t].at("pp", L, nb, t))
                for t in range(NT):
                    for nb in range(2):
                        x = X[:, t, nb * 512:(nb + 1) * 512]
                        ins = V_.tensor_tensor(x, x, att["sg"][:, 2 * nb + t, :], ALU.add)
                        if nb == 0:
                            step(ins)
                    ins.then_inc(*x_ready.mark(L, "ple", t))
            for L in range(2, 4):
                pre_norm(L, "in", "in")
                delta(L)
                for i in range(8, 14):
                    walk("in", L, i)
                rope(L, 16, C("cos2").rearrange("p (a b) -> p a b", b=8), C("sin2").rearrange("p (a b) -> p a b", b=8))
                attention(L, 8, 4)
                for i in range(4):
                    walk("wo", L, i)
                post_norm(L, "mix", 4 + 2 * L)
                pre_norm(L, "mix", "pre")
                dense_dve(L)
                post_norm(L, "ffn", 5 + 2 * L)


_OUT = (S, DM)


def layout(a):
    def np32(name):
        return np.asarray(a[name])

    def natural(w):
        lead, n = w.shape[:-2], w.shape[-1] // 512
        w = w.reshape(lead + (2, 4, P, n, 512))
        k = len(lead)
        w = w.transpose(tuple(range(k)) + (k + 3, k, k + 2, k + 1, k + 4))
        return np.ascontiguousarray(w).reshape(lead + (2 * n, P, UNIT))

    def paired(g, u):
        lead, n = g.shape[:-2], g.shape[-1] // 256
        k = len(lead)
        both = np.stack([w.reshape(lead + (2, 4, P, n, 256)) for w in (g, u)], axis=-2)
        both = both.transpose(tuple(range(k)) + (k + 3, k, k + 2, k + 1, k + 4, k + 5))
        return np.ascontiguousarray(both).reshape(lead + (n, 2, P, UNIT))

    def rows(w):
        lead, n = w.shape[:-2], w.shape[-2] // 256
        k = len(lead)
        w = w.reshape(lead + (n, 2, P, DM)).transpose(tuple(range(k)) + (k, k + 2, k + 1, k + 3))
        return np.ascontiguousarray(w).reshape(lead + (n, P, UNIT))

    def per_channel(w):
        return w.reshape(2, -1, P).transpose(0, 2, 1)

    def every(v):
        return np.broadcast_to(np.asarray(v)[..., None, :], np.asarray(v).shape[:-1] + (P, np.asarray(v).shape[-1]))
    out = {}
    x = np32("x")[0]
    out["x"] = x
    out["xT"] = x.T.reshape(KC, P, S).transpose(1, 0, 2)
    out["pT"] = np32("p")[:, 0].transpose(0, 2, 1).reshape(2, 2, P, S).transpose(0, 2, 1, 3)
    out["positions"] = np32("positions")[0].reshape(NT, P).T
    out["sinks"] = every(np32("sinks")[0])
    out["alog"] = np.broadcast_to(np32("dn_a_log_2")[None], (P, 2, DN_H))
    out["dtb"] = np.broadcast_to(np32("dn_dt_bias_2")[None], (P, 2, DN_H))
    out["wr"] = np32("w_router")[0].reshape(KC, P, NE).transpose(1, 0, 2)
    rowsv = []
    for L in range(2):
        rowsv += [np32("ln_mix_g")[L], np32("ln_mix_b")[L], np32("ln_ffn_g")[L], np32("ln_ffn_b")[L]]
    for L in range(2):
        rowsv += [np32("post_mix_norm_2")[L], np32("post_ffn_norm_2")[L]]
    out["vecs"] = every(np.stack(rowsv))
    out["wu_qkv"] = natural(np32("w_qkv"))
    out["wu_o"] = natural(np32("w_o"))
    out["wu_ffn_gu"] = paired(np32("w_ffn_gate")[0], np32("w_ffn_up")[0])
    out["wu_ffn_d"] = rows(np32("w_ffn_down")[0])
    out["wu_pp"] = rows(np32("w_ple_proj"))[:, 0]
    out["wu_pg"] = natural(np32("w_ple_gate"))
    for name, src in (("wu_eg", "w_exp_gate"), ("wu_eu", "w_exp_up")):
        out[name] = natural(np32(src)[0]).reshape(NE, EXP_STEPS, 2, P, UNIT)
    out["wu_ed"] = rows(np32("w_exp_down")[0]).reshape(NE, EXP_STEPS, 2, P, UNIT)
    w_in = np32("w_in_2")
    out["wu_in"] = natural(np.concatenate([w_in[:, :, :2048], w_in[:, :, 2056:]], axis=2))
    out["wba"] = w_in[:, :, 2048:2056].reshape(2, KC, P, 8).transpose(0, 2, 1, 3)
    out["wu_out"] = natural(np32("w_out_2"))
    up = np32("ffn_up_2")
    out["wu_up"] = paired(up[:, :, :FF2], up[:, :, FF2:])
    out["wu_down"] = rows(np32("ffn_down_2"))
    out["cw"] = np32("dn_conv_2").reshape(2, 4, 12, P).transpose(0, 3, 2, 1)
    out["fcw"] = np.concatenate([np32("ffn_conv_2"), np32("ffn_conv_bias_2")[:, None]], axis=1) \
        .reshape(2, 4, 44, P).transpose(0, 3, 2, 1)
    out["prew"] = np.stack([per_channel(np32("pre_mix_norm_2")), per_channel(np32("pre_ffn_norm_2"))], axis=2)
    out["onorm"] = every(np32("dn_out_norm_2"))
    out["cst"] = constants()[0]
    out["masks"] = masks()
    return {k: np.ascontiguousarray(v) for k, v in out.items()}


def kernel(_debug=None, **inputs):
    import concourse.bacc as bacc
    from concourse.bass_utils import run_bass_kernel_spmd

    arrays = layout(inputs)
    plan = Plan()
    for _ in range(2):
        plan.opens.clear()
        nc = bacc.Bacc("TRN2", target_bir_lowering=False, num_devices=1)
        aps = {n: nc.dram_tensor(f"in_{n}", list(v.shape), mybir.dt.from_np(v.dtype), kind="ExternalInput").ap()
               for n, v in arrays.items()}
        aps["out"] = nc.dram_tensor("out_x", list(_OUT), F32, kind="ExternalOutput").ap()
        if _debug:
            aps["dbg"] = nc.dram_tensor("dbg", [len(_debug["dump"]), S, DM], F32, kind="ExternalOutput").ap()
        build_program(nc, aps, plan, _debug)
    r = run_bass_kernel_spmd(nc, [{f"in_{n}": v for n, v in arrays.items()}], core_ids=[0])
    if _debug:
        return r
    return r.results[0]["out_x"].reshape(1, S, DM)
```

```python
from contextlib import ExitStack

import numpy as np
import concourse.bass as bass
from concourse import mybir

F32R = mybir.dt.float32r
F32 = mybir.dt.float32
I32 = mybir.dt.int32
ALU = mybir.AluOpType
ACT = mybir.ActivationFunctionType
AXX = mybir.AxisListType.X

P = 128
S = 256
NT = S // P
DM = 1024
KC = DM // P
NHEAD = 16
DH = 64
FF1 = 3584
FF2 = 2816
NE = 8
UNIT = 2048
WARM_START, WARM_LN, WARM_PLE, WARM_RMS = 6, 8, 6, 10
RAW = 6
SPLIT = 3
NEG = -1.0e30
ALPHA = float((2.0 * 2) ** 0.25)
LN_EPS = 1e-5
RMS_EPS = 1e-6
DN_H = 4
N_DN = DN_H * NT
LEVELS = 7
MAGIC = 12582912.0
VSLOTS = 2

FFN_STEPS = {0: FF1 // 256, 2: FF2 // 256, 3: FF2 // 256}
EXP_STEPS = FF1 // 512


def masks():
    p, f = np.arange(P)[:, None], np.arange(P)[None, :]
    q0, q1 = np.arange(P)[:, None], P + np.arange(P)[:, None]
    k0, k1 = np.arange(P)[None, :], np.arange(S)[None, :]
    out = np.zeros((4, P, 1024), np.float32)

    def both(rule):
        return np.concatenate([rule(q0 - k0), rule(q1 - k1)], axis=1)

    def dilated(d):
        n = ((d >= 0) & (d <= 128)).astype(np.float64)
        n = n + ((d >= 0) & (d % 4 == 0)) + ((d >= 0) & (d % 16 == 0))
        return np.where(n > 0, np.log(np.maximum(n, 1.0)), NEG)
    out[0, :, :384] = both(lambda d: np.where(d >= 0, 0.0, NEG))
    out[1, :, :384] = both(lambda d: np.where((d >= 0) & (d < 128), 0.0, NEG))
    out[2, :, :384] = both(dilated)
    for n in range(LEVELS):
        b = 1 << n
        same = (p // (2 * b)) == (f // (2 * b))
        out[3, :, n * P:(n + 1) * P] = same & ((f // b) % 2 == 1) & ((p // b) % 2 == 0)
    out[3, :, LEVELS * P:(LEVELS + 1) * P] = np.where(f >= p, 0.0, NEG)
    return out


def constants():
    p = np.arange(P)[:, None]
    f = np.arange(P)[None, :]
    parts = {}
    parts["ident"] = (p == f)
    parts["ones"] = np.ones((P, P))
    parts["upto"] = (p <= f)
    parts["before"] = (p < f)
    parts["iota"] = np.broadcast_to(np.arange(S)[None, :], (P, S))
    parts["rank"] = np.broadcast_to(8.0 - np.arange(NE)[None, :], (P, NE))
    inv = (1.0 / (np.float32(500000.0) ** (np.arange(0, 16, 2, dtype=np.float32) / np.float32(16)))).astype(np.float32)
    parts["inv"] = np.broadcast_to(inv[None, :], (P, 8))
    inv2 = (np.float32(500000.0) ** (-np.arange(0, 16, 2, dtype=np.float32) / np.float32(16))).astype(np.float32)
    ang = np.arange(S, dtype=np.float32)[:, None] * inv2[None, :]
    tab = ang.reshape(NT, P, 8).transpose(1, 0, 2).reshape(P, NT * 8).astype(np.float64)
    parts["cos2"] = np.cos(tab)
    parts["sin2"] = np.sin(tab)
    parts["ln_eps"] = np.full((P, 1), LN_EPS)
    parts["rms_eps"] = np.full((P, 1), RMS_EPS)
    at, cols, n = {}, [], 0
    for name, a in parts.items():
        a = np.asarray(a, dtype=np.float32)
        at[name] = (n, a.shape[1])
        n += a.shape[1]
        cols.append(a)
    return np.ascontiguousarray(np.concatenate(cols, axis=1)), at


class Plan:

    def __init__(self):
        self.value, self.per, self.in_loop, self.opens, self.counted = {}, {}, set(), {}, False


class Events:

    def __init__(self, nc, ctx, plan, tag):
        self.nc, self.ctx, self.plan, self.tag = nc, ctx, plan, tag
        self.turn, self.marked, self.seen = None, None, 0

    def new(self, name, step=1):
        return Event(self, name, step)

    def loop(self, turn):
        return Turns(self, turn)


class Turns:

    def __init__(self, events, turn):
        self.events, self.turn = events, turn

    def __enter__(self):
        self.events.turn, self.events.marked = self.turn, {}

    def __exit__(self, *_):
        ev = self.events
        for event, n in ev.marked.items():
            ev.plan.per[event.name] = n
            event.n += (NE - 1) * n
        ev.turn = ev.marked = None


class Event:
    counts = False

    def __init__(self, events, name, step):
        self.ev, self.name, self.step, self.n = events, events.tag + name, step, 0
        self.sem = events.ctx.enter_context(events.nc.semaphore(self.name)) if step else None

    def _turns(self):
        per = self.ev.plan.per.get(self.name, 0)
        return self.ev.turn * per if self.ev.turn is not None and per else 0

    def mark(self, *key):
        self.n += self.step or 1
        if self.ev.marked is not None:
            self.ev.marked[self] = self.ev.marked.get(self, 0) + (self.step or 1)
            self.ev.plan.in_loop.add((self.name, key))
        self.ev.plan.value[self.name, key] = self.n
        return self.sem, self.step

    def at(self, *key):
        value = self.ev.plan.value
        v = value[self.name, key] if self.ev.plan.counted else value.get((self.name, key), 1)
        if self.counts:
            self.ev.seen = max(self.ev.seen, v + (self.ev.turn is None and (self.name, key) in self.ev.plan.in_loop)
                               * (NE - 1) * self.ev.plan.per.get(self.name, 0))
        if self.ev.turn is not None:
            return self.sem, v + self._turns()
        if (self.name, key) in self.ev.plan.in_loop:
            v += (NE - 1) * self.ev.plan.per.get(self.name, 0)
        return self.sem, v

    def last(self):
        return self.sem, self.n + self._turns()


class Groups(Event):
    counts = True


class Free(Event):

    def opened(self, groups):
        opens = self.ev.plan.opens.setdefault(self.name, [])
        turns = self._turns()
        n = self.n
        self.n += 1
        if self.ev.marked is not None:
            self.ev.marked[self] = self.ev.marked.get(self, 0) + 1
        opens.append((groups.n, self.n))
        return n, n + turns

    def mark(self, *key):
        use = 1
        for before, n in self.ev.plan.opens.get(self.name, ()):
            if before < self.ev.seen:
                use = max(use, n)
        self.ev.plan.value[self.name, key] = use
        if self.ev.marked is not None:
            self.ev.plan.in_loop.add((self.name, key))
        return self.sem, 1


def build_program(nc, A, plan, debug=None):
    cst_np, cst_at = constants()
    NC = cst_np.shape[1]
    with ExitStack() as ctx:
        def sb(name, shape, dt=F32):
            return ctx.enter_context(nc.sbuf_tensor(name, shape, dt))

        raw = sb("raw", [P, RAW, UNIT])
        w_hi = sb("w_hi", [P, SPLIT, UNIT], F32R)
        w_lo = sb("w_lo", [P, SPLIT, UNIT], F32R)
        cst = sb("cst", [P, NC])
        X = sb("X", [P, NT, DM])
        R = sb("R", [P, NT, DM])
        xT = [sb(f"xT_{part}", [P, KC, S], F32R) for part in ("hi", "lo")]
        aT = [sb(f"aT_{part}", [P, KC, S], F32R) for part in ("hi", "lo")]
        hT = [a[:, 0:4, :].rearrange("p (i m) n -> p i m n", m=2) for a in aT]
        hTe = [a[:, 4:8, :].rearrange("p (i m) n -> p i (m n)", m=2) for a in aT]
        xe = [a[:, 0:4, :].rearrange("p c n -> p (c n)").rearrange("p (c n) -> p c n", n=P) for a in xT]
        msk = sb("msk", [P, 1024])
        vec = sb("vec", [P, VSLOTS, DM])
        small = sb("small", [P, 640])
        pos_i = sb("pos_i", [P, NT], I32)
        flag_i = sb("flag_i", [P, 1], I32)
        ARENA = 10240
        arena = sb("arena", [P, ARENA])

        def carve(start, shapes):
            out, at = {}, start
            for name, shape in shapes:
                n = int(np.prod(shape))
                ap = arena[:, at:at + n]
                if len(shape) > 1:
                    letters = "abcd"[:len(shape)]
                    ap = ap.rearrange("p (" + " ".join(letters) + ") -> p " + " ".join(letters),
                                      **{c: s for c, s in zip(letters[1:], shape[1:])})
                out[name] = ap
                at += n
            assert at <= ARENA, at
            return out

        att = carve(0, [("qn", (NT, 1536)), ("kd", (NT, 4, 2, DH)), ("qT", (8, S)), ("kT", (4, S)),
                        ("pt", (2, 384)), ("tmp", (4, 20, 8))])
        qk2 = vec
        for name, t in (("s", 0), ("pr", 1)):
            att[name] = att["qn"][:, t, 0:768].rearrange("p (i n) -> p i n", i=2)
        Rf = R[:, :, :].rearrange("p t d -> p (t d)")
        att["sg"] = Rf.rearrange("p (a n) -> p a n", n=512)
        dn = carve(0, [("cv", (12, S)), ("z", (NT, 512)), ("gB", (N_DN, P)), ("bB", (N_DN, P)),
                       ("gam", (N_DN, P)), ("kb", (DN_H, S)), ("DT", (N_DN, P)), ("Xl", (N_DN, P))])
        diag = R[:, 0, 0:NT * P].rearrange("p (t n) -> p t n", n=P)
        dn["vb"] = Rf[:, 0:1024].rearrange("p (a n) -> p a n", n=P)
        dn["kbg"] = Rf[:, 1024:1536].rearrange("p (a n) -> p a n", n=P)
        dn["kdec"] = Rf[:, 1536:2048].rearrange("p (a n) -> p a n", n=P)
        dn["LT"] = dn["kb"].rearrange("p a b -> p (a b)").rearrange("p (a n) -> p a n", n=P)
        dn["D"] = dn["gam"]
        dn["AT"] = dn["gB"]
        dn["qk"] = dn["bB"]
        dn["u"] = dn["LT"]
        dn["wT"] = dn["Xl"][:, 0:DN_H, :]
        dn["state"] = dn["Xl"][:, DN_H:, :]
        dn["vn"] = dn["kdec"]
        dn["o"] = dn["D"]
        dn["sq"] = dn["gam"]
        ffn = carve(0, [("sg", (2, 2, S)), ("cbg", (2, 2, S)), ("cbv", (2, 2, S)), ("gg", (2, 2, S)), ("h", (2, 2, S))])
        moe = carve(0, [("sel", (NT, P)), ("selg", (NT, P)), ("sgT", (S,)), ("sg", (2, 512)), ("h", (2, 512)),
                        ("ye", (DM,))])
        turned_in = carve(0, [("w", (4, 4, P))])["w"]
        junk = arena[:, 7680:9728].rearrange("p (t d) -> p t d", t=NT)
        pT = arena[:, 9728:10240].rearrange("p (c n) -> p c n", c=2)

        bank = [ctx.enter_context(nc.psum_tensor(f"bank{b}", [P, 512], F32)) for b in range(8)]

        def C(name, a=0, b=None):
            at, n = cst_at[name]
            return cst[:, at + a:at + (n if b is None else b)]

        ident, ones = C("ident"), C("ones")
        used = [0]

        def sm(*shape):
            n = int(np.prod(shape))
            ap = small[:, used[0]:used[0] + n]
            used[0] += n
            if len(shape) > 1:
                letters = "abcd"[:len(shape)]
                ap = ap.rearrange("p (" + " ".join(letters) + ") -> p " + " ".join(letters),
                                  **{c: s for c, s in zip(letters[1:], shape[1:])})
            return ap
        cos1, sin1 = sm(NT, 8), sm(NT, 8)
        ang, red, rnd = sm(NT, 8), sm(NT, 8), sm(NT, 8)
        pos_f = sm(NT)
        sinks = sm(NHEAD)
        nmax, rsum, esink, rden = sm(2, 2), sm(2, 2), sm(2, 2), sm(2, 2)
        st6, mv, sd, rstd = sm(NT, 2, 6), sm(NT, 2), sm(NT), sm(NT)
        ss = sm(NT, DN_H)
        lg, lg2, oh1, oh2, sc8 = sm(NT, NE), sm(NT, NE), sm(NT, NE), sm(NT, NE), sm(NT, NE)
        m1, m2, w1, w2 = sm(NT), sm(NT), sm(NT), sm(NT)
        memb, gates, posx = sm(NT, NE), sm(NT, NE), sm(NT, NE + 1)
        pcol, pcol2, gcol = sm(NT), sm(NT), sm(NT)
        flag_f = sm(1)
        tick = sm(9)
        ba, beta, sp1, sp2, gl = sm(NT, 8), sm(NT, DN_H), sm(NT, DN_H), sm(NT, DN_H), sm(NT, DN_H)
        alog, dtb = sm(2, DN_H), sm(2, DN_H)
        ngc, expg, kdsc, bexp = sm(NT, DN_H), sm(NT, DN_H), sm(DN_H), sm(DN_H)
        rn8 = sm(NT, DN_H)
        nsink = sm(NHEAD)
        wr = sb("wr", [P, KC, NE])
        wba = sb("wba", [P, KC, 8])
        wr_s = [sb(f"wr_{part}", [P, KC, NE], F32R) for part in ("hi", "lo")]
        wba_s = [sb(f"wba_{part}", [P, KC, 8], F32R) for part in ("hi", "lo")]
        cw = sb("cw", [P, 12, 4])
        fcw = sb("fcw", [P, 44, 4])
        prew = sb("prew", [P, 2, KC])
        onorm = sb("onorm", [P, P])

        def events(tag):
            ev = Events(nc, ctx, plan, tag)

            class E:
                pass
            E.ev = ev
            E.groups = Groups(ev, "groups", 1)
            E.free = [Free(ev, f"free{b}", 1) for b in range(8)]
            E.dve = ev.new("dve_step")
            E.act = ev.new("act_step")
            E.loaded = [ev.new(f"loaded{s}", 16) for s in range(RAW)]
            E.hi = ev.new("hi_ready")
            E.lo = ev.new("lo_ready")
            return E
        M = events("")
        V = events("ovf_")
        for event in V.free + [V.groups]:
            event.n = 1
        ev = M.ev
        x_ready = ev.new("x_ready")
        params = ev.new("params_loaded", 16)
        consts = ev.new("consts_loaded", 16)
        vecs = [ev.new(f"vec_loaded{s}", 16) for s in range(VSLOTS)]
        vec_used = ev.new("vec_used")
        mask_in = ev.new("mask_loaded", 16)
        first_x = ev.new("x_turned_loaded", 16)
        xs_ready = ev.new("xT_split")
        wsmall = ev.new("small_weights_split")
        stored = ev.new("stored", 16)
        probs, roped, maxed, exped = ev.new("probs"), ev.new("roped"), ev.new("maxed"), ev.new("exped")
        stats, rooted, prenorm, hidden = ev.new("stats"), ev.new("rooted"), ev.new("prenorm"), ev.new("hidden")
        member, decided, flag_done = ev.new("member"), ev.new("decided"), ev.new("flag_done")
        angles, angles_done = ev.new("angles"), ev.new("angles_done")
        squares, decay, normed, inverse, gated = (ev.new("squares"), ev.new("decay"), ev.new("normed"), ev.new("inverse"),
                                                  ev.new("gated"))

        def overflow_done():
            return V.free[3].at("ovf", "own", "sc", 1, 1)

        wo_halves = [("wo", t, nb, 2 * nb + t, (nb, t)) for nb in range(2) for t in range(NT)]
        y_halves = [("y", t, nb, 2 * t + nb, (t, nb)) for t in range(NT) for nb in range(2)]

        def stream_order():
            for L in range(4):
                if L < 2:
                    yield from [(("qkv", L, i), "wu_qkv", (L, i)) for i in range(6)]
                    yield from [(("wo", L, i), "wu_o", (L, i)) for i in range(4)]
                else:
                    yield from [(("in", L, i), "wu_in", (L - 2, i)) for i in range(14)]
                    yield from [(("wo", L, i), "wu_out", (L - 2, i)) for i in range(4)]
                if L == 1:
                    yield (("experts",), None, None)
                else:
                    n = FFN_STEPS[L]
                    gu, dw, pre = ("wu_ffn_gu", "wu_ffn_d", ()) if L == 0 else ("wu_up", "wu_down", (L - 2,))
                    for s in range(n):
                        yield (("gu", L, s, 0), gu, pre + (s, 0))
                        yield (("gu", L, s, 1), gu, pre + (s, 1))
                        if s:
                            yield (("dn", L, s - 1), dw, pre + (s - 1,))
                    yield (("dn", L, n - 1), dw, pre + (n - 1,))
                if L < 2:
                    yield from [(("pg", L, i), "wu_pg", (L, i)) for i in range(4)]
                    yield (("pp", L), "wu_pp", (L,))

        def expert_order():
            def gu(f):
                return [(("gu", f, h, i), ("wu_eg", "wu_eu")[h], (f, i)) for h in range(2) for i in range(2)]

            def down(f):
                return [(("dn", f, i), "wu_ed", (f, i)) for i in range(2)]
            out = gu(0)
            for f in range(EXP_STEPS):
                if f + 1 < EXP_STEPS:
                    out += gu(f + 1)
                if f:
                    out += down(f - 1)
            return out + down(EXP_STEPS - 1)
        EXPERT = expert_order()
        TURN = len(EXPERT)
        assert TURN % RAW == 0 and TURN % SPLIT == 0
        unit_at, n = {}, 0
        for key, arr, idx in stream_order():
            if key == ("experts",):
                expert_base = n
                n += NE * len(EXPERT)
            else:
                unit_at[key] = n
                n += 1
        whole = {unit_at["pp", L] for L in range(2)}
        last_read = plan.value.setdefault("last_read", {})
        after = expert_base + NE * TURN

        def split_no(i):
            return i - sum(1 for w in whole if w < i)

        def place(i):
            return split_no(i) % SPLIT

        def key_of(i):
            if i >= after and i - after < SPLIT:
                return expert_base + TURN + i - after
            return i

        def wait_loaded(E, eng, i):
            slot, n = i % RAW, 16 * (i // RAW + 1)
            if E.ev.turn is not None:
                n = n + E.ev.turn * (16 * TURN // RAW)
            eng.wait_ge(E.loaded[slot].sem, n)
            return raw[:, slot, :]

        def index(key, base=None):
            return unit_at[key] if base is None else base + order.index(key)
        order = [k for k, _, _ in EXPERT]

        def unit(E, pe, key, base=None):
            i = index(key, base)
            pe.wait_ge(*E.lo.at("unit", key_of(i)))
            return w_hi[:, place(i), :], w_lo[:, place(i), :]

        def released(E, i, *key):
            last_read[E.ev.tag, i] = key

        def reader(E, i):
            if E is M and expert_base <= i < after:
                i = expert_base + (i - expert_base) % TURN
            return E.groups.at(*last_read.get((E.ev.tag, i), ("none",)))

        def split_hi(E, ac, i):
            src = wait_loaded(E, ac, i)
            back = i - SPLIT - (1 if any(i - SPLIT <= w < i for w in whole) else 0)
            if E is V and i < SPLIT:
                ac.wait_ge(E.groups.sem, 1 + E.ev.turn * plan.per.get("ovf_groups", 0))
            elif back >= 0:
                ac.wait_ge(*reader(E, back))
            nc.scalar.copy(w_hi[:, place(i), :], src).then_inc(*E.hi.mark("unit", i))

        def split_lo(E, ve, i):
            ve.wait_ge(*E.hi.at("unit", i))
            nc.vector.tensor_tensor(w_lo[:, place(i), :], raw[:, i % RAW, :], w_hi[:, place(i), :].bitcast(F32), ALU.subtract) \
                .then_inc(*E.lo.mark("unit", i))

        def ahead(E, split, eng, key, base=None):
            i = index(key, base)
            if i in whole and E is M:
                return
            j = i + SPLIT
            if E is V and j >= TURN:
                return
            if E is M and base is None and i < expert_base <= j:
                return
            if E is M:
                j += sum(1 for w in whole if i < w <= j)
                if j in whole:
                    j += 1
            if j < n_units:
                split(E, eng, j)
        n_units = n

        block = ctx.enter_context(nc.Block())

        @block.sync
        def _(sp):
            sp.dma_start(Rf, A["xT"].rearrange("p c n -> p (c n)")).then_inc(*first_x.mark())
            for key, arr, idx in stream_order():
                if key == ("experts",):
                    sp.wait_ge(*M.lo.at("unit", expert_base - 1))
                    sp.wait_ge(*flag_done.at())
                    r = sp.value_load(flag_i[0:1, 0:1], min_val=0, max_val=1)
                    with sp.If(r > 0):
                        with sp.Fori(0, NE) as e:
                            with V.ev.loop(e):
                                sp.wait_ge(V.groups.sem, e * plan.per.get("ovf_groups", 0) + 1)
                                for j, (ekey, earr, eidx) in enumerate(EXPERT):
                                    if j >= RAW:
                                        sp.wait_ge(*V.lo.at("unit", j - RAW))
                                    sp.dma_start(raw[:, j % RAW, :], A[earr][e, eidx[0], eidx[1]]) \
                                        .then_inc(*V.loaded[j % RAW].mark())
                        sp.wait_ge(*overflow_done())
                    with sp.Fori(0, NE) as e:
                        with ev.loop(e):
                            for j, (ekey, earr, eidx) in enumerate(EXPERT):
                                i = expert_base + j
                                sem, v = M.lo.at("unit", expert_base + (j - RAW) % TURN)
                                sp.wait_ge(sem, v - plan.per.get("lo_ready", 0) if j < RAW else v)
                                sp.dma_start(raw[:, i % RAW, :], A[earr][e, eidx[0], eidx[1]]) \
                                    .then_inc(*M.loaded[i % RAW].mark())
                    continue
                i = unit_at[key]
                if i >= RAW:
                    old = i - RAW
                    if expert_base <= old < after:
                        old = expert_base + (old - expert_base) % TURN
                    sp.wait_ge(*(reader(M, old) if old in whole else M.lo.at("unit", key_of(old))))
                src = A[arr][idx] if len(idx) > 1 else A[arr][idx[0]]
                sp.dma_start(raw[:, i % RAW, :], src).then_inc(*M.loaded[i % RAW].mark())
            sp.wait_ge(*x_ready.at(3, "ffn", 1))
            sp.dma_start(A["out"].rearrange("(t p) d -> p t d", p=P), X[:, :, :]).then_inc(*stored.mark())
            sp.wait_ge(*stored.at())

        @block.gpsimd
        def _(gp):
            def load(*loads):
                for dst, src, key in loads:
                    gp.dma_start(dst, src).then_inc(*params.mark())
                for dst, src, key in loads:
                    plan.value[params.name, key] = params.n

            def load_vec(v):
                s = v % VSLOTS
                if v >= VSLOTS:
                    old = v - VSLOTS
                    if old >= 8:
                        gp.wait_ge(*x_ready.at(2, "mix" if old == 8 else "ffn", 1))
                    elif old % 2 == 0:
                        gp.wait_ge(*vec_used.at(old))
                    else:
                        gp.wait_ge(*x_ready.at(old // 4, "mix" if old % 4 == 1 else "ffn", 1))
                gp.dma_start(vec[:, s, :], A["vecs"][v]).then_inc(*vecs[s].mark())
            def load_mask(n):
                gp.dma_start(msk[:, :], A["masks"][n]).then_inc(*mask_in.mark())

            def load_layer(L):
                gp.wait_ge(*params.last())
                load((wba[:, :, :], A["wba"][L - 2], ("wba", L)), (cw[:, :, :], A["cw"][L - 2], ("cw", L)),
                     (fcw[:, :, :], A["fcw"][L - 2], ("fcw", L)), (prew[:, :, :], A["prew"][L - 2], ("prew", L)),
                     (onorm[:, :], A["onorm"][L - 2], ("onorm", L)))
            gp.dma_start(cst[:, :], A["cst"]).then_inc(*consts.mark())
            load((pos_i[:, :], A["positions"], ("pos",)), (sinks, A["sinks"], ("sinks",)))
            load_mask(0)
            gp.wait_ge(*params.last())
            load((X[:, :, :], A["x"].rearrange("(t p) d -> p t d", p=P), ("X",)),
                 (alog, A["alog"], ("alog",)), (dtb, A["dtb"], ("dtb",)), (wr[:, :, :], A["wr"], ("wr",)))
            load_vec(0)
            load_vec(1)
            for L in range(2):
                gp.wait_ge(*maxed.at(L, NHEAD - 1))
                load_mask(1 if L == 0 else 3)
                load_vec(4 * L + 2)
                load_vec(4 * L + 3)
                gp.wait_ge(*params.last())
                load((pT, A["pT"][L], ("pT", L)))
                if L == 0:
                    load_vec(4)
                    load_vec(5)
            load_layer(2)
            for L in (2, 3):
                gp.wait_ge(*inverse.at(L, LEVELS - 1, "LT", 1))
                load_mask(2)
                gp.wait_ge(*maxed.at(L, 7))
                load_vec(2 * L + 4)
                load_vec(2 * L + 5)
                if L == 2:
                    load_mask(3)
                    gp.wait_ge(*x_ready.at(2, "ffn", 1))
                    load_layer(3)
            if debug:
                k = 0
                for L, w in debug["dump"]:
                    gp.wait_ge(*x_ready.at(L, w, 1))
                    gp.dma_start(A["dbg"][k].rearrange("(t p) d -> p t d", p=P), X[:, :, :]).then_inc(*stored.mark("dbg", k))
                    k += 1

        @block.tensor
        def _(pe):
            def open_bank(E, b):
                before, n = E.free[b].opened(E.groups)
                if before:
                    pe.wait_ge(E.free[b].sem, n)
                return bank[b]

            def transposes(stage, ready, scaled=False):
                for t in range(NT):
                    pe.wait_ge(*ready(t))
                    for g in range(2):
                        o = open_bank(M, 2 * t + g)
                        for c in range(4):
                            dst, src = o[:, c * P:(c + 1) * P], X[:, t, (4 * g + c) * P:(4 * g + c + 1) * P]
                            if scaled:
                                mm = nc.tensor.matmul(dst, src, diag[:, t, :], start=True, stop=True)
                            else:
                                mm = nc.tensor.transpose(dst, src, ident)
                        mm.then_inc(*M.groups.mark("tx", stage, t, g))

            def keep_warm(n, b):
                if M.free[b].n:
                    pe.wait_ge(M.free[b].sem, M.free[b].n)
                for _ in range(n):
                    nc.tensor.matmul(bank[b][:, :], ident, cst[:, 0:512], start=True, stop=True)

            def mm3(o, l, r, first, last, lone=True, lcols=slice(None), rcols=slice(None)):
                for n, (i, j) in enumerate(((0, 0), (0, 1), (1, 0))):
                    mm = nc.tensor.matmul(o, l[i], r[j], start=(first and n == 0), stop=(last and n == 2),
                                          skip_group_check=not lone)
                return mm

            def part(name, L, units, n, lhs, b0, i, t):
                key = (units, L, 2 * n + i)
                u = unit(M, pe, key)
                o = open_bank(M, b0 + t) if i == 0 else bank[b0 + t]
                for kc in range(4 * i, 4 * i + 4):
                    mm = mm3(o[:, :], [a[:, kc, t * P:(t + 1) * P] for a in lhs],
                             [w[:, (kc % 4) * 512:(kc % 4 + 1) * 512] for w in u], kc == 0, kc == KC - 1)
                last = (name, L, n, t) if i else ("unit",) + key
                if i or t:
                    mm.then_inc(*M.groups.mark(*last))
                if t:
                    released(M, unit_at[key], *last)

            def linear(name, L, blocks, lhs, units=None):
                for n in range(blocks):
                    for i in range(2):
                        for t in range(NT):
                            part(name, L, units or name, n, lhs, (2 * n) % 4, i, t)

            def features(o, key_a, key_b, cols, name_a, names_b):
                for i, key in enumerate((key_a, key_b)):
                    u = unit(M, pe, key)
                    for half in range(2):
                        for m in range(2):
                            for kc in range(4 * i, 4 * i + 4):
                                c0 = (kc % 4) * 512 + cols(half, m)
                                mm = mm3(o[half][:, m * S:(m + 1) * S], [w[:, c0:c0 + P] for w in u],
                                         [a[:, kc, :] for a in xT], kc == 0 and m == 0, kc == KC - 1, lone=False)
                        if i == 1:
                            mm.then_inc(*M.groups.mark(*names_b[half]))
                    if i == 0:
                        mm.then_inc(*M.groups.mark(*name_a))
                        released(M, unit_at[key], *name_a)
                    else:
                        released(M, unit_at[key], *names_b[1])

            def attention(L, heads, kchunk, out0):
                def scores(h):
                    j, lo = h // 2, DH * (h % 2)
                    o = open_bank(M, 4 + h % 2)
                    q = att["qT"][lo:lo + DH, j, :]
                    k = att["kT"][lo:lo + DH, kchunk(h), :]
                    nc.tensor.matmul(o[:, 0:P], q[:, 0:P], k[:, 0:P], start=True, stop=True)
                    nc.tensor.matmul(o[:, P:3 * P], q[:, P:S], k[:, :], start=True, stop=True) \
                        .then_inc(*M.groups.mark("sc", L, h))

                def turn(h):
                    pe.wait_ge(*probs.at(L, h))
                    o = open_bank(M, 6 + h % 2)
                    for c in range(3):
                        mm = nc.tensor.transpose(o[:, c * P:(c + 1) * P], att["pr"][:, h % 2, c * P:(c + 1) * P], ident)
                    mm.then_inc(*M.groups.mark("pt", L, h))

                def values(h):
                    j, lo = h // 2, DH * (h % 2)
                    o = bank[2 + j % 2] if h % 2 else open_bank(M, 2 + j % 2)
                    pe.wait_ge(*M.free[6 + h % 2].at("pt", L, h))
                    vcol = 1280 + DH * (h // 4) if L < 2 else 1024 + DH * h
                    nc.tensor.matmul(o[lo:lo + DH, 0:S], att["qn"][:, 0, vcol:vcol + DH], att["pt"][:, h % 2, 0:S],
                                     start=True, stop=False)
                    nc.tensor.matmul(o[lo:lo + DH, P:S], att["qn"][:, 1, vcol:vcol + DH], att["pt"][:, h % 2, S:S + P],
                                     start=False, stop=True).then_inc(*M.groups.mark("pv", L, h))
                for i in range(heads + 3):
                    if i < heads:
                        scores(i)
                    if 2 <= i < heads + 2:
                        turn(i - 2)
                    if i >= 3:
                        values(i - 3)

            def turn_qk(L, nq):
                for t in range(NT):
                    pe.wait_ge(*roped.at(L, t, NHEAD if L < 2 else 0))
                    for g in range(nq // 4 + 1):
                        o = open_bank(M, (3 * t + g) % 4)
                        for c in range(4):
                            if L >= 2:
                                src = qk2[:, t, (4 * g + c) * P:(4 * g + c + 1) * P]
                            elif g < nq // 4:
                                src = att["qn"][:, t, (4 * g + c) * P:(4 * g + c + 1) * P]
                            else:
                                src = att["kd"][:, t, c, :, :].rearrange("p a b -> p (a b)")
                            mm = nc.tensor.transpose(o[:, c * P:(c + 1) * P], src, ident)
                        mm.then_inc(*M.groups.mark("qkT", L, t, g))
                for t in range(NT):
                    for g in range(nq // 4 + 1):
                        pe.wait_ge(*M.free[(3 * t + g) % 4].at("qkT", L, t, g))

            def xT_ready(stage):
                for t in range(NT):
                    for g in range(2):
                        if stage[0] < 2:
                            pe.wait_ge(*M.free[2 * t + g].at("xT", stage, t, g))
                        else:
                            pe.wait_ge(*xs_ready.at(stage, t, g))

            def dense_ffn(L):
                n = FFN_STEPS[L]

                def gate_up(s):
                    o = [open_bank(M, 4 + 2 * (s % 2) + half) for half in range(2)]
                    features(o, ("gu", L, s, 0), ("gu", L, s, 1), lambda half, m: half * 256 + m * P,
                             ("unit", "gu", L, s, 0), [("gu", L, s, 0), ("gu", L, s, 1)])

                def down(s):
                    d = unit(M, pe, ("dn", L, s))
                    pe.wait_ge(*hidden.at(L, s))
                    for t in range(NT):
                        for nb in range(2):
                            o = open_bank(M, 2 * t + nb) if s == 0 else bank[2 * t + nb]
                            for m in range(2):
                                c0 = m * DM + nb * 512
                                mm = mm3(o[:, :], [a[:, s % 2, m, t * P:(t + 1) * P] for a in hT],
                                         [w[:, c0:c0 + 512] for w in d], s == 0 and m == 0, s == n - 1 and m == 1)
                            if s == n - 1:
                                mm.then_inc(*M.groups.mark("y", L, t, nb))
                    if s < n - 1:
                        mm.then_inc(*M.groups.mark("down", L, s))
                    released(M, unit_at["dn", L, s], *(("down", L, s) if s < n - 1 else ("y", L, 1, 1)))
                gate_up(0)
                for s in range(n):
                    if s + 1 < n:
                        gate_up(s + 1)
                    down(s)

            def router():
                pe.wait_ge(*wsmall.at("wr"))
                for t in range(NT):
                    o = open_bank(M, t)
                    for kc in range(KC):
                        mm = mm3(o[:, 0:NE], [a[:, kc, t * P:(t + 1) * P] for a in xT], [w[:, kc, :] for w in wr_s],
                                 kc == 0, kc == KC - 1)
                    mm.then_inc(*M.groups.mark("router", t))
                pe.wait_ge(*member.at())
                o = open_bank(M, 2)
                nc.tensor.matmul(o[:, 0:NE], C("before"), memb[:, 0, :], start=True, stop=True)
                nc.tensor.matmul(o[:, NE:2 * NE], ones, memb[:, 0, :], start=True, stop=False)
                nc.tensor.matmul(o[:, NE:2 * NE], C("before"), memb[:, 1, :], start=False, stop=True)
                nc.tensor.matmul(o[:, 2 * NE:3 * NE], ones, memb[:, 0, :], start=True, stop=False)
                nc.tensor.matmul(o[:, 2 * NE:3 * NE], ones, memb[:, 1, :], start=False, stop=True) \
                    .then_inc(*M.groups.mark("ranks"))

            def gather(E, tag, which):
                pe.wait_ge(*E.dve.at(tag, which, "sel"))
                for g in range(2):
                    o = open_bank(E, 2 + g)
                    for c in range(4):
                        for t in range(NT):
                            mm = nc.tensor.matmul(o[:, c * P:(c + 1) * P], X[:, t, (4 * g + c) * P:(4 * g + c + 1) * P],
                                                  moe["sel"][:, t, :], start=(t == 0), stop=(t == NT - 1))
                    mm.then_inc(*E.groups.mark(tag, which, "ga", g))

            def gathered(E, tag, which):
                for g in range(2):
                    pe.wait_ge(*E.free[2 + g].at(tag, which, "xe", g))

            def scatter(E, tag, which):
                for t in range(NT):
                    for nb in range(2):
                        o = open_bank(E, 2 * t + nb)
                        nc.tensor.matmul(o[:, :], moe["sgT"][:, t * P:(t + 1) * P], moe["ye"][:, nb * 512:(nb + 1) * 512],
                                         start=True, stop=True).then_inc(*E.groups.mark(tag, which, "sc", t, nb))

            def experts(E, tag, base):
                if E is V:
                    gather(E, tag, "own")
                    gathered(E, tag, "own")

                def turn_gates():
                    pe.wait_ge(*E.dve.at(tag, "selg"))
                    o = open_bank(E, 3)
                    for t in range(NT):
                        mm = nc.tensor.transpose(o[:, t * P:(t + 1) * P], moe["selg"][:, t, :], ident)
                    mm.then_inc(*E.groups.mark(tag, "tg"))

                def gate_up(f):
                    for half in range(2):
                        o = open_bank(E, 4 + 2 * (f % 2) + half)
                        for i in range(2):
                            key = ("gu", f, half, i)
                            u = unit(E, pe, key, base)
                            for kc in range(4 * i, 4 * i + 4):
                                mm = mm3(o[:, :], [a[:, kc, :] for a in xe], [w[:, (kc % 4) * 512:(kc % 4 + 1) * 512] for w in u],
                                         kc == 0, kc == KC - 1)
                            name = (tag, "unit") + key if i == 0 else (tag, "gu", f, half)
                            mm.then_inc(*E.groups.mark(*name))
                            released(E, index(key, base), *name)

                def turn(f):
                    pe.wait_ge(*E.free[5 + 2 * (f % 2)].at(tag, "h", f))
                    o = open_bank(E, 2 + f % 2)
                    for c in range(4):
                        mm = nc.tensor.transpose(o[:, c * P:(c + 1) * P], moe["h"][:, f % 2, c * P:(c + 1) * P], ident)
                    mm.then_inc(*E.groups.mark(tag, "tr", f))

                def down(f):
                    o = [open_bank(E, nb) if f == 0 else bank[nb] for nb in range(2)]
                    for i in range(2):
                        key = ("dn", f, i)
                        d = unit(E, pe, key, base)
                        if i == 0:
                            pe.wait_ge(*E.free[2 + f % 2].at(tag, "hTe", f))
                        for nb in range(2):
                            for c in range(2):
                                cc = 2 * i + c
                                c0 = c * DM + nb * 512
                                mm = mm3(o[nb][:, :], [a[:, f % 2, cc * P:(cc + 1) * P] for a in hTe], [w[:, c0:c0 + 512] for w in d],
                                         f == 0 and cc == 0, f == EXP_STEPS - 1 and cc == 3)
                        name = (tag, "unit") + key if i == 0 else (tag, "dn", f)
                        mm.then_inc(*E.groups.mark(*name))
                        released(E, index(key, base), *name)
                gate_up(0)
                if E is M:
                    scatter(E, tag, "before")
                for f in range(EXP_STEPS):
                    if f + 1 < EXP_STEPS:
                        gate_up(f + 1)
                    turn(f)
                    if f == 0:
                        turn_gates()
                    else:
                        down(f - 1)
                    if E is M and f == EXP_STEPS - 1:
                        gather(E, tag, "next")
                down(EXP_STEPS - 1)
                if E is V:
                    scatter(E, tag, "own")
                else:
                    gathered(E, tag, "next")

            def delta(L):
                for nb in range(3):
                    o = [open_bank(M, 2 * (nb % 2) + j) for j in range(2)]
                    features(o, ("in", L, 2 * nb), ("in", L, 2 * nb + 1), lambda j, m: (2 * j + m) * P,
                             ("unit", "in", L, 2 * nb), [("cv", L, 2 * nb), ("cv", L, 2 * nb + 1)])
                pe.wait_ge(*wsmall.at("wba", L))
                o = open_bank(M, 2)
                for t in range(NT):
                    for kc in range(KC):
                        mm = mm3(o[:, t * 8:t * 8 + 8], [a[:, kc, t * P:(t + 1) * P] for a in xT],
                                 [w[:, kc, :] for w in wba_s], kc == 0, kc == KC - 1)
                mm.then_inc(*M.groups.mark("ba", L))
                for i in range(2):
                    for t in range(NT):
                        part("in", L, "in", 3, xT, 0, i, t)
                for g in range(4):
                    pe.wait_ge(*squares.at(L, g))
                    o = open_bank(M, 4 + g)
                    nc.tensor.matmul(o[:, :], ones, dn["sq"][:, 4 * (g % 2):4 * (g % 2) + 4, :].rearrange("p a b -> p (a b)"),
                                     start=True, stop=True).then_inc(*M.groups.mark("ssq", L, g))
                for i in range(2):
                    for t in range(NT):
                        part("in", L, "in", 4, xT, 0, i, t)
                pe.wait_ge(*decay.at(L, "g"))
                o = open_bank(M, 6)
                for t in range(NT):
                    mm = nc.tensor.matmul(o[:, t * DN_H:(t + 1) * DN_H], C("upto"), gl[:, t, :], start=True, stop=True)
                mm.then_inc(*M.groups.mark("gcol", L))
                pe.wait_ge(*decay.at(L, "rows"))
                for name, src, rhs, b0 in (("grow", dn["gB"], C("upto"), 0), ("brow", dn["bB"], ident, 2)):
                    for t in range(NT):
                        o = open_bank(M, b0 + t)
                        for h in range(DN_H):
                            mm = nc.tensor.matmul(o[:, h * P:(h + 1) * P], src[:, t * DN_H + h, :], rhs, start=True, stop=True)
                        mm.then_inc(*M.groups.mark(name, L, t))
                pe.wait_ge(*normed.at(L, 3))
                for name, c0, b0 in (("kn", DN_H, 4), ("vn", 2 * DN_H, 6)):
                    for t in range(NT):
                        o = open_bank(M, b0 + t)
                        for h in range(DN_H):
                            mm = nc.tensor.transpose(o[:, h * P:(h + 1) * P], dn["cv"][:, c0 + h, t * P:(t + 1) * P], ident)
                        mm.then_inc(*M.groups.mark(name, L, t))
                for name, b0 in (("kk", 0), ("kq", 2)):
                    for t in range(NT):
                        if name == "kk":
                            pe.wait_ge(*M.free[2 + t].at("brow", L, t))
                        o = open_bank(M, b0 + t)
                        for h in range(DN_H):
                            rhs = dn["kb"][:, h, t * P:(t + 1) * P] if name == "kk" else dn["cv"][:, h, t * P:(t + 1) * P]
                            mm = nc.tensor.matmul(o[:, h * P:(h + 1) * P], dn["cv"][:, DN_H + h, t * P:(t + 1) * P], rhs,
                                                  start=True, stop=True)
                        mm.then_inc(*M.groups.mark(name, L, t))
                for n in range(LEVELS):
                    for t in range(NT):
                        pe.wait_ge(*inverse.at(L, n, "LT", t))
                        if n == 1:
                            pe.wait_ge(*M.free[t].at("lv", L, 0, "X", t))
                        elif n > 1:
                            pe.wait_ge(*M.free[2 + t].at("lv", L, n - 1, "D", t))
                        o = open_bank(M, t)
                        for h in range(DN_H):
                            i = t * DN_H + h
                            if n == 0:
                                mm = nc.tensor.transpose(o[:, h * P:(h + 1) * P], dn["LT"][:, i, :], ident)
                            else:
                                mm = nc.tensor.matmul(o[:, h * P:(h + 1) * P], dn["LT"][:, i, :], dn["D"][:, i, :], start=True, stop=True)
                        mm.then_inc(*M.groups.mark("lv", L, n, "X", t))
                    if n == 0:
                        continue
                    if n <= 4:
                        part("in", L, "in", 5, xT, 6, (n - 1) // 2, (n - 1) % 2)
                    for t in range(NT):
                        pe.wait_ge(*M.free[t].at("lv", L, n, "X", t))
                        if n > 1:
                            pe.wait_ge(*M.free[4 + t].at("lv", L, n - 1, "DT", t))
                        for which, b in ((0, 2 + t), (1, 4 + t)):
                            if which == 0 and n == LEVELS - 1:
                                continue
                            o = open_bank(M, b)
                            for h in range(DN_H):
                                i = t * DN_H + h
                                a, r = (dn["DT"], dn["Xl"]) if which == 0 else (dn["Xl"], dn["DT"])
                                mm = nc.tensor.matmul(o[:, h * P:(h + 1) * P], a[:, i, :], r[:, i, :], start=True, stop=True)
                            mm.then_inc(*M.groups.mark("lv", L, n, "D" if which == 0 else "DT", t))
                for t in range(NT):
                    pe.wait_ge(*M.free[4 + t].at("lv", L, LEVELS - 1, "DT", t))
                for t in range(NT):
                    pe.wait_ge(*M.free[4 + t].at("kn", L, t))
                    pe.wait_ge(*M.free[6 + t].at("vn", L, t))
                for t in range(NT):
                    o = open_bank(M, t)
                    for h in range(DN_H):
                        i = t * DN_H + h
                        mm = nc.tensor.matmul(o[:, h * P:(h + 1) * P], dn["DT"][:, i, :], dn["vb"][:, i, :], start=True, stop=True)
                    mm.then_inc(*M.groups.mark("u", L, t))
                o = open_bank(M, 2)
                for h in range(DN_H):
                    mm = nc.tensor.matmul(o[:, h * P:(h + 1) * P], dn["kbg"][:, h, :], dn["DT"][:, DN_H + h, :], start=True, stop=True)
                mm.then_inc(*M.groups.mark("wT", L))
                pe.wait_ge(*M.free[0].at("u", L, 0))
                o = open_bank(M, 3)
                for h in range(DN_H):
                    mm = nc.tensor.matmul(o[:, h * P:(h + 1) * P], dn["kdec"][:, h, :], dn["u"][:, h, :], start=True, stop=True)
                mm.then_inc(*M.groups.mark("state", L))
                o = open_bank(M, 4)
                for h in range(DN_H):
                    mm = nc.tensor.matmul(o[:, h * P:(h + 1) * P], dn["qk"][:, h, :], dn["u"][:, h, :], start=True, stop=True)
                mm.then_inc(*M.groups.mark("o0", L))
                pe.wait_ge(*M.free[3].at("state", L))
                pe.wait_ge(*M.free[2].at("wT", L))
                o = open_bank(M, 5)
                for h in range(DN_H):
                    mm = nc.tensor.matmul(o[:, h * P:(h + 1) * P], dn["wT"][:, h, :], dn["state"][:, h, :], start=True, stop=True)
                mm.then_inc(*M.groups.mark("ws", L))
                o = open_bank(M, 6)
                for h in range(DN_H):
                    mm = nc.tensor.matmul(o[:, h * P:(h + 1) * P], dn["cv"][:, h, P:S], dn["state"][:, h, :], start=True, stop=True)
                mm.then_inc(*M.groups.mark("qs", L))
                pe.wait_ge(*M.free[5].at("ws", L))
                o = open_bank(M, 7)
                for h in range(DN_H):
                    mm = nc.tensor.matmul(o[:, h * P:(h + 1) * P], dn["qk"][:, DN_H + h, :], dn["vn"][:, h, :], start=True, stop=True)
                mm.then_inc(*M.groups.mark("o1", L))
                for i in range(2):
                    for t in range(NT):
                        part("in", L, "in", 6, xT, 2, i, t)
                for t in range(NT):
                    pe.wait_ge(*gated.at(L, t))
                    o = open_bank(M, t)
                    for h in range(DN_H):
                        mm = nc.tensor.transpose(o[:, h * P:(h + 1) * P], dn["o"][:, t * DN_H + h, :], ident)
                    mm.then_inc(*M.groups.mark("oT", L, t))

            for L in range(2):
                if L == 0:
                    pe.wait_ge(*consts.at())
                    keep_warm(WARM_START, 6)
                    pe.wait_ge(*xs_ready.at("first"))
                else:
                    keep_warm(WARM_PLE, 0)
                    transposes((L, "in"), lambda t: x_ready.at(0, "ple", t))
                    xT_ready((L, "in"))
                linear("qkv", L, 3, xT)
                turn_qk(L, 8)
                attention(L, NHEAD, lambda h: h // 4, 0)
                for j in range(8):
                    pe.wait_ge(*M.free[2 + j % 2].at("pv", L, j))
                linear("wo", L, 2, aT)
                keep_warm(WARM_LN, 6)
                transposes((L, "mix"), lambda t: x_ready.at(L, "mix", t))
                xT_ready((L, "mix"))
                if L == 0:
                    dense_ffn(0)
                else:
                    router()
                    pe.wait_ge(*flag_done.at())
                    r = pe.value_load(flag_i[0:1, 0:1], min_val=0, max_val=1)
                    with pe.If(r > 0):
                        with pe.Fori(0, NE) as e:
                            with V.ev.loop(e):
                                experts(V, "ovf", 0)
                        pe.wait_ge(*overflow_done())
                    gather(M, "moe", "first")
                    gathered(M, "moe", "first")
                    pe.wait_ge(*M.dve.at("moe", "zeroed"))
                    with pe.Fori(0, NE) as e:
                        with ev.loop(e):
                            experts(M, "moe", expert_base)
                    scatter(M, "moe", "last")
                keep_warm(WARM_LN, 6)
                transposes((L, "ffn"), lambda t: x_ready.at(L, "ffn", t))
                xT_ready((L, "ffn"))
                linear("pg", L, 2, xT)
                u = wait_loaded(M, pe, unit_at["pp", L])
                pe.wait_ge(*params.at("pT", L))
                for nb in range(2):
                    for t in range(NT):
                        o = open_bank(M, 4 + 2 * nb + t)
                        for kc in range(2):
                            mm = nc.tensor.matmul(o[:, :], pT[:, kc, t * P:(t + 1) * P],
                                                  u[:, kc * DM + nb * 512:kc * DM + (nb + 1) * 512],
                                                  start=(kc == 0), stop=(kc == 1))
                        mm.then_inc(*M.groups.mark("pp", L, nb, t))
                released(M, unit_at["pp", L], "pp", L, 1, 1)
            for L in range(2, 4):
                keep_warm(WARM_PLE if L == 2 else WARM_RMS, 0 if L == 2 else 6)
                transposes((L, "in"), lambda t: prenorm.at(L, "in", t), True)
                xT_ready((L, "in"))
                delta(L)
                turn_qk(L, 4)
                attention(L, 8, lambda h: h // 2, 4)
                for t in range(NT):
                    pe.wait_ge(*M.free[t].at("oT", L, t))
                for j in range(4):
                    pe.wait_ge(*M.free[2 + j % 2].at("pv", L, j))
                linear("wo", L, 2, aT)
                keep_warm(WARM_RMS, 6)
                transposes((L, "mix"), lambda t: prenorm.at(L, "mix", t), True)
                xT_ready((L, "mix"))
                dense_ffn(L)

        @block.scalar
        def _(ac):
            def wait_self(E=M):
                ac.wait_ge(*E.act.last())

            def walk(*key):
                ahead(M, split_hi, ac, key)

            def copy_T(stage, L):
                for t in range(NT):
                    for g in range(2):
                        if L < 2:
                            ac.wait_ge(*M.groups.at("tx", stage, t, g))
                            src = bank[2 * t + g][:, :].rearrange("p (c n) -> p c n", n=P)
                        else:
                            ac.wait_ge(*M.free[2 * t + g].at("xT", stage, t, g))
                            src = turned_in[:, 2 * t + g, :, :]
                        nc.scalar.copy(xT[0][:, 4 * g:4 * g + 4, t * P:(t + 1) * P], src) \
                            .then_inc(*M.act.mark("xT", stage, t, g))

            def block_out(name, L, n, b0, dst, scale=1.0):
                for t in range(NT):
                    ac.wait_ge(*M.groups.at(name, L, n, t))
                    nc.scalar.activation(dst[:, t, :], bank[b0 + t][:, :], ACT.Copy, scale=scale) \
                        .then_inc(*M.free[b0 + t].mark(name, L, n, t))

            def qkv_out(L):
                for n in range(3):
                    walk("qkv", L, 2 * n)
                    block_out("qkv", L, n, (2 * n) % 4, att["qn"][:, :, n * 512:(n + 1) * 512], DH ** -0.5 if n < 2 else 1.0)
                    walk("qkv", L, 2 * n + 1)

            def copy_qkT(L, nq):
                for t in range(NT):
                    for g in range(nq // 4 + 1):
                        b = (3 * t + g) % 4
                        ac.wait_ge(*M.groups.at("qkT", L, t, g))
                        dst = att["qT"][:, 4 * g:4 * g + 4, t * P:(t + 1) * P] if g < nq // 4 \
                            else att["kT"][:, :, t * P:(t + 1) * P]
                        nc.scalar.copy(dst, bank[b][:, :].rearrange("p (c n) -> p c n", n=P)) \
                            .then_inc(*M.free[b].mark("qkT", L, t, g))

            def attention(L, heads, out0):
                def exps(h):
                    i = h % 2
                    ac.wait_ge(*maxed.at(L, h))
                    if h >= 2:
                        ac.wait_ge(*M.groups.at("pt", L, h - 2))
                    for q, (a, b) in enumerate(((0, P), (P, 3 * P))):
                        ins = nc.scalar.activation(att["pr"][:, i, a:b], att["s"][:, i, a:b], ACT.Exp,
                                                   bias=nmax[:, i, q:q + 1], accum_out=rsum[:, i, q:q + 1])
                    if L == 1:
                        ins = nc.scalar.activation(esink[:, i, :], nmax[:, i, :], ACT.Exp, bias=sinks[:, h:h + 1])
                    ins.then_inc(*exped.mark(L, h))

                def turned(h):
                    ac.wait_ge(*M.groups.at("pt", L, h))
                    if h >= 2:
                        ac.wait_ge(*M.groups.at("pv", L, h - 2))
                    nc.scalar.copy(att["pt"][:, h % 2, :], bank[6 + h % 2][:, 0:384]).then_inc(*M.free[6 + h % 2].mark("pt", L, h))

                def out(j):
                    ac.wait_ge(*M.groups.at("pv", L, 2 * j + 1))
                    nc.scalar.copy(aT[0][:, out0 + j, :], bank[2 + j % 2][:, 0:S]).then_inc(*M.act.mark("aT", L, j))
                for i in range(heads + 3):
                    if i < heads:
                        exps(i)
                    if 2 <= i < heads + 2:
                        turned(i - 2)
                    if i >= 4 and i % 2 == 0:
                        out(i // 2 - 2)

            def root(L, which, src, scale, eps):
                ac.wait_ge(*stats.at(L, which))
                nc.scalar.activation(sd, src, ACT.Sqrt, bias=eps, scale=scale).then_inc(*rooted.mark(L, which))

            def sum_squares(L, which, src, ready):
                if M.act.n:
                    wait_self()
                for t in range(NT):
                    ac.wait_ge(*ready(t))
                    ins = nc.scalar.activation(junk[:, t, :], src[:, t, :], ACT.Square, accum_out=ss[:, t, 0:1])
                ins.then_inc(*M.act.mark("ss", L, which))
                wait_self()
                nc.scalar.activation(sd, ss[:, :, 0], ACT.Sqrt, bias=C("rms_eps"), scale=1.0 / DM) \
                    .then_inc(*rooted.mark(L, which))

            def half_squares(L, which, halves):
                wait_self()
                for name, t, nb, b, key in halves:
                    ac.wait_ge(*M.groups.at(name, L, *key))
                    nc.scalar.activation(junk[:, t, nb * 512:(nb + 1) * 512], bank[b][:, :], ACT.Square,
                                         accum_out=ss[:, t, nb:nb + 1]).then_inc(*M.act.mark("sq", L, which, nb, t))
                root(L, which, ss[:, :, 0], 1.0 / DM, C("rms_eps"))

            def dense_act(L):
                n = FFN_STEPS[L]
                for s in range(n):
                    b = 4 + 2 * (s % 2)
                    walk("gu", L, s, 0)
                    if L == 0:
                        ac.wait_ge(*M.groups.at("gu", L, s, 0))
                        if s >= 2:
                            ac.wait_ge(*hidden.at(L, s - 2))
                        nc.scalar.activation(ffn["sg"][:, s % 2, :, :].rearrange("p a b -> p (a b)"), bank[b][:, :], ACT.Silu) \
                            .then_inc(*M.free[b].mark("sg", L, s))
                        walk("gu", L, s, 1)
                        if s:
                            walk("dn", L, s - 1)
                        continue
                    if s >= 2:
                        ac.wait_ge(*hidden.at(L, s - 2))
                    for half, buf in enumerate((ffn["cbg"], ffn["cbv"])):
                        ac.wait_ge(*M.groups.at("gu", L, s, half))
                        for m in range(2):
                            c = half * 22 + 2 * s + m
                            ins = nc.scalar.activation(buf[:, s % 2, m, :], bank[b + half][:, m * S:(m + 1) * S], ACT.Identity,
                                                       bias=fcw[:, c, 3:4], scale=fcw[:, c, 2:3])
                        ins.then_inc(*M.act.mark("tap", L, s, half))
                    walk("gu", L, s, 1)
                    gelu(L, s)
                    if s:
                        walk("dn", L, s - 1)
                if L == 0:
                    walk("dn", L, n - 1)

            def gelu(L, s):
                ac.wait_ge(*M.free[4 + 2 * (s % 2)].at("cb", L, s, 0))
                nc.scalar.activation(ffn["gg"][:, s % 2, :, :].rearrange("p a b -> p (a b)"),
                                     ffn["cbg"][:, s % 2, :, :].rearrange("p a b -> p (a b)"), ACT.Gelu_apprx_tanh) \
                    .then_inc(*M.act.mark("gelu", L, s))

            def gathered(E, tag, which):
                for g in range(2):
                    ac.wait_ge(*E.groups.at(tag, which, "ga", g))
                    nc.scalar.copy(xe[0][:, 4 * g:4 * g + 4, :], bank[2 + g][:, :].rearrange("p (c n) -> p c n", n=P)) \
                        .then_inc(*E.act.mark(tag, which, "xe", g))

            def experts(E, tag, base):
                def walk(*key):
                    ahead(E, split_hi, ac, key, base)
                if E is V:
                    for i in range(SPLIT):
                        split_hi(E, ac, i)
                    gathered(E, tag, "own")
                def silu(f):
                    b = 4 + 2 * (f % 2)
                    walk("gu", f, 0, 0)
                    ac.wait_ge(*E.groups.at(tag, "gu", f, 0))
                    if f >= 2:
                        ac.wait_ge(*E.free[b + 1].at(tag, "h", f - 2))
                    nc.scalar.activation(moe["sg"][:, f % 2, :], bank[b][:, :], ACT.Silu).then_inc(*E.free[b].mark(tag, "sg", f))
                    walk("gu", f, 0, 1)
                    walk("gu", f, 1, 0)
                    walk("gu", f, 1, 1)

                def turned(f):
                    ac.wait_ge(*E.groups.at(tag, "tr", f))
                    if f >= 2:
                        ac.wait_ge(*E.groups.at(tag, "dn", f - 2))
                    nc.scalar.copy(hTe[0][:, f % 2, :], bank[2 + f % 2][:, :]).then_inc(*E.act.mark(tag, "hTe", f))

                def down(f):
                    walk("dn", f, 0)
                    walk("dn", f, 1)
                silu(0)
                for f in range(EXP_STEPS):
                    if f + 1 < EXP_STEPS:
                        silu(f + 1)
                    turned(f)
                    if f == 0:
                        ac.wait_ge(*E.groups.at(tag, "tg"))
                        nc.scalar.copy(moe["sgT"], bank[3][:, 0:S]).then_inc(*E.free[3].mark(tag, "sgT"))
                    else:
                        down(f - 1)
                    if E is M and f == EXP_STEPS - 1:
                        gathered(E, tag, "next")
                down(EXP_STEPS - 1)
                ac.wait_ge(*E.groups.at(tag, "dn", EXP_STEPS - 1))
                nc.scalar.copy(moe["ye"][:, 0:512], bank[0][:, :]).then_inc(*E.free[0].mark(tag, "ye", 0))

            def delta(L):
                ac.wait_ge(*params.at("cw", L))
                nc.scalar.copy(wba_s[0][:, :, :], wba[:, :, :]).then_inc(*M.act.mark("wba", L))
                for j in range(6):
                    b = 2 * ((j // 2) % 2) + j % 2
                    if j % 2 == 0:
                        walk("in", L, j)
                    ac.wait_ge(*M.groups.at("cv", L, j))
                    for m in range(2):
                        ins = nc.scalar.activation(dn["cv"][:, 2 * j + m, :], bank[b][:, m * S:(m + 1) * S], ACT.Identity,
                                                   scale=cw[:, 2 * j + m, 3:4])
                    ins.then_inc(*M.act.mark("tap", L, j))
                    if j % 2:
                        walk("in", L, j)
                ac.wait_ge(*M.groups.at("ba", L))
                nc.scalar.copy(ba.rearrange("p a b -> p (a b)"), bank[2][:, 0:16]).then_inc(*M.free[2].mark("ba", L))
                for j in range(6):
                    ac.wait_ge(*M.free[2 * ((j // 2) % 2) + j % 2].at("cv", L, j))
                    v = dn["cv"][:, 2 * j:2 * j + 2, :].rearrange("p a b -> p (a b)")
                    nc.scalar.activation(v, v, ACT.Silu).then_inc(*M.act.mark("silu", L, j))
                ac.wait_ge(*M.free[2].at("ba", L))
                nc.scalar.activation(beta, ba[:, :, 0:DN_H], ACT.Sigmoid).then_inc(*M.act.mark("beta", L))
                ac.wait_ge(*decay.at(L, "y"))
                nc.scalar.activation(sp1, sp1, ACT.Abs).then_inc(*M.act.mark())
                wait_self()
                nc.scalar.activation(sp1, sp1, ACT.Exp, scale=-1.0).then_inc(*M.act.mark())
                wait_self()
                nc.scalar.activation(sp1, sp1, ACT.Ln, bias=1.0).then_inc(*M.act.mark())
                nc.scalar.activation(gl, alog[:, L - 2:L - 1, :].to_broadcast([P, NT, DN_H]), ACT.Exp).then_inc(*M.act.mark("sp", L))
                for g in range(4):
                    if g == 2:
                        walk("in", L, 6)
                        block_out("in", L, 3, 0, dn["z"])
                        walk("in", L, 7)
                    if g >= 2:
                        ac.wait_ge(*M.groups.at("ssq", L, g - 2))
                    ac.wait_ge(*M.act.at("silu", L, g))
                    nc.scalar.activation(dn["sq"][:, 4 * (g % 2):4 * (g % 2) + 4, :].rearrange("p a b -> p (a b)"),
                                         dn["cv"][:, 2 * g:2 * g + 2, :].rearrange("p a b -> p (a b)"), ACT.Square) \
                        .then_inc(*squares.mark(L, g))
                for g in range(4):
                    ac.wait_ge(*M.groups.at("ssq", L, g))
                    ac.wait_ge(*M.groups.at("ssq", L, 3))
                    if g >= 2:
                        ac.wait_ge(*normed.at(L, g - 2))
                    nc.scalar.activation(dn["sq"][:, 4 * (g % 2):4 * (g % 2) + 4, :].rearrange("p a b -> p (a b)"),
                                         bank[4 + g][:, :], ACT.Sqrt, bias=C("rms_eps")) \
                        .then_inc(*M.free[4 + g].mark("len", L, g))
                walk("in", L, 8)
                block_out("in", L, 4, 0, qk2[:, :, 0:512], DH ** -0.5)
                walk("in", L, 9)
                ac.wait_ge(*M.groups.at("gcol", L))
                nc.scalar.activation(ngc.rearrange("p a b -> p (a b)"), bank[6][:, 0:N_DN], ACT.Copy, scale=-1.0) \
                    .then_inc(*M.free[6].mark("gcol", L))
                ac.wait_ge(*M.free[6].at("gcol", L))
                nc.scalar.activation(expg, ngc, ACT.Exp, scale=-1.0).then_inc(*M.act.mark("expg", L))
                ac.wait_ge(*decay.at(L, "last"))
                nc.scalar.activation(kdsc, kdsc, ACT.Exp).then_inc(*M.act.mark("kdsc", L))
                for t in range(NT):
                    ac.wait_ge(*M.free[t].at("grow", L, t))
                    for h in range(DN_H):
                        ins = nc.scalar.activation(dn["gam"][:, t * DN_H + h, :], dn["gam"][:, t * DN_H + h, :], ACT.Exp,
                                                   bias=ngc[:, t, h:h + 1])
                    ins.then_inc(*M.act.mark("gam", L, t))
                for n in range(1, LEVELS):
                    for t in range(NT):
                        ac.wait_ge(*M.groups.at("lv", L, n, "X", t))
                        nc.scalar.copy(dn["Xl"][:, t * DN_H:(t + 1) * DN_H, :], bank[t][:, :].rearrange("p (h n) -> p h n", n=P)) \
                            .then_inc(*M.free[t].mark("lv", L, n, "X", t))
                    if n in (3, 5):
                        walk("in", L, 10 + (n - 3) // 2)
                block_out("in", L, 5, 6, qk2[:, :, 512:1024])
                for t in range(NT):
                    nc.scalar.activation(dn["z"][:, t, :], dn["z"][:, t, :], ACT.Silu).then_inc(*M.act.mark("zs", L, t))
                ac.wait_ge(*M.groups.at("u", L, 0))
                nc.scalar.copy(dn["u"][:, 0:DN_H, :].rearrange("p a b -> p (a b)"), bank[0][:, :]).then_inc(*M.free[0].mark("u", L, 0))
                ac.wait_ge(*M.groups.at("u", L, 1))
                nc.scalar.copy(dn["u"][:, DN_H:, :].rearrange("p a b -> p (a b)"), bank[1][:, :]).then_inc(*M.free[1].mark("u", L, 1))
                ac.wait_ge(*M.groups.at("wT", L))
                nc.scalar.copy(dn["wT"].rearrange("p a b -> p (a b)"), bank[2][:, :]).then_inc(*M.free[2].mark("wT", L))
                ac.wait_ge(*M.groups.at("state", L))
                nc.scalar.copy(dn["state"].rearrange("p a b -> p (a b)"), bank[3][:, :]).then_inc(*M.free[3].mark("state", L))
                for t in range(NT):
                    ac.wait_ge(*(M.free[4].at("o0", L) if t == 0 else M.free[7].at("o1", L)))
                    for h in range(DN_H):
                        ins = nc.scalar.activation(dn["AT"][:, t * DN_H + h, :], dn["o"][:, t * DN_H + h, :], ACT.Square, accum_out=ss[:, t, h:h + 1])
                ins.then_inc(*M.act.mark("oss", L))
                wait_self()
                nc.scalar.activation(rn8, ss, ACT.Sqrt, bias=C("rms_eps"), scale=1.0 / P).then_inc(*M.act.mark("ort", L))
                block_out("in", L, 6, 2, att["qn"][:, :, 1024:1536])
                for t in range(NT):
                    ac.wait_ge(*M.groups.at("oT", L, t))
                    nc.scalar.copy(aT[0][:, 0:4, t * P:(t + 1) * P], bank[t][:, :].rearrange("p (c n) -> p c n", n=P)) \
                        .then_inc(*M.act.mark("oT", L, t))

            M.ev.seen = V.ev.seen = 0
            ac.wait_ge(*first_x.at())
            nc.scalar.copy(xT[0][:, :, :], Rf.rearrange("p (c n) -> p c n", n=S)).then_inc(*M.act.mark("xT", "first"))
            for i in range(SPLIT):
                split_hi(M, ac, i)
            ac.wait_ge(*consts.at())
            ac.wait_ge(*angles.at("sin"))
            nc.scalar.activation(sin1, red, ACT.Sin).then_inc(*angles_done.mark("sin"))
            ac.wait_ge(*angles.at("cos"))
            nc.scalar.activation(cos1, ang, ACT.Sin).then_inc(*angles_done.mark("cos"))
            ac.wait_ge(*params.at("sinks"))
            for L in range(2):
                if L:
                    copy_T((L, "in"), L)
                qkv_out(L)
                copy_qkT(L, 8)
                attention(L, NHEAD, 0)
                for i in range(4):
                    walk("wo", L, i)
                root(L, "mix", mv[:, :, 1], 1.0, C("ln_eps"))
                copy_T((L, "mix"), L)
                if L == 0:
                    dense_act(0)
                else:
                    ac.wait_ge(*params.at("wr"))
                    nc.scalar.copy(wr_s[0][:, :, :], wr[:, :, :]).then_inc(*M.act.mark("wr"))
                    ac.wait_ge(*decided.at("m"))
                    nc.scalar.activation(w2, w2, ACT.Exp).then_inc(*M.act.mark("w2"))
                    ac.wait_ge(*flag_done.at())
                    r = ac.value_load(flag_i[0:1, 0:1], min_val=0, max_val=1)
                    with ac.If(r > 0):
                        with ac.Fori(0, NE) as e:
                            with V.ev.loop(e):
                                experts(V, "ovf", 0)
                        ac.wait_ge(*overflow_done())
                    for i in range(SPLIT):
                        split_hi(M, ac, expert_base + i)
                    gathered(M, "moe", "first")
                    with ac.Fori(0, NE) as e:
                        with ev.loop(e):
                            experts(M, "moe", expert_base)
                root(L, "ffn", mv[:, :, 1], 1.0, C("ln_eps"))
                copy_T((L, "ffn"), L)
                for nb in range(2):
                    walk("pg", L, 2 * nb)
                    for t in range(NT):
                        b = (2 * nb + t) % 4
                        ac.wait_ge(*M.groups.at("pg", L, nb, t))
                        nc.scalar.activation(att["sg"][:, 2 * nb + t, :], bank[b][:, :], ACT.Sigmoid).then_inc(*M.free[b].mark("pg", L, nb, t))
                    walk("pg", L, 2 * nb + 1)
            for L in range(2, 4):
                sum_squares(L, "in", X, lambda t: x_ready.at(*((1, "ple", t) if L == 2 else (2, "ffn", t))))
                copy_T((L, "in"), L)
                delta(L)
                walk("in", L, 12)
                walk("in", L, 13)
                copy_qkT(L, 4)
                attention(L, 8, 4)
                for i in range(3):
                    walk("wo", L, i)
                half_squares(L, "mix", wo_halves)
                walk("wo", L, 3)
                sum_squares(L, "pre", X, lambda t: x_ready.at(L, "mix", t))
                copy_T((L, "mix"), L)
                dense_act(L)
                half_squares(L, "ffn", y_halves)
                walk("dn", L, FFN_STEPS[L] - 1)

        @block.vector
        def _(ve):
            V_ = nc.vector

            def sync(E=M):
                ve.wait_ge(*E.dve.last())

            def step(ins, E=M, *key):
                ins.then_inc(*E.dve.mark(*key))

            def chain(ins, E=M, *key):
                step(ins, E, *key)
                sync(E)

            def walk(*key):
                ahead(M, split_lo, ve, key)

            def rest_T(stage, L):
                for t in range(NT):
                    for g in range(2):
                        ve.wait_ge(*M.groups.at("tx", stage, t, g))
                        ve.wait_ge(*M.act.at("xT", stage, t, g))
                        cols = slice(t * P, (t + 1) * P)
                        hi = xT[0][:, 4 * g:4 * g + 4, cols].bitcast(F32)
                        dst = xT[1][:, 4 * g:4 * g + 4, cols]
                        if L < 2:
                            V_.tensor_tensor(dst, bank[2 * t + g][:, :].rearrange("p (c n) -> p c n", n=P), hi, ALU.subtract) \
                                .then_inc(*M.free[2 * t + g].mark("xT", stage, t, g))
                        else:
                            V_.tensor_tensor(dst, turned_in[:, 2 * t + g, :, :], hi, ALU.subtract) \
                                .then_inc(*xs_ready.mark(stage, t, g))

            def vec_row(v):
                s = v % VSLOTS
                ve.wait_ge(vecs[s].sem, 16 * (v // VSLOTS + 1))
                return vec[:, s, :]

            def rope(L, blocks, h0, h1, cos, sin):
                n_h = h1 - h0
                for t in range(NT):
                    for name, n, b in blocks:
                        ve.wait_ge(*M.free[b + t].at(name, L, n, t))
                    q = (att["qn"] if L < 2 else qk2)[:, t, h0 * DH:h1 * DH].rearrange("p (h d) -> p h d", d=DH)
                    x1, x2 = q[:, :, 0:8], q[:, :, 8:16]
                    c = cos[:, t, :].unsqueeze(1).to_broadcast([P, n_h, 8])
                    s = sin[:, t, :].unsqueeze(1).to_broadcast([P, n_h, 8])
                    tm = [att["tmp"][:, i, 0:n_h, :] for i in range(4)]
                    step(V_.tensor_tensor(tm[0], x1, c, ALU.mult))
                    step(V_.tensor_tensor(tm[1], x2, s, ALU.mult))
                    step(V_.tensor_tensor(tm[2], x2, c, ALU.mult))
                    chain(V_.tensor_tensor(tm[3], x1, s, ALU.mult))
                    step(V_.tensor_tensor(x1, tm[0], tm[1], ALU.subtract))
                    last = V_.tensor_tensor(x2, tm[2], tm[3], ALU.add)
                    if L < 2 and h0:
                        chain(last)
                        k = att["qn"][:, t, 1024:1280].rearrange("p (h d) -> p h d", d=DH)
                        V_.tensor_copy(att["kd"][:, t, :, 0, :], k)
                        last = V_.tensor_copy(att["kd"][:, t, :, 1, :], k)
                    last.then_inc(*roped.mark(L, t, h0))
                    ve.wait_ge(*roped.at(L, t, h0))

            def attention(L, heads, out0):
                ve.wait_ge(mask_in.sem, 16 * (L + 1 if L < 2 else 2 * L))

                def scores(h):
                    i, b = h % 2, 4 + h % 2
                    ve.wait_ge(*M.groups.at("sc", L, h))
                    if h >= 2:
                        ve.wait_ge(*exped.at(L, h - 2))
                    V_.tensor_tensor(att["s"][:, i, :], bank[b][:, 0:384], msk[:, 0:384], ALU.add).then_inc(*M.free[b].mark("sc", L, h))
                    ve.wait_ge(*M.free[b].at("sc", L, h))
                    for q, (a, c) in enumerate(((0, P), (P, 3 * P))):
                        ins = V_.tensor_reduce(nmax[:, i, q:q + 1], att["s"][:, i, a:c], AXX, ALU.max, negate=True)
                    if L == 1:
                        chain(ins)
                        ins = V_.tensor_scalar(nmax[:, i, :], nmax[:, i, :], nsink[:, h:h + 1], None, ALU.min)
                    ins.then_inc(*maxed.mark(L, h))

                def normalise(h):
                    i = h % 2
                    ve.wait_ge(*exped.at(L, h))
                    if L == 1:
                        chain(V_.tensor_tensor(rsum[:, i, :], rsum[:, i, :], esink[:, i, :], ALU.add))
                    chain(V_.reciprocal(rden[:, i, :], rsum[:, i, :]))
                    for q, (a, c) in enumerate(((0, P), (P, 3 * P))):
                        ins = V_.tensor_scalar(att["pr"][:, i, a:c], att["pr"][:, i, a:c], rden[:, i, q:q + 1], None, ALU.mult)
                    ins.then_inc(*probs.mark(L, h))

                def rest(j):
                    ve.wait_ge(*M.groups.at("pv", L, 2 * j + 1))
                    ve.wait_ge(*M.act.at("aT", L, j))
                    V_.tensor_tensor(aT[1][:, out0 + j, :], bank[2 + j % 2][:, 0:S], aT[0][:, out0 + j, :].bitcast(F32), ALU.subtract) \
                        .then_inc(*M.free[2 + j % 2].mark("pv", L, j))
                for i in range(heads + 3):
                    if i < heads:
                        scores(i)
                    if 1 <= i <= heads:
                        normalise(i - 1)
                    if i >= 4 and i % 2 == 0:
                        rest(i // 2 - 2)

            def layer_norm(L, which, v, take):
                for nb in range(2):
                    for t in range(NT):
                        take(t, nb)
                        step(V_.bn_stats(st6[:, t, nb, :], R[:, t, nb * 512:(nb + 1) * 512]))
                sync()
                for t in range(NT):
                    ins = V_.bn_aggr(mv[:, t, :], st6[:, t, :, :].rearrange("p a b -> p (a b)"))
                    if t == 0:
                        step(ins)
                ins.then_inc(*stats.mark(L, which))
                sync()
                ve.wait_ge(*stats.at(L, which))
                g, b = vec_row(v), vec_row(v + 1)
                for t in range(NT):
                    ins = V_.scalar_tensor_tensor(R[:, t, :], R[:, t, :], mv[:, t, 0:1], g, ALU.subtract, ALU.mult)
                    if t == 0:
                        step(ins)
                ins.then_inc(*vec_used.mark(v))
                ve.wait_ge(*rooted.at(L, which))
                chain(V_.reciprocal(rstd, sd))
                ve.wait_ge(*vec_used.at(v))
                for t in range(NT):
                    V_.scalar_tensor_tensor(X[:, t, :], R[:, t, :], rstd[:, t:t + 1], b, ALU.mult, ALU.add) \
                        .then_inc(*x_ready.mark(L, which, t))

            def post_norm(L, which, v, halves):
                ve.wait_ge(*M.act.at("sq", L, which, 1, 1))
                V_.tensor_tensor(ss[:, :, 0], ss[:, :, 0], ss[:, :, 1], ALU.add).then_inc(*stats.mark(L, which))
                ve.wait_ge(*rooted.at(L, which))
                chain(V_.reciprocal(rstd, sd))
                w = vec_row(v)
                for t in range(NT):
                    for name, th, nb, b, key in halves:
                        if th == t:
                            ve.wait_ge(*M.groups.at(name, L, *key))
                            cols = slice(nb * 512, (nb + 1) * 512)
                            V_.scalar_tensor_tensor(R[:, t, cols], bank[b][:, :], rstd[:, t:t + 1], w[:, cols], ALU.mult, ALU.mult) \
                                .then_inc(*M.free[b].mark(name, L, nb, t))
                    for name, th, nb, b, key in halves:
                        if th == t:
                            ve.wait_ge(*M.free[b].at(name, L, nb, t))
                    V_.tensor_tensor(X[:, t, :], X[:, t, :], R[:, t, :], ALU.add).then_inc(*x_ready.mark(L, which, t))

            def pre_norm(L, which, rt):
                ve.wait_ge(*rooted.at(L, rt))
                ve.wait_ge(*x_ready.at(*((L, "mix", 1) if which == "mix" else (1, "ple", 1) if L == 2 else (2, "ffn", 1))))
                chain(V_.reciprocal(rstd, sd))
                for t in range(NT):
                    V_.tensor_scalar(diag[:, t, :], ident, rstd[:, t:t + 1], None, ALU.mult).then_inc(*prenorm.mark(L, which, t))
                w = prew[:, 0 if which == "in" else 1, :]
                ve.wait_ge(*params.at("prew", L))
                for t in range(NT):
                    for g in range(2):
                        ve.wait_ge(*M.groups.at("tx", (L, which), t, g))
                        V_.tensor_tensor(turned_in[:, 2 * t + g, :, :],
                                         bank[2 * t + g][:, :].rearrange("p (c n) -> p c n", n=P),
                                         w[:, 4 * g:4 * g + 4].unsqueeze(2).to_broadcast([P, 4, P]), ALU.mult) \
                            .then_inc(*M.free[2 * t + g].mark("xT", (L, which), t, g))
                rest_T((L, which), L)

            def dense_dve(L):
                n = FFN_STEPS[L]
                for s in range(n):
                    b = 4 + 2 * (s % 2)
                    walk("gu", L, s, 0)
                    if L == 0:
                        ve.wait_ge(*M.free[b].at("sg", L, s))
                        ve.wait_ge(*M.groups.at("gu", L, s, 1))
                        V_.tensor_tensor(ffn["h"][:, s % 2, :, :].rearrange("p a b -> p (a b)"),
                                         ffn["sg"][:, s % 2, :, :].rearrange("p a b -> p (a b)"), bank[b + 1][:, :], ALU.mult) \
                            .then_inc(*M.free[b + 1].mark("h", L, s))
                        walk("gu", L, s, 1)
                        ve.wait_ge(*M.free[b + 1].at("h", L, s))
                        split_hidden(L, s)
                        if s:
                            walk("dn", L, s - 1)
                        continue
                    for half, buf in enumerate((ffn["cbg"], ffn["cbv"])):
                        ve.wait_ge(*M.groups.at("gu", L, s, half))
                        ve.wait_ge(*M.act.at("tap", L, s, half))
                        o = bank[b + half]
                        for m in range(2):
                            c = half * 22 + 2 * s + m
                            step(V_.scalar_tensor_tensor(buf[:, s % 2, m, 1:S], o[:, m * S:m * S + S - 1], fcw[:, c, 1:2],
                                                         buf[:, s % 2, m, 1:S], ALU.mult, ALU.add))
                        sync()
                        for m in range(2):
                            c = half * 22 + 2 * s + m
                            ins = V_.scalar_tensor_tensor(buf[:, s % 2, m, 2:S], o[:, m * S:m * S + S - 2], fcw[:, c, 0:1],
                                                          buf[:, s % 2, m, 2:S], ALU.mult, ALU.add)
                        ins.then_inc(*M.free[b + half].mark("cb", L, s, half))
                    walk("gu", L, s, 1)
                    gated_mul(L, s)
                    if s:
                        walk("dn", L, s - 1)

            def gated_mul(L, s):
                ve.wait_ge(*M.act.at("gelu", L, s))
                ve.wait_ge(*M.free[5 + 2 * (s % 2)].at("cb", L, s, 1))
                chain(V_.tensor_tensor(ffn["h"][:, s % 2, :, :], ffn["gg"][:, s % 2, :, :], ffn["cbv"][:, s % 2, :, :], ALU.mult))
                split_hidden(L, s)

            def split_hidden(L, s):
                if s >= 2:
                    ve.wait_ge(*M.groups.at("down", L, s - 2))
                h = ffn["h"][:, s % 2, :, :]
                chain(V_.tensor_copy(hT[0][:, s % 2, :, :], h))
                V_.tensor_tensor(hT[1][:, s % 2, :, :], h, hT[0][:, s % 2, :, :].bitcast(F32), ALU.subtract) \
                    .then_inc(*hidden.mark(L, s))

            def route():
                for t in range(NT):
                    ve.wait_ge(*M.groups.at("router", t))
                    V_.tensor_copy(lg[:, t, :], bank[t][:, 0:NE]).then_inc(*M.free[t].mark("router", t))
                    ve.wait_ge(*M.free[t].at("router", t))
                rank = C("rank").unsqueeze(1).to_broadcast([P, NT, NE])

                def pick(src, top, hot):
                    chain(V_.tensor_reduce(top, src, AXX, ALU.max))
                    chain(V_.tensor_tensor(sc8, src, top.unsqueeze(2).to_broadcast([P, NT, NE]), ALU.is_equal))
                    chain(V_.tensor_tensor(sc8, sc8, rank, ALU.mult))
                    chain(V_.tensor_reduce(w1, sc8, AXX, ALU.max))
                    chain(V_.tensor_tensor(hot, sc8, w1.unsqueeze(2).to_broadcast([P, NT, NE]), ALU.is_equal))
                pick(lg, m1, oh1)
                chain(V_.scalar_tensor_tensor(lg2.rearrange("p a b -> p (a b)"), oh1.rearrange("p a b -> p (a b)"), -3.0e38,
                                              lg.rearrange("p a b -> p (a b)"), ALU.mult, ALU.add))
                pick(lg2, m2, oh2)
                V_.tensor_tensor(memb, oh1, oh2, ALU.add).then_inc(*member.mark())
                V_.tensor_tensor(w2, m2, m1, ALU.subtract).then_inc(*decided.mark("m"))
                ve.wait_ge(*M.act.at("w2"))
                chain(V_.tensor_scalar(w1, w2, 1.0, None, ALU.add))
                chain(V_.reciprocal(w1, w1))
                chain(V_.tensor_tensor(w2, w2, w1, ALU.mult))
                chain(V_.tensor_tensor(gates, oh1, w1.unsqueeze(2).to_broadcast([P, NT, NE]), ALU.mult))
                chain(V_.tensor_tensor(sc8, oh2, w2.unsqueeze(2).to_broadcast([P, NT, NE]), ALU.mult))
                chain(V_.tensor_tensor(gates, gates, sc8, ALU.add))
                ve.wait_ge(*M.groups.at("ranks"))
                r = bank[2][:, 0:2 * NE].rearrange("p (a b) -> p a b", b=NE)
                chain(V_.memset(posx, 0.0))
                chain(V_.scalar_tensor_tensor(posx[:, :, 0:NE], r, 1.0, memb, ALU.add, ALU.mult))
                chain(V_.tensor_scalar(posx, posx, -1.0, None, ALU.add))
                V_.tensor_reduce(flag_f, bank[2][:, 2 * NE:3 * NE], AXX, ALU.max).then_inc(*M.free[2].mark("ranks"))
                ve.wait_ge(*M.free[2].at("ranks"))
                chain(V_.tensor_scalar(flag_f, flag_f, float(P) + 0.5, None, ALU.is_gt))
                V_.tensor_copy(flag_i[:, :], flag_f).then_inc(*flag_done.mark())
                ve.wait_ge(*flag_done.at())
                for t in range(NT):
                    step(V_.tensor_scalar(R[:, t, :], X[:, t, :], ALPHA, None, ALU.mult))
                sync()

            def select(E, tag, which, e, tile):
                chain(V_.tensor_copy(pcol, posx[:, :, e]), E)
                for t in range(NT):
                    step(V_.tensor_scalar(moe["sel"][:, t, :], C("iota", tile * P, (tile + 1) * P), pcol[:, t:t + 1], None,
                                          ALU.is_equal), E, tag, which, "sel")

            def rest_x(E, tag, which):
                for g in range(2):
                    ve.wait_ge(*E.groups.at(tag, which, "ga", g))
                    ve.wait_ge(*E.act.at(tag, which, "xe", g))
                    V_.tensor_tensor(xe[1][:, 4 * g:4 * g + 4, :], bank[2 + g][:, :].rearrange("p (c n) -> p c n", n=P),
                                     xe[0][:, 4 * g:4 * g + 4, :].bitcast(F32), ALU.subtract) \
                        .then_inc(*E.free[2 + g].mark(tag, which, "xe", g))

            def add_rows(E, tag, which):
                for t in range(NT):
                    for nb in range(2):
                        ve.wait_ge(*E.groups.at(tag, which, "sc", t, nb))
                        r = R[:, t, nb * 512:(nb + 1) * 512]
                        V_.tensor_tensor(r, r, bank[2 * t + nb][:, :], ALU.add).then_inc(*E.free[2 * t + nb].mark(tag, which, "sc", t, nb))
                for t in range(NT):
                    for nb in range(2):
                        ve.wait_ge(*E.free[2 * t + nb].at(tag, which, "sc", t, nb))

            def experts(E, tag, base, e, tile):
                def walk(*key):
                    ahead(E, split_lo, ve, key, base)
                if E is V:
                    select(E, tag, "own", e, tile)
                    for i in range(SPLIT):
                        split_lo(E, ve, i)
                    rest_x(E, tag, "own")
                step(V_.tensor_copy(pcol2, posx[:, :, e]), E)
                chain(V_.tensor_copy(gcol, gates[:, :, e]), E)
                for t in range(NT):
                    step(V_.tensor_scalar(moe["selg"][:, t, :], C("iota", tile * P, (tile + 1) * P), pcol2[:, t:t + 1],
                                          gcol[:, t:t + 1], ALU.is_equal, ALU.mult), E, tag, "selg")

                def hidden_of(f):
                    b = 4 + 2 * (f % 2)
                    for half in range(2):
                        walk("gu", f, half, 0)
                        if half == 0:
                            walk("gu", f, 0, 1)
                    ve.wait_ge(*E.free[b].at(tag, "sg", f))
                    ve.wait_ge(*E.groups.at(tag, "gu", f, 1))
                    if f >= 2:
                        ve.wait_ge(*E.groups.at(tag, "tr", f - 2))
                    V_.tensor_tensor(moe["h"][:, f % 2, :], moe["sg"][:, f % 2, :], bank[b + 1][:, :], ALU.mult) \
                        .then_inc(*E.free[b + 1].mark(tag, "h", f))
                    walk("gu", f, 1, 1)

                def rest_h(f):
                    ve.wait_ge(*E.groups.at(tag, "tr", f))
                    ve.wait_ge(*E.act.at(tag, "hTe", f))
                    V_.tensor_tensor(hTe[1][:, f % 2, :], bank[2 + f % 2][:, :], hTe[0][:, f % 2, :].bitcast(F32), ALU.subtract) \
                        .then_inc(*E.free[2 + f % 2].mark(tag, "hTe", f))
                hidden_of(0)
                if E is M:
                    add_rows(E, tag, "before")
                for f in range(EXP_STEPS):
                    if f + 1 < EXP_STEPS:
                        hidden_of(f + 1)
                    if E is M and f == 1:
                        select(E, tag, "next", e + 1, tile)
                    rest_h(f)
                    if f:
                        walk("dn", f - 1, 0)
                        walk("dn", f - 1, 1)
                    if E is M and f == EXP_STEPS - 1:
                        rest_x(E, tag, "next")
                walk("dn", EXP_STEPS - 1, 0)
                walk("dn", EXP_STEPS - 1, 1)
                ve.wait_ge(*E.groups.at(tag, "dn", EXP_STEPS - 1))
                V_.tensor_copy(moe["ye"][:, 512:1024], bank[1][:, :]).then_inc(*E.free[1].mark(tag, "ye", 1))
                if E is V:
                    add_rows(E, tag, "own")

            def delta(L):
                ve.wait_ge(*M.act.at("wba", L))
                V_.tensor_tensor(wba_s[1][:, :, :], wba[:, :, :], wba_s[0][:, :, :].bitcast(F32), ALU.subtract) \
                    .then_inc(*wsmall.mark("wba", L))
                for j in range(6):
                    b = 2 * ((j // 2) % 2) + j % 2
                    if j % 2 == 0:
                        walk("in", L, j)
                    ve.wait_ge(*M.groups.at("cv", L, j))
                    ve.wait_ge(*M.act.at("tap", L, j))
                    for tap in (2, 1, 0):
                        d = 3 - tap
                        for m in range(2):
                            c = 2 * j + m
                            ins = V_.scalar_tensor_tensor(dn["cv"][:, c, d:S], bank[b][:, m * S:m * S + S - d], cw[:, c, tap:tap + 1],
                                                          dn["cv"][:, c, d:S], ALU.mult, ALU.add)
                            if tap or not m:
                                step(ins)
                        if tap:
                            sync()
                    ins.then_inc(*M.free[b].mark("cv", L, j))
                    if j % 2:
                        walk("in", L, j)
                ve.wait_ge(*M.free[2].at("ba", L))
                chain(V_.tensor_tensor(sp1, ba[:, :, DN_H:8], dtb[:, L - 2:L - 1, :].to_broadcast([P, NT, DN_H]), ALU.add))
                V_.tensor_scalar(sp2, sp1, 0.0, None, ALU.max).then_inc(*decay.mark(L, "y"))
                ve.wait_ge(*M.act.at("sp", L))
                ve.wait_ge(*decay.at(L, "y"))
                chain(V_.tensor_tensor(sp2, sp2, sp1, ALU.add))
                V_.scalar_tensor_tensor(gl.rearrange("p a b -> p (a b)"), sp2.rearrange("p a b -> p (a b)"), -1.0,
                                        gl.rearrange("p a b -> p (a b)"), ALU.mult, ALU.mult).then_inc(*decay.mark(L, "g"))
                ve.wait_ge(*decay.at(L, "g"))
                ve.wait_ge(*M.act.at("beta", L))
                step(V_.tensor_copy(dn["gB"], gl.rearrange("p a b -> p (a b)").unsqueeze(2).to_broadcast([P, N_DN, P])))
                V_.tensor_copy(dn["bB"], beta.rearrange("p a b -> p (a b)").unsqueeze(2).to_broadcast([P, N_DN, P])) \
                    .then_inc(*decay.mark(L, "rows"))
                walk("in", L, 6)
                walk("in", L, 7)
                for g in range(4):
                    ve.wait_ge(*M.free[4 + g].at("len", L, g))
                    v = dn["cv"][:, 2 * g:2 * g + 2, :].rearrange("p a b -> p (a b)")
                    ln = dn["sq"][:, 4 * (g % 2):4 * (g % 2) + 4, :].rearrange("p a b -> p (a b)")
                    chain(V_.reciprocal(ln, ln))
                    V_.scalar_tensor_tensor(v, v, (float(P) ** -0.5 if g < 2 else 1.0), ln, ALU.mult, ALU.mult) \
                        .then_inc(*normed.mark(L, g))
                ve.wait_ge(*normed.at(L, 3))
                walk("in", L, 8)
                ve.wait_ge(*M.free[6].at("gcol", L))
                ve.wait_ge(mask_in.sem, 16 * (2 * L - 1))
                for t in range(NT):
                    ve.wait_ge(*M.groups.at("grow", L, t))
                    gr = bank[t][:, :].rearrange("p (h n) -> p h n", n=P)
                    if t == 0:
                        V_.tensor_tensor(kdsc, gr[:, :, P - 1], ngc[:, 0, :], ALU.add).then_inc(*decay.mark(L, "last"))
                    V_.tensor_tensor(dn["gam"][:, t * DN_H:(t + 1) * DN_H, :], gr,
                                     msk[:, LEVELS * P:(LEVELS + 1) * P].unsqueeze(1).to_broadcast([P, DN_H, P]), ALU.add) \
                        .then_inc(*M.free[t].mark("grow", L, t))
                for t in range(NT):
                    ve.wait_ge(*M.groups.at("brow", L, t))
                    V_.tensor_tensor(dn["kb"][:, :, t * P:(t + 1) * P], dn["cv"][:, DN_H:2 * DN_H, t * P:(t + 1) * P],
                                     bank[2 + t][:, :].rearrange("p (h n) -> p h n", n=P), ALU.mult) \
                        .then_inc(*M.free[2 + t].mark("brow", L, t))
                def decayed(name, b0, dst):
                    for t in range(NT):
                        ve.wait_ge(*M.groups.at(name, L, t))
                        ve.wait_ge(*M.act.at("gam", L, t))
                        V_.tensor_tensor(dst[:, t * DN_H:(t + 1) * DN_H, :], bank[b0 + t][:, :].rearrange("p (h n) -> p h n", n=P),
                                         dn["gam"][:, t * DN_H:(t + 1) * DN_H, :], ALU.mult).then_inc(*M.free[b0 + t].mark(name, L, t))
                    for t in range(NT):
                        ve.wait_ge(*M.free[b0 + t].at(name, L, t))

                def token_keys():
                    ve.wait_ge(*M.act.at("kdsc", L))
                    chain(V_.tensor_tensor(bexp, beta[:, 1, :], expg[:, 1, :], ALU.mult))
                    for t in range(NT):
                        ve.wait_ge(*M.groups.at("kn", L, t))
                        for h in range(DN_H):
                            dst, sc = (dn["kdec"], kdsc) if t == 0 else (dn["kbg"], bexp)
                            ins = V_.tensor_scalar(dst[:, h, :], bank[4 + t][:, h * P:(h + 1) * P], sc[:, h:h + 1], None, ALU.mult)
                        ins.then_inc(*M.free[4 + t].mark("kn", L, t))

                def token_values():
                    for t in range(NT):
                        ve.wait_ge(*M.groups.at("vn", L, t))
                        for h in range(DN_H):
                            ins = V_.tensor_scalar(dn["vb"][:, t * DN_H + h, :], bank[6 + t][:, h * P:(h + 1) * P],
                                                   beta[:, t, h:h + 1], None, ALU.mult)
                        ins.then_inc(*M.free[6 + t].mark("vn", L, t))
                decayed("kk", 0, dn["AT"])
                half = [slice(t * DN_H, (t + 1) * DN_H) for t in range(NT)]

                def level_blocks(n):
                    for t in range(NT):
                        if n:
                            ve.wait_ge(*M.groups.at("lv", L, n - 1, "X", t))
                        V_.tensor_tensor(dn["LT"][:, half[t], :], dn["AT"][:, half[t], :],
                                         msk[:, n * P:(n + 1) * P].unsqueeze(1).to_broadcast([P, DN_H, P]), ALU.mult).then_inc(*inverse.mark(L, n, "LT", t))
                level_blocks(0)
                token_keys()
                decayed("kq", 2, dn["qk"])
                for t in range(NT):
                    ve.wait_ge(*inverse.at(L, 0, "LT", t))
                    ve.wait_ge(*M.groups.at("lv", L, 0, "X", t))
                    idb = ident.unsqueeze(1).to_broadcast([P, DN_H, P])
                    step(V_.tensor_tensor(dn["DT"][:, half[t], :], idb, dn["LT"][:, half[t], :], ALU.subtract))
                    V_.tensor_tensor(dn["D"][:, half[t], :], idb, bank[t][:, :].rearrange("p (h n) -> p h n", n=P), ALU.subtract) \
                        .then_inc(*M.free[t].mark("lv", L, 0, "X", t))
                    ve.wait_ge(*M.free[t].at("lv", L, 0, "X", t))
                sync()
                level_blocks(1)
                token_values()
                for n in range(1, LEVELS):
                    if n + 1 < LEVELS:
                        level_blocks(n + 1)
                    for t in range(NT):
                        for which, b, dst in (("D", 2 + t, dn["D"]), ("DT", 4 + t, dn["DT"])):
                            if which == "D" and n == LEVELS - 1:
                                continue
                            ve.wait_ge(*M.groups.at("lv", L, n, which, t))
                            V_.tensor_tensor(dst[:, half[t], :], dst[:, half[t], :], bank[b][:, :].rearrange("p (h n) -> p h n", n=P),
                                             ALU.subtract).then_inc(*M.free[b].mark("lv", L, n, which, t))
                    if n in (1, 3, 5):
                        walk("in", L, 9 + (n - 1) // 2)
                    for t in range(NT):
                        if n < LEVELS - 1:
                            ve.wait_ge(*M.free[2 + t].at("lv", L, n, "D", t))
                        ve.wait_ge(*M.free[4 + t].at("lv", L, n, "DT", t))
                ve.wait_ge(*M.groups.at("o0", L))
                V_.tensor_copy(dn["o"][:, 0:DN_H, :].rearrange("p a b -> p (a b)"), bank[4][:, :]).then_inc(*M.free[4].mark("o0", L))
                ve.wait_ge(*M.groups.at("ws", L))
                ve.wait_ge(*M.free[1].at("u", L, 1))
                V_.tensor_tensor(dn["vn"].rearrange("p a b -> p (a b)"), dn["u"][:, DN_H:, :].rearrange("p a b -> p (a b)"),
                                 bank[5][:, :], ALU.subtract).then_inc(*M.free[5].mark("ws", L))
                ve.wait_ge(*M.groups.at("qs", L))
                for h in range(DN_H):
                    ins = V_.tensor_scalar(dn["o"][:, DN_H + h, :], bank[6][:, h * P:(h + 1) * P], expg[:, 1, h:h + 1], None, ALU.mult)
                ins.then_inc(*M.free[6].mark("qs", L))
                ve.wait_ge(*M.free[6].at("qs", L))
                ve.wait_ge(*M.groups.at("o1", L))
                o1 = dn["o"][:, DN_H:, :].rearrange("p a b -> p (a b)")
                V_.tensor_tensor(o1, o1, bank[7][:, :], ALU.add).then_inc(*M.free[7].mark("o1", L))
                ve.wait_ge(*M.act.at("ort", L))
                chain(V_.reciprocal(rn8, rn8))
                ve.wait_ge(*params.at("onorm", L))
                for t in range(NT):
                    for h in range(DN_H):
                        o = dn["o"][:, t * DN_H + h, :]
                        step(V_.scalar_tensor_tensor(o, o, rn8[:, t, h:h + 1], onorm[:, :], ALU.mult, ALU.mult))
                sync()
                for t in range(NT):
                    ve.wait_ge(*M.act.at("zs", L, t))
                    o = dn["o"][:, t * DN_H:(t + 1) * DN_H, :].rearrange("p a b -> p (a b)")
                    V_.tensor_tensor(o, o, dn["z"][:, t, :], ALU.mult).then_inc(*gated.mark(L, t))
                rope(L, (("in", 4, 0), ("in", 5, 6)), 0, 16,
                     C("cos2").rearrange("p (a b) -> p a b", b=8), C("sin2").rearrange("p (a b) -> p a b", b=8))
                walk("in", L, 12)
                for t in range(NT):
                    ve.wait_ge(*M.groups.at("oT", L, t))
                    ve.wait_ge(*M.act.at("oT", L, t))
                    V_.tensor_tensor(aT[1][:, 0:4, t * P:(t + 1) * P], bank[t][:, :].rearrange("p (c n) -> p c n", n=P),
                                     aT[0][:, 0:4, t * P:(t + 1) * P].bitcast(F32), ALU.subtract) \
                        .then_inc(*M.free[t].mark("oT", L, t))

            M.ev.seen = V.ev.seen = 0
            ve.wait_ge(*M.act.at("xT", "first"))
            V_.tensor_tensor(xT[1][:, :, :], Rf.rearrange("p (c n) -> p c n", n=S), xT[0][:, :, :].bitcast(F32), ALU.subtract) \
                .then_inc(*xs_ready.mark("first"))
            for i in range(SPLIT):
                split_lo(M, ve, i)
            ve.wait_ge(*consts.at())
            ve.wait_ge(*params.at("pos"))
            chain(V_.tensor_copy(pos_f, pos_i[:, :]))
            for t in range(NT):
                step(V_.tensor_scalar(ang[:, t, :], C("inv"), pos_f[:, t:t + 1], None, ALU.mult))
            sync()
            chain(V_.tensor_scalar(rnd, ang, float(1.0 / (2 * np.pi)), MAGIC, ALU.mult, ALU.add))
            chain(V_.tensor_scalar(rnd, rnd, -MAGIC, None, ALU.add))
            c1 = 6.28125
            c2 = float(np.float32(np.round((2 * np.pi - c1) * 2 ** 20) / 2 ** 20))
            c3 = float(2 * np.pi - c1 - c2)

            def flat(a):
                return a.rearrange("p a b -> p (a b)")
            for c in (c1, c2, c3):
                chain(V_.scalar_tensor_tensor(flat(ang), flat(rnd), -c, flat(ang), ALU.mult, ALU.add))
            PI = 3.1415925
            V_.tensor_scalar(red, ang, PI, -PI, ALU.min, ALU.max).then_inc(*angles.mark("sin"))
            chain(V_.tensor_scalar(ang, ang, float(np.pi / 2), None, ALU.add))
            chain(V_.tensor_scalar(rnd, ang, float(np.pi), float(2 * np.pi), ALU.is_gt, ALU.mult))
            chain(V_.tensor_tensor(ang, ang, rnd, ALU.subtract))
            V_.tensor_scalar(ang, ang, PI, -PI, ALU.min, ALU.max).then_inc(*angles.mark("cos"))
            ve.wait_ge(*params.at("sinks"))
            chain(V_.tensor_scalar(nsink, sinks, -1.0, None, ALU.mult))
            ve.wait_ge(*angles_done.at("cos"))
            for L in range(2):
                if L:
                    rest_T((L, "in"), L)
                for i in range(5):
                    walk("qkv", L, i)
                rope(L, (("qkv", 0, 0), ("qkv", 1, 2)), 0, NHEAD, cos1, sin1)
                walk("qkv", L, 5)
                rope(L, (("qkv", 2, 0),), NHEAD, NHEAD + 4, cos1, sin1)
                attention(L, NHEAD, 0)

                def take(t, nb, name, b):
                    ve.wait_ge(*M.groups.at(name, L, *((nb, t) if name == "wo" else (t, nb))))
                    V_.scalar_tensor_tensor(R[:, t, nb * 512:(nb + 1) * 512], X[:, t, nb * 512:(nb + 1) * 512], ALPHA,
                                            bank[b][:, :], ALU.mult, ALU.add).then_inc(*M.free[b].mark(name, L, nb, t))
                    ve.wait_ge(*M.free[b].at(name, L, nb, t))

                def take_wo(t, nb):
                    if t == 0:
                        walk("wo", L, 2 * nb)
                        if nb == 0:
                            walk("wo", L, 1)
                    take(t, nb, "wo", (2 * nb + t) % 4)

                def take_y(t, nb):
                    take(t, nb, "y", 2 * t + nb)
                if L == 0:
                    ve.wait_ge(*params.at("X"))
                layer_norm(L, "mix", 4 * L, take_wo)
                rest_T((L, "mix"), L)
                walk("wo", L, 3)
                if L == 1:
                    ve.wait_ge(*M.act.at("wr"))
                    V_.tensor_tensor(wr_s[1][:, :, :], wr[:, :, :], wr_s[0][:, :, :].bitcast(F32), ALU.subtract).then_inc(*wsmall.mark("wr"))
                if L == 0:
                    dense_dve(0)
                    layer_norm(L, "ffn", 4 * L + 2, take_y)
                    walk("dn", 0, FFN_STEPS[0] - 1)
                else:
                    route()
                    r = ve.value_load(flag_i[0:1, 0:1], min_val=0, max_val=1)
                    with ve.If(r > 0):
                        for n, event in enumerate(V.free + [V.groups]):
                            V_.memset(tick[:, n:n + 1], 0.0).then_inc(event.sem, 1)
                        with ve.Fori(0, NE) as e:
                            with V.ev.loop(e):
                                experts(V, "ovf", 0, e, 1)
                    select(M, "moe", "first", 0, 0)
                    for i in range(SPLIT):
                        split_lo(M, ve, expert_base + i)
                    rest_x(M, "moe", "first")
                    V_.memset(moe["ye"], 0.0)
                    step(V_.memset(moe["sgT"], 0.0), M, "moe", "zeroed")
                    with ve.Fori(0, NE) as e:
                        with ev.loop(e):
                            experts(M, "moe", expert_base, e, 0)
                    add_rows(M, "moe", "last")
                    layer_norm(L, "ffn", 4 * L + 2, lambda t, nb: None)
                rest_T((L, "ffn"), L)
                for i in range(4):
                    walk("pg", L, i)
                for nb in range(2):
                    for t in range(NT):
                        b = (2 * nb + t) % 4
                        ve.wait_ge(*M.free[b].at("pg", L, nb, t))
                        ve.wait_ge(*M.groups.at("pp", L, nb, t))
                        V_.tensor_tensor(att["sg"][:, 2 * nb + t, :], att["sg"][:, 2 * nb + t, :], bank[4 + 2 * nb + t][:, :], ALU.mult) \
                            .then_inc(*M.free[4 + 2 * nb + t].mark("pp", L, nb, t))
                        ve.wait_ge(*M.free[4 + 2 * nb + t].at("pp", L, nb, t))
                for t in range(NT):
                    for nb in range(2):
                        x = X[:, t, nb * 512:(nb + 1) * 512]
                        ins = V_.tensor_tensor(x, x, att["sg"][:, 2 * nb + t, :], ALU.add)
                        if nb == 0:
                            step(ins)
                    ins.then_inc(*x_ready.mark(L, "ple", t))
            for L in range(2, 4):
                pre_norm(L, "in", "in")
                if L == 3:
                    walk("dn", 2, FFN_STEPS[2] - 1)
                delta(L)
                walk("in", L, 13)
                attention(L, 8, 4)
                for i in range(3):
                    walk("wo", L, i)
                post_norm(L, "mix", 4 + 2 * L, wo_halves)
                pre_norm(L, "mix", "pre")
                walk("wo", L, 3)
                dense_dve(L)
                post_norm(L, "ffn", 5 + 2 * L, y_halves)


_OUT = (S, DM)


def layout(a):
    def np32(name):
        return np.asarray(a[name])

    def natural(w):
        lead, n = w.shape[:-2], w.shape[-1] // 512
        w = w.reshape(lead + (2, 4, P, n, 512))
        k = len(lead)
        w = w.transpose(tuple(range(k)) + (k + 3, k, k + 2, k + 1, k + 4))
        return np.ascontiguousarray(w).reshape(lead + (2 * n, P, UNIT))

    def paired(g, u):
        lead, n = g.shape[:-2], g.shape[-1] // 256
        k = len(lead)
        both = np.stack([w.reshape(lead + (2, 4, P, n, 256)) for w in (g, u)], axis=-2)
        both = both.transpose(tuple(range(k)) + (k + 3, k, k + 2, k + 1, k + 4, k + 5))
        return np.ascontiguousarray(both).reshape(lead + (n, 2, P, UNIT))

    def rows(w):
        lead, n = w.shape[:-2], w.shape[-2] // 256
        k = len(lead)
        w = w.reshape(lead + (n, 2, P, DM)).transpose(tuple(range(k)) + (k, k + 2, k + 1, k + 3))
        return np.ascontiguousarray(w).reshape(lead + (n, P, UNIT))

    def per_channel(w):
        return w.reshape(2, -1, P).transpose(0, 2, 1)

    def every(v):
        return np.broadcast_to(np.asarray(v)[..., None, :], np.asarray(v).shape[:-1] + (P, np.asarray(v).shape[-1]))
    out = {}
    x = np32("x")[0]
    out["x"] = x
    out["xT"] = x.T.reshape(KC, P, S).transpose(1, 0, 2)
    out["pT"] = np32("p")[:, 0].transpose(0, 2, 1).reshape(2, 2, P, S).transpose(0, 2, 1, 3)
    out["positions"] = np32("positions")[0].reshape(NT, P).T
    out["sinks"] = every(np32("sinks")[0])
    out["alog"] = np.broadcast_to(np32("dn_a_log_2")[None], (P, 2, DN_H))
    out["dtb"] = np.broadcast_to(np32("dn_dt_bias_2")[None], (P, 2, DN_H))
    out["wr"] = np32("w_router")[0].reshape(KC, P, NE).transpose(1, 0, 2)
    rowsv = []
    for L in range(2):
        rowsv += [np32("ln_mix_g")[L], np32("ln_mix_b")[L], np32("ln_ffn_g")[L], np32("ln_ffn_b")[L]]
    for L in range(2):
        rowsv += [np32("post_mix_norm_2")[L], np32("post_ffn_norm_2")[L]]
    out["vecs"] = every(np.stack(rowsv))
    out["wu_qkv"] = natural(np32("w_qkv"))
    out["wu_o"] = natural(np32("w_o"))
    out["wu_ffn_gu"] = paired(np32("w_ffn_gate")[0], np32("w_ffn_up")[0])
    out["wu_ffn_d"] = rows(np32("w_ffn_down")[0])
    out["wu_pp"] = rows(np32("w_ple_proj"))[:, 0]
    out["wu_pg"] = natural(np32("w_ple_gate"))
    for name, src in (("wu_eg", "w_exp_gate"), ("wu_eu", "w_exp_up")):
        out[name] = natural(np32(src)[0]).reshape(NE, EXP_STEPS, 2, P, UNIT)
    out["wu_ed"] = rows(np32("w_exp_down")[0]).reshape(NE, EXP_STEPS, 2, P, UNIT)
    w_in = np32("w_in_2")
    out["wu_in"] = natural(np.concatenate([w_in[:, :, :2048], w_in[:, :, 2056:]], axis=2))
    out["wba"] = w_in[:, :, 2048:2056].reshape(2, KC, P, 8).transpose(0, 2, 1, 3)
    out["wu_out"] = natural(np32("w_out_2"))
    up = np32("ffn_up_2")
    out["wu_up"] = paired(up[:, :, :FF2], up[:, :, FF2:])
    out["wu_down"] = rows(np32("ffn_down_2"))
    out["cw"] = np32("dn_conv_2").reshape(2, 4, 12, P).transpose(0, 3, 2, 1)
    out["fcw"] = np.concatenate([np32("ffn_conv_2"), np32("ffn_conv_bias_2")[:, None]], axis=1) \
        .reshape(2, 4, 44, P).transpose(0, 3, 2, 1)
    out["prew"] = np.stack([per_channel(np32("pre_mix_norm_2")), per_channel(np32("pre_ffn_norm_2"))], axis=2)
    out["onorm"] = every(np32("dn_out_norm_2"))
    out["cst"] = constants()[0]
    out["masks"] = masks()
    return {k: np.ascontiguousarray(v) for k, v in out.items()}


def kernel(_debug=None, **inputs):
    import concourse.bacc as bacc
    from concourse.bass_utils import run_bass_kernel_spmd

    arrays = layout(inputs)
    plan = Plan()
    for _ in range(2):
        plan.opens.clear()
        nc = bacc.Bacc("TRN2", target_bir_lowering=False, num_devices=1)
        aps = {n: nc.dram_tensor(f"in_{n}", list(v.shape), mybir.dt.from_np(v.dtype), kind="ExternalInput").ap()
               for n, v in arrays.items()}
        aps["out"] = nc.dram_tensor("out_x", list(_OUT), F32, kind="ExternalOutput").ap()
        if _debug:
            aps["dbg"] = nc.dram_tensor("dbg", [len(_debug["dump"]), S, DM], F32, kind="ExternalOutput").ap()
        build_program(nc, aps, plan, _debug)
        plan.counted = True
    r = run_bass_kernel_spmd(nc, [{f"in_{n}": v for n, v in arrays.items()}], core_ids=[0])
    if _debug:
        return r
    return r.results[0]["out_x"].reshape(1, S, DM)
```
